# Optimizing a Trainium2 kernel written in Bass

```python
import math
import jax
import jax.numpy as jnp
from jax import lax
import numpy as np

D_MODEL = 1024
BATCH = 1
SEQ = 512
DEPTH = 2
DEC_BATCH = 8
DEC_SEQ = 4
PAST_LEN = 1024
PAGE_SIZE = 128

N_MIXERS = 2
N_ATTN_LAYERS = (DEPTH + 1) // 2
N_MLSTM_LAYERS = DEPTH // 2
NORM_EPS = 1e-6
D_FF = ((8 * D_MODEL // 3 + 127) // 128) * 128
N_HEADS = 16
HEAD_DIM = D_MODEL // N_HEADS
KV_HEADS = 4
GROUP = N_HEADS // KV_HEADS
ROT_DIM = HEAD_DIM // 4
ROPE_THETA = 500000.0
CMP_BLOCK = 32
CMP_STRIDE = 16
CMP_HIDDEN = 2 * HEAD_DIM
SEL_BLOCK = 64
SEL_TOPK = 16
WINDOW = 512
Q_BLOCK = 64
NSA_Q = N_HEADS * HEAD_DIM
NSA_KV = 3 * 2 * KV_HEADS * HEAD_DIM
NSA_PROJ = NSA_Q + NSA_KV + 3 * N_HEADS
NEG = -1e30
BIG = 1e30
ML_INNER = 2 * D_MODEL
ML_HEADS = 4
ML_HEAD_DIM = ML_INNER // ML_HEADS
QKV_BLOCK = 4
CONV_W = 4
ML_CHUNK = 64
ML_PROJ = 2 * ML_INNER + 2 * ML_HEADS

kernel_name = 'nsa_mlstm_macaron_adaln_decode_step'

def _rmsnorm(x, g):
    xf = x.astype(jnp.float32)
    y = xf * lax.rsqrt(jnp.mean(xf * xf, axis=-1, keepdims=True) + NORM_EPS)
    return (y * g.astype(jnp.float32)).astype(x.dtype)

def _modulate(x, g, shift, scale):
    return _rmsnorm(x, g) * (1.0 + scale[:, None, :]) + shift[:, None, :]

def _adaln(c, w, b):
    return (jax.nn.silu(c) @ w + b).reshape(c.shape[0], 9, D_MODEL)

def _swiglu(u, w_in, w_out):
    gate, up = jnp.split(u @ w_in, 2, axis=-1)
    return (jax.nn.silu(gate) * up) @ w_out

def _half_ffn(x, mod, slot, g, w_in, w_out):
    shift, scale, gate = mod[:, 3 * slot], mod[:, 3 * slot + 1], mod[:, 3 * slot + 2]
    return x + 0.5 * (1.0 + gate[:, None, :]) * _swiglu(_modulate(x, g, shift, scale), w_in, w_out)

def _rope_partial(x, pos):
    half = ROT_DIM // 2
    inv = ROPE_THETA ** (-jnp.arange(0, ROT_DIM, 2, dtype=jnp.float32) / ROT_DIM)
    ang = pos.astype(jnp.float32)[:, None] * inv[None, :]
    shp = (pos.shape[0],) + (1,) * (x.ndim - 3) + (half,)
    cos = jnp.cos(ang).reshape(shp)
    sin = jnp.sin(ang).reshape(shp)
    xf = x.astype(jnp.float32)
    x1, x2 = xf[..., :half], xf[..., half:ROT_DIM]
    out = jnp.concatenate([x1 * cos - x2 * sin, x1 * sin + x2 * cos, xf[..., ROT_DIM:]], axis=-1)
    return out.astype(x.dtype)

def _nsa_project(u, w_in, pos):
    b, t, _ = u.shape
    proj = u @ w_in
    q = _rope_partial(proj[..., :NSA_Q].reshape(b, t, N_HEADS, HEAD_DIM), pos)
    kv = proj[..., NSA_Q:NSA_Q + NSA_KV].reshape(b, t, 3, 2, KV_HEADS, HEAD_DIM)
    kv = jnp.stack([_rope_partial(kv[:, :, :, 0], pos), kv[:, :, :, 1]], axis=3)
    gates = jax.nn.sigmoid(proj[..., NSA_Q + NSA_KV:].astype(jnp.float32)).reshape(b, t, 3, N_HEADS)
    return q, kv[:, :, 0], kv[:, :, 1], kv[:, :, 2], gates

def _compress(kv, pos_emb, w1, w2):
    b, l = kv.shape[:2]
    nseg = l // CMP_STRIDE
    seg = kv[:, :nseg * CMP_STRIDE].reshape(b, nseg, CMP_STRIDE, 2, KV_HEADS, HEAD_DIM)
    pe = pos_emb[:, :, None, :]
    first = jnp.einsum('bnlsgd,sldf->bnsgf', seg + pe[:CMP_STRIDE], w1[:, :CMP_STRIDE])
    second = jnp.einsum('bnlsgd,sldf->bnsgf', seg + pe[CMP_STRIDE:], w1[:, CMP_STRIDE:])
    hid = jax.nn.gelu(first[:, :-1] + second[:, 1:])
    out = jnp.einsum('bcsgf,sfd->bcsgd', hid, w2)
    return out[:, :, 0], out[:, :, 1]

def _cmp_branch(q, kc, vc, q_pos):
    b, tq = q.shape[:2]
    nc = kc.shape[1]
    qg = q.reshape(b, tq, KV_HEADS, GROUP, HEAD_DIM)
    s = jnp.einsum('bqgrd,bcgd->bgrqc', qg, kc).astype(jnp.float32) * (HEAD_DIM ** -0.5)
    blk_last = jnp.arange(nc) * CMP_STRIDE + CMP_BLOCK - 1
    valid = blk_last[None, :] <= q_pos[:, None]
    p = jax.nn.softmax(jnp.where(valid, s, NEG), axis=-1) * valid
    o = jnp.einsum('bgrqc,bcgd->bqgrd', p, vc.astype(jnp.float32)).reshape(b, tq, N_HEADS, HEAD_DIM)
    return o, p.sum(axis=2)

def _select_blocks(p_grp, q_pos, seq_len):
    nc = p_grp.shape[-1]
    n_sel = -(-seq_len // SEL_BLOCK)
    i = np.arange(nc)[:, None]
    j = np.arange(n_sel)[None, :]
    overlap = np.maximum(np.minimum(i * CMP_STRIDE + CMP_BLOCK, (j + 1) * SEL_BLOCK) - np.maximum(i * CMP_STRIDE, j * SEL_BLOCK), 0)
    m = jnp.asarray(overlap / CMP_STRIDE, dtype=jnp.float32)
    imp = jnp.einsum('bgqc,cj->bgqj', p_grp, m)
    cur = (q_pos // SEL_BLOCK)[:, None]
    jj = jnp.arange(n_sel)[None, :]
    forced = (jj == 0) | (jj == cur) | (jj == cur - 1)
    score = jnp.where(forced, BIG, jnp.where(jj <= cur, imp, NEG))
    _, idx = lax.top_k(score, min(SEL_TOPK, n_sel))
    return idx

def _attend_gathered(qg, k, v, mask):
    s = jnp.einsum('bgrqd,bgqnd->bgrqn', qg, k).astype(jnp.float32) * (HEAD_DIM ** -0.5)
    p = jax.nn.softmax(jnp.where(mask[:, :, None], s, NEG), axis=-1)
    return jnp.einsum('bgrqn,bgqnd->bgrqd', p, v.astype(jnp.float32))

def _attend_shared(qg, k, v, mask):
    s = jnp.einsum('bgrqd,bngd->bgrqn', qg, k).astype(jnp.float32) * (HEAD_DIM ** -0.5)
    p = jax.nn.softmax(jnp.where(mask, s, NEG), axis=-1)
    return jnp.einsum('bgrqn,bngd->bgrqd', p, v.astype(jnp.float32))

def _heads_to_seq(o):
    b, _, _, t, _ = o.shape
    return o.transpose(0, 3, 1, 2, 4).reshape(b, t, N_HEADS, HEAD_DIM)

def _nsa_combine(u, gates, o_cmp, o_sel, o_win, w_out):
    b, t = u.shape[:2]
    o = gates[:, :, 0, :, None] * o_cmp + gates[:, :, 1, :, None] * o_sel + gates[:, :, 2, :, None] * o_win
    return o.reshape(b, t, NSA_Q).astype(u.dtype) @ w_out

def _nsa_prompt(u, w_in, w_out, pos_emb, w1, w2):
    b, t, _ = u.shape
    pos = jnp.arange(t)
    q, cmp_kv, sel_kv, win_kv, gates = _nsa_project(u, w_in, pos)
    kc, vc = _compress(cmp_kv, pos_emb, w1, w2)
    o_cmp, p_grp = _cmp_branch(q, kc, vc, pos)
    idx = _select_blocks(p_grp, pos, t)
    n_sel = -(-t // SEL_BLOCK)
    sel_pad = jnp.pad(sel_kv, ((0, 0), (0, n_sel * SEL_BLOCK - t), (0, 0), (0, 0), (0, 0)))
    sel_blocks = sel_pad.reshape(b, n_sel, SEL_BLOCK, 2, KV_HEADS, HEAD_DIM).transpose(0, 4, 1, 2, 3, 5)
    win_pad = jnp.pad(win_kv, ((0, 0), (WINDOW, 0), (0, 0), (0, 0), (0, 0)))
    qg = q.reshape(b, t, KV_HEADS, GROUP, HEAD_DIM).transpose(0, 2, 3, 1, 4)
    qb_len = math.gcd(t, Q_BLOCK)
    n_top = idx.shape[-1]
    bi = jnp.arange(b)[:, None, None, None]
    gi = jnp.arange(KV_HEADS)[None, :, None, None]

    def block(start):
        qp = start + jnp.arange(qb_len)
        qb = lax.dynamic_slice_in_dim(qg, start, qb_len, axis=3)
        ib = lax.dynamic_slice_in_dim(idx, start, qb_len, axis=2)
        kvg = sel_blocks[bi, gi, ib].reshape(b, KV_HEADS, qb_len, n_top * SEL_BLOCK, 2, HEAD_DIM)
        kp = (ib[..., None] * SEL_BLOCK + jnp.arange(SEL_BLOCK)).reshape(b, KV_HEADS, qb_len, n_top * SEL_BLOCK)
        o_sel = _attend_gathered(qb, kvg[..., 0, :], kvg[..., 1, :], kp <= qp[:, None])
        wkv = lax.dynamic_slice_in_dim(win_pad, start, qb_len + WINDOW, axis=1)
        kpw = start - WINDOW + jnp.arange(qb_len + WINDOW)
        d = qp[:, None] - kpw[None, :]
        o_win = _attend_shared(qb, wkv[:, :, 0], wkv[:, :, 1], (kpw[None, :] >= 0) & (d >= 0) & (d < WINDOW))
        return o_sel, o_win

    o_sel, o_win = lax.map(block, jnp.arange(0, t, qb_len))
    o_sel = _heads_to_seq(o_sel.transpose(1, 2, 3, 0, 4, 5).reshape(b, KV_HEADS, GROUP, t, HEAD_DIM))
    o_win = _heads_to_seq(o_win.transpose(1, 2, 3, 0, 4, 5).reshape(b, KV_HEADS, GROUP, t, HEAD_DIM))
    out = _nsa_combine(u, gates, o_cmp, o_sel, o_win, w_out)
    return out, cmp_kv, sel_kv, win_kv[:, t - min(WINDOW, t):]

def _nsa_sample(u, w_in, w_out, pos_emb, w1, w2, cache_cmp_l, cache_sel_l, win_buf, page_table):
    b, t, _ = u.shape
    n_pages = page_table.shape[1]
    past = n_pages * PAGE_SIZE
    pos = past + jnp.arange(t)
    q, cmp_kv, sel_kv, win_kv, gates = _nsa_project(u, w_in, pos)
    past_cmp = cache_cmp_l[page_table].reshape(b, past, 2, KV_HEADS, HEAD_DIM)
    all_cmp = jnp.concatenate([past_cmp, cmp_kv.astype(past_cmp.dtype)], axis=1)
    kc, vc = _compress(all_cmp, pos_emb, w1, w2)
    o_cmp, p_grp = _cmp_branch(q, kc, vc, pos)
    idx = _select_blocks(p_grp, pos, past + t)
    bpp = PAGE_SIZE // SEL_BLOCK
    n_past_blk = past // SEL_BLOCK
    n_tail = -(-t // SEL_BLOCK)
    pool_blk = cache_sel_l.reshape(-1, bpp, SEL_BLOCK, 2, KV_HEADS, HEAD_DIM)
    tail = jnp.pad(sel_kv.astype(cache_sel_l.dtype), ((0, 0), (0, n_tail * SEL_BLOCK - t), (0, 0), (0, 0), (0, 0)))
    tail = tail.reshape(b, n_tail, SEL_BLOCK, 2, KV_HEADS, HEAD_DIM)
    bi = jnp.arange(b)[:, None, None, None]
    gi = jnp.arange(KV_HEADS)[None, :, None, None]
    jc = jnp.minimum(idx, n_past_blk - 1)
    phys = page_table[bi, jc // bpp]
    from_pool = pool_blk[phys, jc % bpp, :, :, gi]
    jt = jnp.clip(idx - n_past_blk, 0, n_tail - 1)
    from_tail = tail[bi, jt, :, :, gi]
    kvg = jnp.where((idx < n_past_blk)[..., None, None, None], from_pool, from_tail)
    n_top = idx.shape[-1]
    kvg = kvg.reshape(b, KV_HEADS, t, n_top * SEL_BLOCK, 2, HEAD_DIM)
    kp = (idx[..., None] * SEL_BLOCK + jnp.arange(SEL_BLOCK)).reshape(b, KV_HEADS, t, n_top * SEL_BLOCK)
    qg = q.reshape(b, t, KV_HEADS, GROUP, HEAD_DIM).transpose(0, 2, 3, 1, 4)
    o_sel = _heads_to_seq(_attend_gathered(qg, kvg[..., 0, :], kvg[..., 1, :], kp <= pos[:, None]))
    wb = win_buf.shape[1]
    wkv = jnp.concatenate([win_buf, win_kv.astype(win_buf.dtype)], axis=1)
    kpw = past - wb + jnp.arange(wb + t)
    d = pos[:, None] - kpw[None, :]
    o_win = _heads_to_seq(_attend_shared(qg, wkv[:, :, 0], wkv[:, :, 1], (d >= 0) & (d < WINDOW)))
    out = _nsa_combine(u, gates, o_cmp, o_sel, o_win, w_out)
    return out, cmp_kv, sel_kv, wkv[:, wb + t - min(WINDOW, wb + t):]

def _headwise(x, w):
    b, t, _ = x.shape
    return jnp.einsum('btnc,ncd->btnd', x.reshape(b, t, -1, QKV_BLOCK), w).reshape(b, t, -1)

def _mlstm_chunkwise(q, k, v, ig, lf, c0, n0, m0):
    b, h, t, d = q.shape
    lc = math.gcd(t, ML_CHUNK)
    nck = t // lc
    tri = jnp.tril(jnp.ones((lc, lc), dtype=bool))

    def chunks(a):
        return jnp.moveaxis(a.reshape(a.shape[:2] + (nck, lc) + a.shape[3:]), 2, 0)

    def step(carry, inp):
        c, n, m = carry
        qc, kc, vc, ic, fc = inp
        bcum = jnp.cumsum(fc, axis=-1)
        dmat = jnp.where(tri, bcum[..., :, None] - bcum[..., None, :] + ic[..., None, :], -jnp.inf)
        inter = bcum + m[..., None]
        m_t = jnp.maximum(inter, dmat.max(axis=-1))
        w_int = jnp.exp(inter - m_t)
        s = jnp.einsum('bhtd,bhsd->bhts', qc, kc) * jnp.exp(dmat - m_t[..., None])
        num = w_int[..., None] * jnp.einsum('bhtd,bhde->bhte', qc, c) + jnp.einsum('bhts,bhse->bhte', s, vc)
        den = w_int * jnp.einsum('bhtd,bhd->bht', qc, n) + s.sum(axis=-1)
        hc = num / jnp.maximum(jnp.abs(den), jnp.exp(-m_t))[..., None]
        m_new = m_t[..., -1]
        w_dec = jnp.exp(bcum[..., -1] + m - m_new)
        w_s = jnp.exp(bcum[..., -1:] - bcum + ic - m_new[..., None])
        c_new = w_dec[..., None, None] * c + jnp.einsum('bhs,bhsd,bhse->bhde', w_s, kc, vc)
        n_new = w_dec[..., None] * n + jnp.einsum('bhs,bhsd->bhd', w_s, kc)
        return (c_new, n_new, m_new), hc

    (c, n, m), hs = lax.scan(step, (c0, n0, m0), (chunks(q), chunks(k), chunks(v), chunks(ig), chunks(lf)))
    return jnp.moveaxis(hs, 0, 2).reshape(b, h, t, d), c, n, m

def _mlstm_mixer(u, w_in, b_gate, conv_w, conv_b, wq, wk, wv, skip, gn_g, w_out, conv_buf, c0, n0, m0):
    b, t, _ = u.shape
    proj = u @ w_in
    xm = proj[..., :ML_INNER]
    z = proj[..., ML_INNER:2 * ML_INNER]
    gl = proj[..., 2 * ML_INNER:].astype(jnp.float32).reshape(b, t, 2, ML_HEADS) + b_gate.astype(jnp.float32)
    ig = gl[:, :, 0].transpose(0, 2, 1)
    lf = jax.nn.log_sigmoid(gl[:, :, 1]).transpose(0, 2, 1)
    xpad = jnp.concatenate([conv_buf.astype(xm.dtype), xm], axis=1)
    xc = conv_b
    for w in range(CONV_W):
        xc = xc + xpad[:, w:w + t] * conv_w[w]
    xc = jax.nn.silu(xc)

    def heads(a):
        return a.reshape(b, t, ML_HEADS, ML_HEAD_DIM).transpose(0, 2, 1, 3).astype(jnp.float32)

    q = heads(_headwise(xc, wq))
    k = heads(_headwise(xc, wk)) * (ML_HEAD_DIM ** -0.5)
    v = heads(_headwise(xm, wv))
    hcell, c, n, m = _mlstm_chunkwise(q, k, v, ig, lf, c0.astype(jnp.float32), n0.astype(jnp.float32), m0.astype(jnp.float32))
    hcell = hcell.transpose(0, 2, 1, 3) * jax.nn.sigmoid(z.astype(jnp.float32)).reshape(b, t, ML_HEADS, ML_HEAD_DIM)
    hn = hcell * lax.rsqrt(jnp.mean(hcell * hcell, axis=-1, keepdims=True) + NORM_EPS)
    hn = hn * gn_g.astype(jnp.float32).reshape(ML_HEADS, ML_HEAD_DIM)
    hn = hn.reshape(b, t, ML_INNER) + skip.astype(jnp.float32) * xc.astype(jnp.float32)
    return hn.astype(u.dtype) @ w_out, c, n, m, xpad[:, t:]

def setup_inputs(seed: int = 0) -> dict:
    key = jax.random.key(seed)
    ks = iter(jax.random.split(key, 40))

    def nrm(shape, scale):
        return jax.random.normal(next(ks), shape, jnp.float32) * scale

    n_pages = PAST_LEN // PAGE_SIZE
    n_used = DEC_BATCH * n_pages
    n_pool = n_used + (n_used + 3) // 4
    win_len = min(WINDOW, PAST_LEN)
    page_table = jax.random.permutation(next(ks), n_pool)[:n_used].reshape(DEC_BATCH, n_pages).astype(jnp.int32)
    b_gate = jnp.stack([nrm((N_MLSTM_LAYERS, ML_HEADS), 0.1), 3.0 + nrm((N_MLSTM_LAYERS, ML_HEADS), 0.5)], axis=1)
    return {
        'x_prompt': nrm((BATCH, SEQ, D_MODEL), 1.0),
        'x_sample': nrm((DEC_BATCH, DEC_SEQ, D_MODEL), 1.0),
        'cache_cmp': nrm((N_ATTN_LAYERS, n_pool, PAGE_SIZE, 2, KV_HEADS, HEAD_DIM), 1.0),
        'cache_sel': nrm((N_ATTN_LAYERS, n_pool, PAGE_SIZE, 2, KV_HEADS, HEAD_DIM), 1.0),
        'cache_win': nrm((N_ATTN_LAYERS, DEC_BATCH, win_len, 2, KV_HEADS, HEAD_DIM), 1.0),
        'state_C': nrm((N_MLSTM_LAYERS, DEC_BATCH, ML_HEADS, ML_HEAD_DIM, ML_HEAD_DIM), 0.05),
        'state_n': nrm((N_MLSTM_LAYERS, DEC_BATCH, ML_HEADS, ML_HEAD_DIM), 0.5),
        'state_m': nrm((N_MLSTM_LAYERS, DEC_BATCH, ML_HEADS), 0.5),
        'state_conv': nrm((N_MLSTM_LAYERS, DEC_BATCH, CONV_W - 1, ML_INNER), 1.0),
        'page_table': page_table,
        'c_prompt': nrm((BATCH, D_MODEL), 1.0),
        'c_sample': nrm((DEC_BATCH, D_MODEL), 1.0),
        'ada_w': nrm((DEPTH, D_MODEL, 9 * D_MODEL), 0.5 * D_MODEL ** -0.5),
        'ada_b': nrm((DEPTH, 9 * D_MODEL), 0.02),
        'norm_g': 1.0 + nrm((DEPTH, 3, D_MODEL), 0.05),
        'ffn_w_in': nrm((DEPTH, 2, D_MODEL, 2 * D_FF), D_MODEL ** -0.5),
        'ffn_w_out': nrm((DEPTH, 2, D_FF, D_MODEL), D_FF ** -0.5),
        'final_norm_g': 1.0 + nrm((D_MODEL,), 0.05),
        'attn_w_in': nrm((N_ATTN_LAYERS, D_MODEL, NSA_PROJ), D_MODEL ** -0.5),
        'attn_w_out': nrm((N_ATTN_LAYERS, NSA_Q, D_MODEL), NSA_Q ** -0.5),
        'cmp_pos': nrm((N_ATTN_LAYERS, CMP_BLOCK, 2, HEAD_DIM), 0.1),
        'cmp_w1': nrm((N_ATTN_LAYERS, 2, CMP_BLOCK, HEAD_DIM, CMP_HIDDEN), (CMP_BLOCK * HEAD_DIM) ** -0.5),
        'cmp_w2': nrm((N_ATTN_LAYERS, 2, CMP_HIDDEN, HEAD_DIM), CMP_HIDDEN ** -0.5),
        'ml_w_in': nrm((N_MLSTM_LAYERS, D_MODEL, ML_PROJ), D_MODEL ** -0.5),
        'ml_b_gate': b_gate,
        'ml_conv_w': nrm((N_MLSTM_LAYERS, CONV_W, ML_INNER), CONV_W ** -0.5),
        'ml_conv_b': nrm((N_MLSTM_LAYERS, ML_INNER), 0.02),
        'ml_wq': nrm((N_MLSTM_LAYERS, ML_INNER // QKV_BLOCK, QKV_BLOCK, QKV_BLOCK), QKV_BLOCK ** -0.5),
        'ml_wk': nrm((N_MLSTM_LAYERS, ML_INNER // QKV_BLOCK, QKV_BLOCK, QKV_BLOCK), QKV_BLOCK ** -0.5),
        'ml_wv': nrm((N_MLSTM_LAYERS, ML_INNER // QKV_BLOCK, QKV_BLOCK, QKV_BLOCK), QKV_BLOCK ** -0.5),
        'ml_skip': 1.0 + nrm((N_MLSTM_LAYERS, ML_INNER), 0.1),
        'ml_gn_g': 1.0 + nrm((N_MLSTM_LAYERS, ML_INNER), 0.05),
        'ml_w_out': nrm((N_MLSTM_LAYERS, ML_INNER, D_MODEL), ML_INNER ** -0.5),
    }

def reference(x_prompt, x_sample, cache_cmp, cache_sel, cache_win, state_C, state_n, state_m, state_conv, page_table,
              c_prompt, c_sample, ada_w, ada_b, norm_g, ffn_w_in, ffn_w_out, final_norm_g,
              attn_w_in, attn_w_out, cmp_pos, cmp_w1, cmp_w2,
              ml_w_in, ml_b_gate, ml_conv_w, ml_conv_b, ml_wq, ml_wk, ml_wv, ml_skip, ml_gn_g, ml_w_out):
    xp, xs = x_prompt, x_sample
    cmp_p, sel_p, win_p, cst_p, nst_p, mst_p, conv_p = [], [], [], [], [], [], []
    cmp_s, sel_s, win_s, cst_s, nst_s, mst_s, conv_s = [], [], [], [], [], [], []
    for i in range(DEPTH):
        mp = _adaln(c_prompt, ada_w[i], ada_b[i])
        ms = _adaln(c_sample, ada_w[i], ada_b[i])
        xp = _half_ffn(xp, mp, 0, norm_g[i, 0], ffn_w_in[i, 0], ffn_w_out[i, 0])
        xs = _half_ffn(xs, ms, 0, norm_g[i, 0], ffn_w_in[i, 0], ffn_w_out[i, 0])
        up = _modulate(xp, norm_g[i, 1], mp[:, 3], mp[:, 4])
        us = _modulate(xs, norm_g[i, 1], ms[:, 3], ms[:, 4])
        j = i // N_MIXERS
        if i % N_MIXERS == 0:
            hp, ckv, skv, wkv = _nsa_prompt(up, attn_w_in[j], attn_w_out[j], cmp_pos[j], cmp_w1[j], cmp_w2[j])
            hs, ckv_s, skv_s, wkv_s = _nsa_sample(us, attn_w_in[j], attn_w_out[j], cmp_pos[j], cmp_w1[j], cmp_w2[j],
                                                  cache_cmp[j], cache_sel[j], cache_win[j], page_table)
            cmp_p.append(ckv)
            sel_p.append(skv)
            win_p.append(wkv)
            cmp_s.append(ckv_s)
            sel_s.append(skv_s)
            win_s.append(wkv_s)
        else:
            bp = up.shape[0]
            hp, c_new, n_new, m_new, buf_new = _mlstm_mixer(
                up, ml_w_in[j], ml_b_gate[j], ml_conv_w[j], ml_conv_b[j], ml_wq[j], ml_wk[j], ml_wv[j],
                ml_skip[j], ml_gn_g[j], ml_w_out[j],
                jnp.zeros((bp, CONV_W - 1, ML_INNER), up.dtype),
                jnp.zeros((bp, ML_HEADS, ML_HEAD_DIM, ML_HEAD_DIM), jnp.float32),
                jnp.zeros((bp, ML_HEADS, ML_HEAD_DIM), jnp.float32),
                jnp.zeros((bp, ML_HEADS), jnp.float32))
            hs, c_s, n_s, m_s, buf_s = _mlstm_mixer(
                us, ml_w_in[j], ml_b_gate[j], ml_conv_w[j], ml_conv_b[j], ml_wq[j], ml_wk[j], ml_wv[j],
                ml_skip[j], ml_gn_g[j], ml_w_out[j], state_conv[j], state_C[j], state_n[j], state_m[j])
            cst_p.append(c_new)
            nst_p.append(n_new)
            mst_p.append(m_new)
            conv_p.append(buf_new)
            cst_s.append(c_s)
            nst_s.append(n_s)
            mst_s.append(m_s)
            conv_s.append(buf_s)
        xp = xp + (1.0 + mp[:, 5])[:, None, :] * hp
        xs = xs + (1.0 + ms[:, 5])[:, None, :] * hs
        xp = _half_ffn(xp, mp, 2, norm_g[i, 2], ffn_w_in[i, 1], ffn_w_out[i, 1])
        xs = _half_ffn(xs, ms, 2, norm_g[i, 2], ffn_w_in[i, 1], ffn_w_out[i, 1])
    y_prompt = _rmsnorm(xp, final_norm_g)
    y_sample = _rmsnorm(xs, final_norm_g)
    return (y_prompt, y_sample,
            jnp.stack(cmp_p), jnp.stack(sel_p), jnp.stack(win_p),
            jnp.stack(cst_p), jnp.stack(nst_p), jnp.stack(mst_p), jnp.stack(conv_p),
            jnp.stack(cmp_s), jnp.stack(sel_s), jnp.stack(win_s),
            jnp.stack(cst_s), jnp.stack(nst_s), jnp.stack(mst_s), jnp.stack(conv_s))


_drawn_inputs = setup_inputs


def setup_inputs(seed=0):
    import zlib

    import numpy as np

    out = dict(_drawn_inputs(seed))
    spreads = {}
    factors = {}
    for name, (base, spread) in spreads.items():
        noise = np.random.default_rng([zlib.crc32(name.encode()), seed]).standard_normal(out[name].shape)
        drawn = base * np.exp(spread * noise) if base else spread * noise
        out[name] = jnp.asarray(drawn.astype(out[name].dtype))
    for name, factor in factors.items():
        out[name] = (out[name] * factor).astype(out[name].dtype)
    return out
```

```python
import concourse.bass as bass
from concourse import mybir
from concourse.alu_op_type import AluOpType as ALU
from contextlib import ExitStack
import numpy as np

F32 = mybir.dt.float32
F32R = mybir.dt.float32r
I32 = mybir.dt.int32
ACT = mybir.ActivationFunctionType
AX = mybir.AxisListType

P = 128
D = 1024
KT = D // P
SEQ = 512
QT = SEQ // P
NB = 8
DS = 4
NTS = NB * DS
T = SEQ + NTS
HB = T // 2
FF = 2816
FT = FF // P
EPS = 1e-6
NEG = -1e30
C9 = 1 + NB
RING = 4
SLOT = 2048
HEADS = 16
KVH = 4
REP = HEADS // KVH
HD = 64
SCALE = HD ** -0.5
NPAGE = 8
NPOOL = 80
NCP = SEQ // 16 - 1
NCS = NPAGE * 8 - 1
NSEL = 17
VR = 560
MH = 4
MI = 2048
MHD = MI // MH
ET = MHD // P
XPW = 3 + SEQ + NB * 7
XCW = XPW - 3


class Stream:

    def __init__(self):
        self.n = 0
        self.full = [0] * RING
        self.done = [0] * RING
        self.plan = {}

    def add(self, name, count, full=(16,), done=(1,)):
        self.plan[name] = (self.n, count, full, done, list(self.full), list(self.done))
        for i in range(count):
            self.full[(self.n + i) % RING] += full[i % len(full)]
            self.done[(self.n + i) % RING] += done[i % len(done)]
        self.n += count


class Chunk:

    def __init__(self, plan, k, it):
        n0, _, full, done, full0, done0 = plan
        s = (n0 + k) % RING
        f, d = full[k % len(full)], done[k % len(done)]
        self.slot = s
        self.k = k
        self.index = it * RING + k
        self.full_at = it * f + (full0[s] + f)
        self.free_at = it * d + done0[s]
        self.done_at = it * d + (done0[s] + d)


def chunks(eng, plan, first=False):
    rounds = plan[1] // RING
    start = 1 if first else 0
    if first:
        for k in range(RING):
            yield Chunk(plan, k, 0)
    with eng.Fori(start, rounds) as it:
        for k in range(RING):
            yield Chunk(plan, k, it)
    for k in range(plan[1] % RING):
        yield Chunk(plan, k, rounds)


class Chain:

    def __init__(self, eng, sem):
        self.eng, self.sem, self.base, self.k = eng, sem, 0, 0

    def __call__(self, ins):
        self.k += 1
        ins.then_inc(self.sem, 1)
        self.eng.wait_ge(self.sem, self.base + self.k)

    def enter(self, it, per):
        self.start, self.per = self.base + self.k, per
        self.base, self.k = it * per + self.start, 0

    def leave(self, rounds):
        assert self.k == self.per, (self.k, self.per)
        self.base, self.k = self.start + rounds * self.per, 0


def constants():
    cols, at = [], {}

    def put(name, a):
        a = np.asarray(a, np.float32)
        full = np.zeros((P, a.shape[1]), np.float32)
        full[:a.shape[0]] = a
        at[name] = (sum(c.shape[1] for c in cols), a.shape[1])
        cols.append(full)

    i = np.arange(P)
    put("ident", np.eye(P))
    put("ones", np.ones((P, P)))
    put("mean_d", np.full((P, P), 1.0 / D))
    put("mean_h", np.full((P, P), 1.0 / MHD))
    rot = np.zeros((P, P))
    for h in (0, HD):
        for j in range(8):
            rot[h + 8 + j, h + j] = -1.0
            rot[h + j, h + 8 + j] = 1.0
    put("rot", rot)
    put("causal", np.where(i[None, :] <= i[:, None], 0.0, NEG))
    put("causal_t", np.where(i[:, None] <= i[None, :], 0.0, NEG))
    g, r, t = i // 32, (i % 32) // DS, i % DS
    put("same_gt", (g[:, None] == g[None, :]) & (t[:, None] == t[None, :]) & (r[:, None] < REP))
    c, j = np.arange(NCS)[:, None], np.arange(NSEL)[None, :]
    put("overlap", np.maximum(np.minimum(c * 16 + 32, (j + 1) * 64) - np.maximum(c * 16, j * 64), 0) / 16)
    put("block_no", np.tile(np.arange(NSEL), (P, 1)))
    tail = np.where(np.arange(DS)[None, :] <= t[:, None], 0.0, NEG)
    put("tails", np.concatenate([tail, tail], 1))
    put("win_edge", np.where(np.arange(DS)[None, :] <= t[:, None], NEG, 0.0))
    q, kk = np.arange(SEQ).reshape(QT, P).T[:, :, None], np.arange(NCP)[None, None, :]
    put("cmp_valid", (kk * 16 + 31 <= q).reshape(P, QT * NCP))
    put("cmp_neg", np.where(kk * 16 + 31 <= q, 0.0, NEG).reshape(P, QT * NCP))
    bt = np.arange(NTS)
    put("pick_t", bt[:, None] % DS == np.where(r < REP, t, -1)[None, :])
    put("own_b", bt[:, None] // DS == np.arange(NB)[None, :])
    put("head_of", np.arange(HEADS)[None, :] == (g * REP + r)[:, None])
    put("own_cols", np.tile((np.arange(NB)[:, None] == bt[None, :] // DS).reshape(1, -1), (P, 1)))
    put("causal_b", np.where((bt[:, None] // DS == bt[None, :] // DS) & (bt[:, None] <= bt[None, :]), 0.0, NEG))
    put("head_row", np.repeat(np.eye(MH), P, 1))
    keep = np.ones(T)
    keep[0] = 0
    keep[SEQ::DS] = 0
    pen = np.zeros(T)
    pen[SEQ::DS] = NEG
    put("restart", np.tile(keep, (MH, 1)))
    put("restart_neg", np.tile(pen, (MH, 1)))
    put("eps", np.full((P, 1), EPS))
    return np.concatenate(cols, 1), at


CONST, CONST_AT = constants()


def rope_tables():
    pos = np.concatenate([np.arange(SEQ), np.tile(1024 + np.arange(DS), NB)]).astype(np.float32)
    inv = np.float32(500000.0) ** (-np.arange(0, 16, 2, dtype=np.float32) / np.float32(16))
    ang = pos[None, :] * inv.astype(np.float32)[:, None]
    cos, sin = np.ones((HD, T), np.float32), np.zeros((HD, T), np.float32)
    cos[:8], cos[8:16], sin[:8], sin[8:16] = np.cos(ang), np.cos(ang), np.sin(ang), np.sin(ang)
    return np.stack([np.tile(cos, (2, 1)), np.tile(sin, (2, 1))], 1)


def program(nc, io):
    V, S, G, PE = nc.vector, nc.scalar, nc.gpsimd, nc.tensor
    stream = Stream()
    stream.add("ada", 2 * 36)
    for f in range(2):
        stream.add(f"in{f}", FT)
        stream.add(f"out{f}", 2 * KT)
        if f == 0:
            stream.add("qkv", 8)
            stream.add("row", 4)
            stream.add("cmp", 2 * NB, full=(64,))
            stream.add("selwin", 4 * NB, full=(64, 64, 16, 16))
            stream.add("aout", 4)
    for f in range(2, 4):
        stream.add(f"in{f}", FT)
        stream.add(f"out{f}", 2 * KT)
        if f == 2:
            stream.add("mgate", 1)
            stream.add("mlstm", 16 * MH, done=(1,) * 4 + (0,) * 8 + (1,) * 4)
    plan = stream.plan
    cs = {k: v for k, v in CONST_AT.items()}

    ctx = ExitStack()
    with ctx:
        def sb(name, shape, dt=F32):
            return ctx.enter_context(nc.sbuf_tensor(name, shape, dt))

        def sem(name):
            return ctx.enter_context(nc.semaphore(name))

        ring = sb("ring", [P, RING, SLOT])
        x = sb("x", [P, KT, T])
        u = sb("u", [P, KT, T])
        mods = sb("mods", [P, 144, C9])
        adab = sb("adab", [P, 144])
        norm_g = sb("norm_g", [P, 7, KT])
        cT = sb("cT", [P, KT, C9])
        cst = sb("cst", [P, CONST.shape[1]])
        rms = sb("rms", [P, 2, HB])
        pages = sb("pages", [1, NB * NPAGE], I32)
        tmp_d = sb("tmp_d", [P, 2, NTS])
        tmp256 = sb("tmp256", [P, 256])
        ARENA = 29660
        with (nc.sbuf_tensor("w_parts", [P, 2, 2, 1024], F32R) as w_parts,
              nc.sbuf_tensor("h_hi", [P, FT, T], F32R) as h_hi,
              nc.sbuf_tensor("h_lo", [P, FT, T], F32R) as h_lo,
              nc.sbuf_tensor("sg", [P, 2, 2, HB], F32) as sg,
              nc.sbuf_tensor("modrow", [P, 256], F32) as modrow):
            pass
        arena = sb("arena", [P, ARENA])
        ps = ctx.enter_context(nc.psum_tensor("ps", [P, 8, 512], F32))

        def const(name, rows=P):
            a, w = cs[name]
            return cst[0:rows, a:a + w]

        top = [0]

        def carve(*dims, at=None):
            n = int(np.prod(dims))
            a = top[0] if at is None else at
            if at is None:
                top[0] = a + n
            assert a + n <= ARENA, (a + n, dims)
            v = arena[:, a:a + n]
            names = "abcd"[:len(dims)]
            if len(dims) > 1:
                v = v.rearrange(f"p ({' '.join(names)}) -> p {' '.join(names)}", **dict(zip(names, dims)))
            return v

        u_hi, u_lo = h_hi[:, 0:KT], h_lo[:, 0:KT]
        full = [sem(f"slot_full{i}") for i in range(RING)]
        done = [sem(f"slot_done{i}") for i in range(RING)]
        consts_in = sem("consts_in")
        x_in = sem("x_in")
        pages_in = sem("pages_in")
        stored = sem("stored")
        c_silu = sem("c_silu")
        ada_rows = sem("ada_rows")
        ada_copied = sem("ada_copied")
        ada_cols = sem("ada_cols")
        mods_in = sem("mods_in")
        mods_done = sem("mods_done")
        x_tile = sem("x_tile")
        squares = sem("squares")
        mean_sq = sem("mean_sq")
        rms_root = sem("rms_root")
        scaled = sem("scaled")
        u_prompt = sem("u_prompt")
        u_decode = sem("u_decode")
        gate_up = sem("gate_up")
        silus = sem("silus")
        hidden = sem("hidden")
        w_rounded = sem("w_rounded")
        w_lo = sem("w_lo")
        w_used = sem("w_used")
        u_dec = sem("u_dec")
        u_rounded = sem("u_rounded")
        u_split = sem("u_split")
        h_rounded = sem("h_rounded")
        h_split = sem("h_split")
        chain_v = sem("chain_v")
        chain_s = sem("chain_s")
        NSTORE = [0]
        ARENA_STORED = [0]

        def ada_pe(pe):
            pe.wait_ge(c_silu, 1)
            pe.wait_ge(rms_root, 1)
            with pe.Fori(0, 18) as it:
                for k in range(4):
                    ch = Chunk(plan["ada"], k, it)
                    pe.wait_ge(full[ch.slot], ch.full_at)
                    w = ring[:, ch.slot, :].rearrange("p (k c) -> p k c", c=D)
                    for j in range(2):
                        kt = 2 * k + j
                        for q in range(4):
                            last = PE.matmul(ps[32 * q:32 * q + C9, 0, 0:256], cT[:, kt, :],
                                             w[:, j, 256 * q:256 * q + 256], start=kt == 0, stop=kt == KT - 1,
                                             skip_group_check=True)
                    last.then_inc(done[ch.slot], 1)
                pe.wait_ge(ada_copied, it + 1)
                pe.wait_ge(mods_in, it + 1)
                for t in range(KT):
                    q = 32 * (t // 2)
                    last = PE.matmul(ps[:, 4 + t // 2, C9 * (t % 2):C9 * (t % 2) + C9], modrow[q:q + C9, P * (t % 2):P * (t % 2) + P],
                                     const("ident")[q:q + C9, q:q + C9], start=True, stop=True)
                last.then_inc(ada_cols, 1)

        def ada_act(act):
            S.activation(cT[:, :, :], cT[:, :, :], ACT.Silu).then_inc(c_silu, 1)
            with act.Fori(0, 18) as it:
                ch = Chunk(plan["ada"], 3, it)
                act.wait_ge(done[ch.slot], ch.done_at)
                for q in range(4):
                    last = S.activation(modrow[32 * q:32 * q + C9, :], ps[32 * q:32 * q + C9, 0, 0:256], ACT.Copy)
                last.then_inc(ada_copied, 1)

        def ada_dve(dve, link):
            with dve.Fori(0, 18) as it:
                dve.wait_ge(ada_cols, it + 1)
                V.tensor_tensor(mods[:, bass.ds(it * KT, KT), :].rearrange("p (q a) b -> p q a b", q=4),
                                ps[:, 4:8, 0:2 * C9].rearrange("p q (a b) -> p q a b", b=C9),
                                adab[:, bass.ds(it * KT, KT)].rearrange("p (q a) -> p q a", q=4).unsqueeze(3)
                                .to_broadcast([P, 4, 2, C9]), ALU.add).then_inc(mods_in, 1)
            dve.wait_ge(mods_in, 19)
            for ls in range(6):
                scale = mods[:, ls * 24 + 8:ls * 24 + 16, :]
                gate = mods[:, ls * 24 + 16:ls * 24 + 24, :]
                link(V.tensor_scalar(scale, scale, 1.0, None, ALU.add))
                V.tensor_tensor(scale, scale, norm_g[:, ls, :].unsqueeze(2).to_broadcast([P, KT, C9]),
                                ALU.mult).then_inc(mods_done, 1)
                half = 1.0 if ls % 3 == 1 else 0.5
                V.tensor_scalar(gate, gate, 1.0, half, ALU.add, ALU.mult).then_inc(mods_done, 1)
            dve.wait_ge(mods_done, 12)

        def x_base(n):
            return 8 * (n if n < 5 else n - 1 + MH)

        def norm_act(act, n):
            for j in range(4):
                act.wait_ge(x_tile, x_base(n) + (8 if n == 2 else 2 * j + 2))
                S.activation(u[:, 2 * j:2 * j + 2, :], x[:, 2 * j:2 * j + 2, :], ACT.Square).then_inc(squares, 1)
            act.wait_ge(mean_sq, n + 1)
            S.activation(rms[:, :, :], ps[:, 4:6, 0:HB], ACT.Sqrt, bias=const("eps")).then_inc(rms_root, 1)

        def modulate_act(act, n, f=None):
            act.wait_ge(mods_done, 12)
            for kt in range(KT + 1):
                if kt < KT:
                    act.wait_ge(scaled, (KT + 1) * n + kt + 2)
                    S.activation(u[:, kt, 0:SEQ], u[:, kt, 0:SEQ], ACT.Identity,
                                 bias=mods[:, n * 24 + kt, 0:1],
                                 scale=mods[:, n * 24 + 8 + kt, 0:1]).then_inc(u_prompt, 1)
                if kt >= 1 and f is not None:
                    act.wait_ge(u_prompt, KT * n + kt)
                    act.wait_ge(u_dec, KT * f + kt)
                    S.activation(u_hi[:, kt - 1, :], u[:, kt - 1, :], ACT.Copy).then_inc(u_rounded, 1)

        def norm_pe(pe, n):
            if n == 0:
                pe.wait_ge(consts_in, 16 * 5)
            for j in range(4):
                pe.wait_ge(squares, 4 * n + j + 1)
                for kt in (2 * j, 2 * j + 1):
                    for hf in range(2):
                        last = PE.matmul(ps[:, 4 + hf, 0:HB], const("mean_d"), u[:, kt, hf * HB:hf * HB + HB],
                                         start=kt == 0, stop=kt == KT - 1, skip_group_check=True)
            last.then_inc(mean_sq, 1)

        def norm_dve(dve, n, link):
            dve.wait_ge(rms_root, n + 1)
            V.reciprocal(rms[:, :, :], rms[:, :, :]).then_inc(scaled, 1)
            dve.wait_ge(scaled, (KT + 1) * n + 1)
            r = rms[:, :, :].rearrange("p a b -> p (a b)")
            for kt in range(KT):
                V.tensor_tensor(u[:, kt, :], x[:, kt, :], r, ALU.mult).then_inc(scaled, 1)
            dve.wait_ge(scaled, (KT + 1) * (n + 1))
            if n == 6:
                for kt in range(KT):
                    V.tensor_scalar(u[:, kt, :], u[:, kt, :], norm_g[:, 6, kt:kt + 1], None,
                                    ALU.mult).then_inc(u_decode, 1)
                return
            ud = u[:, :, SEQ:T].rearrange("p k (b t) -> p k b t", t=DS)
            for kt in range(KT):
                sc = mods[:, n * 24 + 8 + kt, 1:C9].unsqueeze(2).to_broadcast([P, NB, DS])
                last = V.tensor_tensor(ud[:, kt], ud[:, kt], sc, ALU.mult)
            link(last)
            for kt in range(KT):
                sh = mods[:, n * 24 + kt, 1:C9].unsqueeze(2).to_broadcast([P, NB, DS])
                last = V.tensor_tensor(ud[:, kt], ud[:, kt], sh, ALU.add)
            last.then_inc(u_decode, 1)

        def split_norm_dve(dve, n, f, link):
            dve.wait_ge(rms_root, n + 1)
            V.reciprocal(rms[:, :, :], rms[:, :, :]).then_inc(scaled, 1)
            dve.wait_ge(scaled, (KT + 1) * n + 1)
            r = rms[:, :, :].rearrange("p a b -> p (a b)")
            for kt in range(KT + 2):
                if kt < KT:
                    V.tensor_tensor(u[:, kt, :], x[:, kt, :], r, ALU.mult).then_inc(scaled, 1)
                    dve.wait_ge(scaled, (KT + 1) * n + kt + 2)
                    ud = u[:, kt, SEQ:T].rearrange("p (b t) -> p b t", t=DS)
                    sc = mods[:, n * 24 + 8 + kt, 1:C9].unsqueeze(2).to_broadcast([P, NB, DS])
                    sh = mods[:, n * 24 + kt, 1:C9].unsqueeze(2).to_broadcast([P, NB, DS])
                    link(V.tensor_tensor(ud, ud, sc, ALU.mult))
                    V.tensor_tensor(ud, ud, sh, ALU.add).then_inc(u_dec, 1)
                if kt >= 2:
                    dve.wait_ge(u_rounded, KT * f + kt - 1)
                    V.tensor_tensor(u_lo[:, kt - 2, :], u[:, kt - 2, :], u_hi[:, kt - 2, :].bitcast(F32),
                                    ALU.subtract).then_inc(u_split, 1)

        def u_ready(pe, n):
            pe.wait_ge(u_prompt, KT * (n + 1))
            pe.wait_ge(u_decode, 1 if n == 1 else 2)

        def residual(n, m, pair, tmp, link):
            g = mods[:, n * 24 + 16 + m, :]
            rest = SEQ - HB
            V.scalar_tensor_tensor(x[:, m, 0:HB], ps[:, pair, 0:HB], g[:, 0:1], x[:, m, 0:HB], ALU.mult, ALU.add)
            V.scalar_tensor_tensor(x[:, m, HB:SEQ], ps[:, pair + 1, 0:rest], g[:, 0:1], x[:, m, HB:SEQ],
                                   ALU.mult, ALU.add)
            y = ps[:, pair + 1, rest:HB].rearrange("p (b t) -> p b t", t=DS)
            link(V.tensor_tensor(tmp.rearrange("p (b t) -> p b t", t=DS), y,
                                 g[:, 1:C9].unsqueeze(2).to_broadcast([P, NB, DS]), ALU.mult))
            V.tensor_tensor(x[:, m, SEQ:T], x[:, m, SEQ:T], tmp, ALU.add).then_inc(x_tile, 1)

        top[0] = 0
        K2 = FT // 2
        CHUNKS = FT + 2 * KT

        def half_in(g):
            return lambda v: v.rearrange("p (k c) -> p k c", c=256)[:, :, g * P:g * P + P]

        def half_out(g):
            return lambda v: v[:, 0:K2 * P].rearrange("p (k c) -> p k c", c=P)[:, 6 * g:6 + 5 * g]

        def parts(g, n):
            return [w_parts[:, g, part, 0:n * P].rearrange("p (k c) -> p k c", c=P) for part in range(2)]

        def split_products(dst, w, x_hi, x_lo, first, last):
            for a, xs, at in ((w[0], x_hi, 0), (w[0], x_lo, 1), (w[1], x_hi, 2)):
                for hf in range(2):
                    ins = PE.matmul(dst[hf], a, xs[:, hf * HB:hf * HB + HB], start=first and at == 0,
                                    stop=last and at == 2)
            return ins

        def round_weights(act, pl, k, it, base, rows):
            ch = Chunk(pl, k, it)
            act.wait_ge(full[ch.slot], ch.full_at)
            for g in range(2):
                act.wait_ge(w_used, ch.index * 2 + (2 * base + g + 1))
                S.activation(parts(g, rows[g])[0], (half_in if rows[0] == KT else half_out)(g)(ring[:, ch.slot, :]),
                             ACT.Copy).then_inc(w_rounded, 1)
                yield

        def rest_of_weights(dve, pl, k, it, base, rows):
            ch = Chunk(pl, k, it)
            for g in range(2):
                dve.wait_ge(w_rounded, ch.index * 2 + (2 * base + g + 1))
                hi, lo = parts(g, rows[g])
                src = (half_in if rows[0] == KT else half_out)(g)(ring[:, ch.slot, :])
                V.tensor_tensor(lo, src, hi.bitcast(F32), ALU.subtract).then_inc(done[ch.slot] if g else w_lo, 1)

        IN_ROWS, OUT_ROWS = (KT, KT), (6, 5)

        def ffn_pe(pe, f, n):
            c0 = CHUNKS * f

            def weights(ch, base, g):
                if g == 0:
                    pe.wait_ge(w_lo, ch.index + (base + 1))
                else:
                    pe.wait_ge(done[ch.slot], ch.done_at)

            for ch in chunks(pe, plan[f"in{f}"]):
                for g in range(2):
                    weights(ch, c0, g)
                    if g == 0:
                        pe.wait_ge(hidden, ch.index + (FT * f + 1))
                    w = parts(g, KT)
                    b = 4 * (ch.k % 2) + 2 * g
                    dst = [ps[:, b + hf, 0:HB] for hf in range(2)]
                    for kt in range(KT):
                        if g == 0:
                            pe.wait_ge(u_split, KT * f + kt + 1)
                        last = split_products(dst, (w[0][:, kt], w[1][:, kt]), u_hi[:, kt], u_lo[:, kt],
                                              kt == 0, kt == KT - 1)
                    last.then_inc(w_used, 1)
            pe.wait_ge(hidden, FT * (f + 1) + 2)
            for ch in chunks(pe, plan[f"out{f}"]):
                m2, half = ch.k // 2, ch.k % 2
                if half == 0:
                    pe.wait_ge(x_tile, (ch.index - ch.k) // 2 + (x_base(n) + 7 + m2))
                dst = [ps[:, 2 * m2 + hf, 0:HB] for hf in range(2)]
                for g in range(2):
                    weights(ch, c0 + FT, g)
                    if half == 0:
                        pe.wait_ge(h_split, FT * f + (FT - KT if g else K2 + 6 - KT))
                    elif g == 0:
                        pe.wait_ge(h_split, FT * f + FT)
                    w = parts(g, OUT_ROWS[g])
                    for k in range(OUT_ROWS[g]):
                        t = (0 if half else K2) + 6 * g + k
                        last = split_products(dst, (w[0][:, k], w[1][:, k]), h_hi[:, t], h_lo[:, t],
                                              half == 0 and g == 0 and k == 0,
                                              half == 1 and g == 1 and k == OUT_ROWS[1] - 1)
                    last.then_inc(w_used, 1)

        def ffn_act(act, f, n):
            p_in, p_out, c0 = plan[f"in{f}"], plan[f"out{f}"], CHUNKS * f
            rounds_in, rounds_out = FT // RING, 2 * KT // RING

            def all_of(steps):
                for _ in steps:
                    pass

            def silu(k, it):
                act.wait_ge(w_used, (it * RING + k) * 2 + (2 * c0 + 4))
                b = 4 * (k % 2)
                S.activation(sg[:, k % 2], ps[:, b:b + 2, 0:HB], ACT.Silu).then_inc(silus, 1)

            all_of(round_weights(act, p_in, 0, 0, c0, IN_ROWS))
            with act.Fori(0, rounds_in) as it:
                for k in range(RING):
                    nk, ni = (k + 1, it) if k + 1 < RING else (0, it + 1)
                    all_of(round_weights(act, p_in, nk, ni, c0, IN_ROWS))
                    silu(k, it)
            all_of(round_weights(act, p_in, 1, rounds_in, c0, IN_ROWS))
            silu(0, rounds_in)
            steps = round_weights(act, p_out, 0, 0, c0 + FT, OUT_ROWS)
            next(steps)
            silu(1, rounds_in)
            all_of(steps)
            for j in range(0, KT, 4):
                S.activation(h_hi[:, j:j + 4, :], u[:, j:j + 4, :], ACT.Copy).then_inc(h_rounded, 1)

            def out_round(it, last):
                for k in range(1, RING if last else RING + 1):
                    all_of(round_weights(act, p_out, k % RING, it + 1 if k == RING else it, c0 + FT, OUT_ROWS))

            with act.Fori(0, rounds_out - 1) as it:
                out_round(it, False)
            out_round(rounds_out - 1, True)

        def ffn_dve(dve, f, n, link):
            p_in, p_out, c0 = plan[f"in{f}"], plan[f"out{f}"], CHUNKS * f
            rounds_in, rounds_out = FT // RING, 2 * KT // RING

            def hide(k, it, defer):
                t = it * RING + k
                dve.wait_ge(silus, t + (FT * f + 1))
                b = 4 * (k % 2)
                if defer:
                    V.tensor_tensor(u[:, t, :].rearrange("p (a b) -> p a b", b=HB), sg[:, k % 2], ps[:, b + 2:b + 4, 0:HB],
                                    ALU.mult).then_inc(hidden, 1)
                    return
                V.tensor_tensor(sg[:, k % 2], sg[:, k % 2], ps[:, b + 2:b + 4, 0:HB], ALU.mult).then_inc(hidden, 1)
                dve.wait_ge(hidden, t + (FT * f + 3))
                whole = sg[:, k % 2].rearrange("p a b -> p (a b)")
                link(V.tensor_copy(h_hi[:, t, :], whole))
                V.tensor_tensor(h_lo[:, t, :], whole, h_hi[:, t, :].bitcast(F32), ALU.subtract).then_inc(h_split, 1)

            def in_rounds(a, b, defer):
                with dve.Fori(a, b) as it:
                    if not defer:
                        link.enter(it - a, RING)
                    for k in range(RING):
                        nk, ni = (k + 1, it) if k + 1 < RING else (0, it + 1)
                        rest_of_weights(dve, p_in, nk, ni, c0, IN_ROWS)
                        hide(k, it, defer)
                if not defer:
                    link.leave(b - a)

            rest_of_weights(dve, p_in, 0, 0, c0, IN_ROWS)
            in_rounds(0, KT // RING, True)
            in_rounds(KT // RING, rounds_in, False)
            rest_of_weights(dve, p_in, 1, rounds_in, c0, IN_ROWS)
            hide(0, rounds_in, False)
            rest_of_weights(dve, p_out, 0, 0, c0 + FT, OUT_ROWS)
            hide(1, rounds_in, False)
            for j in range(0, KT, 4):
                dve.wait_ge(h_rounded, 2 * f + j // 4 + 1)
                V.tensor_tensor(h_lo[:, j:j + 4, :], u[:, j:j + 4, :], h_hi[:, j:j + 4, :].bitcast(F32),
                                ALU.subtract).then_inc(h_split, 4)

            def out_round(it, last):
                for m2 in range(2):
                    k = 2 * m2 + 1
                    rest_of_weights(dve, p_out, k, it, c0 + FT, OUT_ROWS)
                    if m2 == 0:
                        rest_of_weights(dve, p_out, 2, it, c0 + FT, OUT_ROWS)
                    elif not last:
                        rest_of_weights(dve, p_out, 0, it + 1, c0 + FT, OUT_ROWS)
                    dve.wait_ge(w_used, it * 2 * RING + (2 * (c0 + FT + k) + 4))
                    residual(n, it * 2 + m2, 2 * m2, tmp_d[:, m2], link)

            with dve.Fori(0, rounds_out - 1) as it:
                link.enter(it, 2)
                out_round(it, False)
            link.leave(rounds_out - 1)
            out_round(rounds_out - 1, True)

        top[0] = 0
        qk = carve(16, T)
        vrow = carve(5, VR)
        oacc = carve(QT, HEADS * HD)
        kc_d = carve(NB, 256)
        vc_d = carve(NB, 256)
        w1 = carve(2, 16, P)
        w2k = carve(P)
        w2v = carve(HD)
        cpos = carve(2, 16)
        rope_cs = carve(2, T)
        kc_p = carve(4 * NCP)
        vc_p = carve(256)
        cc = carve(2)
        mx4 = carve(4)
        den4 = carve(4)
        cf4 = carve(4)
        YB = top[0]
        pairs = carve(2, 4, SEQ)
        raw = carve(2, T, at=YB)
        t1 = carve(T, at=YB + 2 * T)
        t2 = carve(T, at=YB + 3 * T)
        hid_p = carve(2, 4, NCP, at=8704 + 5 * VR + 4096 + 4096 + 4096 + P + HD + 32)
        f1 = carve(2, 2, 256, at=YB)
        hid = carve(2, 2, 256, at=YB + 1024)
        W1A = 8704 + 5 * VR + 4096 + 4096
        vtail = carve(NB, 512, at=W1A)
        qs = carve(NB, 2, 32, at=YB + 2048)
        sc = carve(NB, NCS, at=YB)
        pt_c = carve(NB, P, at=YB + 512)
        gm = carve(NB, 48, at=YB + 1536)
        prob = carve(4, SEQ, at=YB)
        pt = carve(QT, 4 * P, at=YB + 2048)
        RC = W1A + 4096 + P + HD + 32
        ocs = carve(NB, HD, at=RC)
        gs = carve(NB, 3, at=RC + 512)
        negm = carve(NB, 14, at=RC + 536)
        m8 = carve(NB, at=RC + 648)
        s8 = carve(NB, at=RC + 656)
        di8 = carve(NB, at=RC + 664)
        imp1 = carve(NB, NSEL, at=RC + 672)
        eqj = carve(NB, 14, at=RC + 808)
        m2s = carve(2, at=RC + 920)
        t2s = carve(2, at=RC + 922)
        nm2 = carve(2, at=RC + 924)
        d4 = carve(4, at=RC + 926)
        d2 = carve(2, at=RC + 930)
        c2 = carve(2, at=RC + 932)
        kcur = carve(4, DS, at=RC + 936)
        qcur = carve(2, 32, at=RC + 952)
        tmpo = carve(HD, at=RC + 1016)
        qkeep = sb("qkeep", [P, NB, 2, 32])
        osum = carve(NB, 2, HD, at=8704 + 5 * VR + 4096)
        vcur = carve(512, at=8704 + 5 * VR + 4096 + 1024)
        gtmp = carve(24, HEADS, at=8704 + 5 * VR + 4096)
        ps_d = carve(1544, at=YB)
        pts_d = carve(12 * P, at=YB + 1544)
        ptt_d = carve(256, at=YB + 1544 + 1536)

        nsa_in = sem("nsa_in")
        proj_even, raw_copied, rope_ps, roped = sem("proj_even"), sem("raw_copied"), sem("rope_ps"), sem("roped")
        row_ready, row_copied = sem("row_ready"), sem("row_copied")
        pairs_in, vtail_in = sem("pairs_in"), sem("vtail_in")
        cc_ready, cc_copied, conv_p, hid_p_ready, kc_p_ps, kc_p_copied = (sem(n) for n in (
            "cc_ready", "cc_copied", "conv_p", "hid_p_ready", "kc_p_ps", "kc_p_copied"))
        conv_d, f1_ready, h1_done, hid_ready, kc_ps, kc_copied = (sem(n) for n in (
            "conv_d", "f1_ready", "h1_done", "hid_ready", "kc_ps", "kc_copied"))
        q_staged, cs_ps, cs_shift, cs_exp, cs_prob, cs_tr, cs_trc, imp_ps, imp_copied, grp_ps, gm_ready, gsel_ps, sel_done = (
            sem(n) for n in ("q_staged", "cs_ps", "cs_shift", "cs_exp", "cs_prob", "cs_tr", "cs_trc", "imp_ps",
                             "imp_copied", "grp_ps", "gm_ready", "gsel_ps", "sel_done"))
        sc_ps, sc_max, sc_exp, sc_masked, tr_ps, tr_copied, o_ps, o_used = (sem(n) for n in (
            "sc_ps", "sc_max", "sc_exp", "sc_masked", "tr_ps", "tr_copied", "o_ps", "o_used"))
        d_staged, d_max, d_exp, d_tr, d_trc, d_ops = (sem(n) for n in (
            "d_staged", "d_max", "d_exp", "d_tr", "d_trc", "d_ops"))
        d_osum, ot_ps, ot_copied, otp_ps, otp_copied, aout_even = (sem(n) for n in (
            "d_osum", "ot_ps", "ot_copied", "otp_ps", "otp_copied", "aout_even"))

        ROPED = [t for t in range(16) if t not in (10, 11)]
        UNITS = [(br, g, qt) for br in range(3) for g in range(KVH) for qt in range(QT)]

        def page_loads(sp, ch, first_page, src):
            for j in range(4):
                page = sp.value_load(pages[0:1, bass.ds(first_page + j, 1)], min_val=0, max_val=NPOOL - 1)
                sp.dma_start(ring[:, ch.slot, j * 512:j * 512 + 512], src[page]).then_inc(full[ch.slot], 16)

        def nsa_sp(sp):
            load_chunks(sp, "qkv", lambda i: io["qkv"][i], SLOT)
            load_chunks(sp, "row", lambda i: io["row"][i], 2 * VR)
            for ch in chunks(sp, plan["cmp"]):
                sp.wait_ge(done[ch.slot], ch.free_at)
                page_loads(sp, ch, ch.index * 4, io["cmp_pages"])
            with sp.Fori(0, NB) as b:
                for k in range(4):
                    ch = Chunk(plan["selwin"], k, b)
                    sp.wait_ge(done[ch.slot], ch.free_at)
                    if k < 2:
                        page_loads(sp, ch, b * NPAGE + 4 * k, io["sel_pages"])
                    else:
                        sp.dma_start(ring[:, ch.slot, 0:1024], io["win"][k - 2, b]).then_inc(full[ch.slot], 16)
            load_chunks(sp, "aout", lambda i: io["attn_out"][i], SLOT)

        def nsa_pool(gp):
            gp.wait_ge(mods_done, 12)
            for b in range(NB):
                gp.dma_start(io["win_k_out"][b, :, :, 0:SEQ - DS],
                             io["win"][0, b].rearrange("p (g t) -> p g t", g=2)[:, :, DS:SEQ]).then_inc(stored, 16)
                gp.dma_start(io["win_v_out"][b, 0:SEQ - DS, :], io["win_v"][b, DS:SEQ, :]).then_inc(stored, 16)
            NSTORE[0] += 32 * NB
            gp.wait_ge(x_tile, 8 * 2)
            for dst, name in ((rope_cs, "rope"), (w1, "w1"), (w2k, "w2k"), (w2v, "w2v"), (cpos, "cpos")):
                gp.dma_start(dst, io[name]).then_inc(nsa_in, 16)
            gp.wait_ge(roped, 14)
            gp.wait_ge(raw_copied, 16)
            for half in range(2):
                for par in range(2):
                    src = qk[par * HD:par * HD + HD, 8:12, half:SEQ].rearrange("p (s g) t -> p s g t", s=2)
                    dst = pairs[half * HD:half * HD + HD, :, par::2, 0:SEQ - half]
                    for s in range(2):
                        gp.dma_start(dst[:, s], src[:, s]).then_inc(pairs_in, 16)
            gp.dma_start(io["kv_t"], qk[:, 8:16, :]).then_inc(stored, 16)
            gp.wait_ge(row_copied, 5)
            gp.dma_start(io["v_rows"], vrow[:, 0:QT, 0:512]).then_inc(stored, 16)
            gp.dma_start(io["v_rows_d"], vrow[0:NTS, QT, 0:512]).then_inc(stored, 16)
            NSTORE[0] += 48
            gp.wait_ge(kc_copied, 2 + NB)
            for b in range(NB):
                gp.dma_start(vtail[0:DS, b, :], vrow[DS * b:DS * b + DS, QT, 0:512]).then_inc(vtail_in, 16)

        def nsa_pe(pe):
            n = 1
            u_ready(pe, n)
            pe.wait_ge(nsa_in, 80)

            def rope(t):
                i = ROPED.index(t)
                pe.wait_ge(raw_copied, t + 1)
                if i >= 1:
                    pe.wait_ge(roped, i)
                for hf in range(2):
                    last = PE.matmul(ps[:, 4 + hf, 0:HB], const("rot"), raw[:, t % 2, hf * HB:hf * HB + HB],
                                     start=True, stop=True)
                last.then_inc(rope_ps, 1)

            for c in range(8):
                ch = Chunk(plan["qkv"], c % RING, c // RING)
                pe.wait_ge(full[ch.slot], ch.full_at)
                w = ring[:, ch.slot, :].rearrange("p (k c) -> p k c", c=256)
                for j in range(2):
                    t = 2 * c + j
                    if t >= 2:
                        pe.wait_ge(raw_copied, t - 1)
                    for kt in range(KT):
                        for hf in range(2):
                            last = PE.matmul(ps[:, 2 * j + hf, 0:HB], w[:, kt, j * P:j * P + P],
                                             u[:, kt, hf * HB:hf * HB + HB], start=kt == 0, stop=kt == KT - 1)
                    last.then_inc(done[ch.slot] if j else proj_even, 1)
                    if t - 1 in ROPED:
                        rope(t - 1)
            rope(15)
            row = [Chunk(plan["row"], k, 0) for k in range(4)]
            for i in range(5):
                rows = P if i < QT else NTS
                bk = 6 if i % 2 == 0 else 2
                if i == 0:
                    for ch in row:
                        pe.wait_ge(full[ch.slot], ch.full_at)
                if i == 1:
                    pe.wait_ge(raw_copied, 16)
                if i >= 2:
                    pe.wait_ge(row_copied, i - 1)
                for kt in range(KT):
                    w = ring[:, row[kt // 2].slot, (kt % 2) * VR:(kt % 2) * VR + VR]
                    a = u[:, kt, i * P:i * P + rows]
                    PE.matmul(ps[0:rows, bk, :], a, w[:, 0:512], start=kt == 0, stop=kt == KT - 1)
                    last = PE.matmul(ps[0:rows, bk + 1, 0:48], a, w[:, 512:VR], start=kt == 0, stop=kt == KT - 1)
                    if i == QT and kt % 2:
                        last.then_inc(done[row[kt // 2].slot], 1)
                if i < QT:
                    last.then_inc(row_ready, 1)
            pe.wait_ge(pairs_in, 16 * 8)
            for s in range(2):
                for lp in range(16):
                    last = PE.matmul(ps[:, 0, s:s + 1], w1[:, s, lp, :], cpos[:, s, lp:lp + 1],
                                     start=lp == 0, stop=lp == 15)
            last.then_inc(cc_ready, 1)
            for s in range(2):
                for lp in range(16):
                    last = PE.matmul(ps[:, 4 + s, 0:4 * NCP], w1[:, s, lp, :],
                                     pairs[:, s, :, 2 * lp:2 * lp + 16 * (NCP - 1) + 1:16],
                                     start=lp == 0, stop=lp == 15)
                last.then_inc(conv_p, 1)
            pe.wait_ge(hid_p_ready, 2)
            PE.matmul(ps[:, 1, 0:4 * NCP], w2k, hid_p[:, 0].rearrange("p a b -> p (a b)"), start=True, stop=True)
            for g in range(KVH):
                last = PE.matmul(ps[0:NCP, 0, g * HD:g * HD + HD], hid_p[:, 1, g, :], w2v, start=True, stop=True)
            last.then_inc(kc_p_ps, 1)
            pe.wait_ge(kc_p_copied, 1)
            with pe.Fori(0, NB // 2) as it:
                for pb in range(2):
                    chA, chB = Chunk(plan["cmp"], 2 * pb, it), Chunk(plan["cmp"], 2 * pb + 1, it)
                    assert chB.slot == chA.slot + 1
                    pe.wait_ge(full[chA.slot], chA.full_at)
                    pe.wait_ge(full[chB.slot], chB.full_at)
                    pe.wait_ge(h1_done, it * 4 + (2 * pb + 2))
                    X = ring[:, chA.slot:chA.slot + 2, :].rearrange("p a (q b n) -> p a q b n", q=4, n=32)
                    for s in range(2):
                        for part in range(2):
                            for lp in range(8):
                                last = PE.matmul(ps[:, 2 * pb + s, part * 256:part * 256 + 256],
                                                 w1[:, s, 8 * part + lp, :], X[:, :, :, s * 8 + lp, :],
                                                 start=lp == 0, stop=lp == 7)
                        last.then_inc(done[chB.slot] if s else conv_d, 1)
                for pb in range(2):
                    chA = Chunk(plan["cmp"], 2 * pb, it)
                    pe.wait_ge(hid_ready, it * 4 + (2 * pb + 2))
                    pe.wait_ge(kc_copied, it * 2 + (pb + 1))
                    PE.matmul(ps[:, 4 + pb, 0:256], w2k, hid[:, pb, 0, :], start=True,
                              stop=True).then_inc(done[chA.slot], 1)
                    for g in range(KVH):
                        last = PE.matmul(ps[0:HD, 6 + pb, g * HD:g * HD + HD], hid[:, pb, 1, g * HD:g * HD + HD],
                                         w2v, start=True, stop=True)
                    last.then_inc(kc_ps, 1)
            pe.wait_ge(kc_copied, 2 + NB)
            pe.wait_ge(q_staged, 1)
            for b in range(NB):
                for g in range(KVH):
                    par = (g % 2) * HD
                    last = PE.matmul(ps[32 * g:32 * g + 32, 0, b * NCS:b * NCS + NCS],
                                     qkeep[par:par + HD, b, g // 2, :],
                                     kc_d[par:par + HD, b, g * HD:g * HD + NCS], start=True, stop=True)
            last.then_inc(cs_ps, 1)
            pe.wait_ge(gm_ready, 1)
            PE.matmul(ps[:, 6, 0:NB * 48], const("pick_t", NTS), gm[0:NTS].rearrange("p a b -> p (a b)"),
                      start=True, stop=True).then_inc(gsel_ps, 1)
            pe.wait_ge(cs_prob, 1)
            for b in range(NB):
                last = PE.transpose(ps[0:NCS, 1 + b // 4, (b % 4) * P:(b % 4) * P + P], sc[:, b, :], const("ident"))
            last.then_inc(cs_tr, 1)
            pe.wait_ge(cs_trc, 1)
            for b in range(NB):
                last = PE.matmul(ps[:, 3, b * NSEL:b * NSEL + NSEL], pt_c[0:NCS, b, :], const("overlap", NCS),
                                 start=True, stop=True)
            last.then_inc(imp_ps, 1)
            for b in range(NB):
                for g in range(KVH):
                    last = PE.matmul(ps[32 * g:32 * g + 32, 4, b * HD:b * HD + HD],
                                     pt_c[0:NCS, b, 32 * g:32 * g + 32], vc_d[0:NCS, b, g * HD:g * HD + HD],
                                     start=True, stop=True)
            last.then_inc(imp_ps, 1)
            pe.wait_ge(imp_copied, 1)
            PE.matmul(ps[:, 5, 0:NB * NSEL], const("same_gt"), imp1.rearrange("p a b -> p (a b)"),
                      start=True, stop=True).then_inc(grp_ps, 1)
            pe.wait_ge(sel_done, 1)

            def keys(i):
                br, g, qt = UNITS[i]
                return NCP if br == 0 else (qt + 1) * P

            def scores(i):
                br, g, qt = UNITS[i]
                par = (g % 2) * HD
                nk = keys(i)
                k = (kc_p[par:par + HD, g * NCP:g * NCP + NCP] if br == 0 else
                     qk[par:par + HD, 10 + 2 * br + g // 2, 0:nk])
                if i >= 1:
                    pe.wait_ge(sc_exp, i)
                for r in range(REP):
                    last = PE.matmul(ps[:, r, 0:nk], qk[par:par + HD, (g // 2) * 4 + r, qt * P:qt * P + P], k,
                                     start=True, stop=True)
                last.then_inc(sc_ps, 1)

            scores(0)
            tiles = 0
            for i, (br, g, qt) in enumerate(UNITS):
                if i + 1 < len(UNITS):
                    scores(i + 1)
                nk = keys(i)
                nt = 1 if br == 0 else qt + 1
                pe.wait_ge(sc_masked if br == 0 else sc_exp, i + 1)
                for kt in range(nt):
                    w = min(P, nk - kt * P)
                    if tiles >= 2:
                        pe.wait_ge(tr_copied, tiles - 1)
                    for r in range(REP):
                        last = PE.transpose(ps[0:w, 4 + tiles % 2, r * P:r * P + P],
                                            prob[:, r, kt * P:kt * P + w], const("ident"))
                    last.then_inc(tr_ps, 1)
                    tiles += 1
                pe.wait_ge(tr_copied, tiles)
                if i >= 2:
                    pe.wait_ge(o_used, i - 1)
                for r in range(REP):
                    for kt in range(nt):
                        w = min(P, nk - kt * P)
                        v = (vc_p[0:NCP, g * HD:g * HD + HD] if br == 0 else
                             vrow[:, kt, (br - 1) * 256 + g * HD:(br - 1) * 256 + g * HD + HD])
                        last = PE.matmul(ps[:, 6 + i % 2, r * HD:r * HD + HD], pt[0:w, kt, r * P:r * P + P], v,
                                         start=kt == 0, stop=kt == nt - 1)
                last.then_inc(o_ps, 1)

            pe.wait_ge(o_used, len(UNITS))
            pe.wait_ge(vtail_in, 16 * NB)
            for b in range(NB):
                ch = [Chunk(plan["selwin"], k, b) for k in range(4)]
                pe.wait_ge(d_staged, b + 1)
                for c in ch:
                    pe.wait_ge(full[c.slot], c.full_at)
                for g in range(KVH):
                    par, gp = (g % 2) * HD, g // 2
                    q = qcur[par:par + HD, gp, :]
                    for j in range(2):
                        PE.matmul(ps[32 * g:32 * g + 32, j, :], q,
                                  ring[par:par + HD, ch[j].slot, :].rearrange("p (a c) -> p a c", a=4)[:, :, gp * P:gp * P + P],
                                  start=True, stop=True)
                    for j in range(2):
                        PE.matmul(ps[32 * g:32 * g + 32, 3, DS * j:DS * j + DS], q,
                                  kcur[par:par + HD, 2 * j + gp, :], start=True, stop=True)
                for g in range(KVH):
                    par, gp = (g % 2) * HD, g // 2
                    last = PE.matmul(ps[32 * g:32 * g + 32, 2, :], qcur[par:par + HD, gp, :],
                                     ring[par:par + HD, ch[2].slot, gp * SEQ:gp * SEQ + SEQ], start=True, stop=True)
                last.then_inc(done[ch[2].slot], 1)
                pe.wait_ge(d_exp, b + 1)
                pe.wait_ge(nsa_in, 80)
                for j in range(12):
                    PE.transpose(ps[:, 4 + j // 4, (j % 4) * P:(j % 4) * P + P], ps_d[:, j * P:j * P + P],
                                 const("ident"))
                for j in range(2):
                    last = PE.transpose(ps[0:DS, 7, 256 + j * P:256 + j * P + P],
                                        ps_d[:, 1536 + DS * j:1536 + DS * j + DS], const("ident"))
                last.then_inc(d_tr, 1)
                pe.wait_ge(d_trc, b + 1)
                for g in range(KVH):
                    o = ps[32 * g:32 * g + 32, 7, 0:HD]
                    for kt in range(8):
                        at = (kt % 4) * 512 + 256 + g * HD
                        m = PE.matmul(o, pts_d[:, kt * P + 32 * g:kt * P + 32 * g + 32],
                                      ring[:, ch[kt // 4].slot, at:at + HD], start=kt == 0, stop=False)
                        if g == 3 and kt % 4 == 3:
                            m.then_inc(done[ch[kt // 4].slot], 1)
                    PE.matmul(o, ptt_d[0:DS, 32 * g:32 * g + 32], vcur[0:DS, g * HD:g * HD + HD],
                              start=False, stop=True)
                    o = ps[32 * g:32 * g + 32, 7, HD:2 * HD]
                    for kt in range(4):
                        at = kt * 256 + g * HD
                        m = PE.matmul(o, pts_d[:, (8 + kt) * P + 32 * g:(8 + kt) * P + 32 * g + 32],
                                      ring[:, ch[3].slot, at:at + HD], start=kt == 0, stop=False)
                        if g == 3 and kt == 3:
                            m.then_inc(done[ch[3].slot], 1)
                    m = PE.matmul(o, ptt_d[0:DS, P + 32 * g:P + 32 * g + 32], vcur[0:DS, 256 + g * HD:256 + g * HD + HD],
                                  start=False, stop=True)
                m.then_inc(d_ops, 1)
            for qt in range(QT):
                if qt >= 2:
                    pe.wait_ge(otp_copied, qt - 1)
                for j in range(KT):
                    last = PE.transpose(ps[:, 2 + 2 * (qt % 2) + j // 4, (j % 4) * P:(j % 4) * P + P],
                                        oacc[:, qt, j * P:j * P + P], const("ident"))
                last.then_inc(otp_ps, 1)
            pe.wait_ge(d_osum, 1)
            for b in range(NB):
                last = PE.transpose(ps[:, b // 4, (b % 4) * P:(b % 4) * P + P],
                                    osum[:, b].rearrange("p a b -> p (a b)"), const("ident"))
            last.then_inc(ot_ps, 1)
            pe.wait_ge(otp_copied, QT)
            pe.wait_ge(ot_copied, 1)
            for c in range(4):
                ch = Chunk(plan["aout"], c, 0)
                pe.wait_ge(full[ch.slot], ch.full_at)
                w = ring[:, ch.slot, :].rearrange("p (k c) -> p k c", c=256)
                for j in range(2):
                    m = 2 * c + j
                    if m >= 2:
                        pe.wait_ge(x_tile, 8 * (n + 1) + m - 1)
                    for kt in range(KT):
                        for hf in range(2):
                            last = PE.matmul(ps[:, 2 * (m % 2) + hf, 0:HB], w[:, kt, j * P:j * P + P],
                                             u[:, kt, hf * HB:hf * HB + HB], start=kt == 0, stop=kt == KT - 1)
                    last.then_inc(done[ch.slot] if j else aout_even, 1)

        def nsa_act(act, link):
            for t in range(16):
                ch = Chunk(plan["qkv"], (t // 2) % RING, t // 2 // RING)
                if t % 2:
                    act.wait_ge(done[ch.slot], ch.done_at)
                else:
                    act.wait_ge(proj_even, t // 2 + 1)
                dst = qk[:, t] if t not in ROPED else raw[:, t % 2]
                if t in ROPED and t >= 2:
                    act.wait_ge(roped, sum(1 for z in ROPED if z <= t - 2))
                S.activation(dst.rearrange("p (a b) -> p a b", b=HB), ps[:, 2 * (t % 2):2 * (t % 2) + 2, 0:HB],
                             ACT.Copy).then_inc(raw_copied, 1)
            row3 = Chunk(plan["row"], 3, 0)
            for i in range(5):
                rows = P if i < QT else NTS
                bk = 6 if i % 2 == 0 else 2
                if i < QT:
                    act.wait_ge(row_ready, i + 1)
                else:
                    act.wait_ge(done[row3.slot], row3.done_at)
                S.activation(vrow[0:rows, i, 0:512], ps[0:rows, bk, :], ACT.Copy)
                S.activation(vrow[0:rows, i, 512:VR], ps[0:rows, bk + 1, 0:48], ACT.Sigmoid).then_inc(row_copied, 1)
            act.wait_ge(cc_ready, 1)
            S.activation(cc, ps[:, 0, 0:2], ACT.Copy).then_inc(cc_copied, 1)
            act.wait_ge(cc_copied, 1)
            for s in range(2):
                act.wait_ge(conv_p, s + 1)
                S.activation(hid_p[:, s].rearrange("p a b -> p (a b)"), ps[:, 4 + s, 0:4 * NCP],
                             ACT.Gelu_apprx_tanh, bias=cc[:, s:s + 1]).then_inc(hid_p_ready, 1)
            act.wait_ge(kc_p_ps, 1)
            S.activation(kc_p, ps[:, 1, 0:4 * NCP], ACT.Copy)
            S.activation(vc_p[0:NCP, :], ps[0:NCP, 0, 0:256], ACT.Copy).then_inc(kc_p_copied, 1)
            with act.Fori(0, NB // 2) as it:
                for pb in range(2):
                    chB = Chunk(plan["cmp"], 2 * pb + 1, it)
                    for s in range(2):
                        if s:
                            act.wait_ge(done[chB.slot], chB.done_at)
                        else:
                            act.wait_ge(conv_d, it * 2 + (pb + 1))
                        S.activation(f1[:, pb, s, :], ps[:, 2 * pb + s, 0:256], ACT.Copy).then_inc(f1_ready, 1)
                    for s in range(2):
                        act.wait_ge(h1_done, it * 4 + (2 * pb + s + 1 + 4))
                        S.activation(hid[:, pb, s].rearrange("p (g q n) -> p q g n", g=4, n=8),
                                     f1[:, pb, s].rearrange("p (q g n) -> p q g n", g=4, n=8),
                                     ACT.Gelu_apprx_tanh, bias=cc[:, s:s + 1]).then_inc(hid_ready, 1)
                for pb in range(2):
                    act.wait_ge(kc_ps, it * 2 + (pb + 1))
                    S.activation(kc_d[:, it * 2 + pb, :], ps[:, 4 + pb, 0:256], ACT.Copy)
                    S.activation(vc_d[0:HD, it * 2 + pb, :], ps[0:HD, 6 + pb, 0:256], ACT.Copy).then_inc(kc_copied, 1)
            act.wait_ge(cs_shift, 1)
            scf = sc.rearrange("p a b -> p (a b)")
            S.activation(scf, scf, ACT.Exp, scale=SCALE).then_inc(cs_exp, 1)
            act.wait_ge(cs_tr, 1)
            S.activation(pt_c[0:NCS].rearrange("p a b -> p (a b)"),
                         ps[0:NCS, 1:3, :].rearrange("p a b -> p (a b)"), ACT.Copy).then_inc(cs_trc, 1)
            act.wait_ge(sel_done, 1)

            def exps(i):
                br, g, qt = UNITS[i]
                nk = NCP if br == 0 else (qt + 1) * P
                act.wait_ge(sc_max, i + 1)
                for r in range(REP):
                    last = S.activation(prob[:, r, 0:nk], ps[:, r, 0:nk], ACT.Exp, scale=SCALE,
                                        bias=mx4[:, r:r + 1], accum_out=den4[:, r:r + 1])
                last.then_inc(sc_exp, 1)

            exps(0)
            tiles = 0
            for i, (br, g, qt) in enumerate(UNITS):
                nk = NCP if br == 0 else (qt + 1) * P
                for kt in range(1 if br == 0 else qt + 1):
                    w = min(P, nk - kt * P)
                    act.wait_ge(tr_ps, tiles + 1)
                    if kt == 0 and i >= 1:
                        act.wait_ge(o_ps, i)
                    S.activation(pt[0:w, kt, :], ps[0:w, 4 + tiles % 2, :], ACT.Copy).then_inc(tr_copied, 1)
                    tiles += 1
                if i + 1 < len(UNITS):
                    act.wait_ge(o_used, i + 1)
                    exps(i + 1)
            with act.Fori(0, NB) as b:
                act.wait_ge(d_max, b + 1)
                for j, (a0, a1, src) in enumerate(((0, 1024, ps[:, 0:2, :].rearrange("p a b -> p (a b)")),
                                                   (1024, 1536, ps[:, 2, :]),
                                                   (1536, 1540, ps[:, 3, 0:DS]), (1540, 1544, ps[:, 3, DS:2 * DS]))):
                    last = S.activation(ps_d[:, a0:a1], src, ACT.Exp, scale=SCALE, bias=nm2[:, j % 2:j % 2 + 1],
                                        accum_out=d4[:, j:j + 1])
                last.then_inc(d_exp, 1)
                act.wait_ge(d_tr, b + 1)
                S.activation(pts_d, ps[:, 4:7, :].rearrange("p a b -> p (a b)"), ACT.Copy)
                S.activation(ptt_d[0:DS, :], ps[0:DS, 7, 256:512], ACT.Copy).then_inc(d_trc, 1)
            for qt in range(QT):
                act.wait_ge(otp_ps, qt + 1)
                b0 = 2 + 2 * (qt % 2)
                S.activation(u[:, :, qt * P:qt * P + P],
                             ps[:, b0:b0 + 2, :].rearrange("p a (b c) -> p (a b) c", c=P), ACT.Copy).then_inc(otp_copied, 1)

        def nsa_dve(dve, link):
            dve.wait_ge(nsa_in, 80)
            for i, t in enumerate(ROPED):
                dve.wait_ge(raw_copied, t + 1)
                link(V.tensor_tensor(t1, raw[:, t % 2], rope_cs[:, 0], ALU.mult))
                dve.wait_ge(rope_ps, i + 1)
                link(V.tensor_tensor(t2.rearrange("p (a b) -> p a b", b=HB), ps[:, 4:6, 0:HB],
                                     rope_cs[:, 1].rearrange("p (a b) -> p a b", b=HB), ALU.mult))
                V.tensor_tensor(qk[:, t], t1, t2, ALU.add).then_inc(roped, 1)
                dve.wait_ge(roped, i + 1)
            link(V.memset(qkeep[:, :, :, :], 0.0))
            V.memset(m8[0:1, 0:1], 0.0).then_inc(h1_done, 4)
            V.memset(s8[0:1, 0:1], 0.0).then_inc(kc_copied, 2)
            for gp in range(2):
                last = V.tensor_copy(qkeep[:, :, gp, 0:16].rearrange("p b (r t) -> p b r t", t=DS),
                                     qk[:, 4 * gp:4 * gp + 4, SEQ:T].rearrange("p r (b t) -> p b r t", t=DS))
            last.then_inc(q_staged, 1)
            with dve.Fori(0, NB // 2) as it:
                for pb in range(2):
                    for s in range(2):
                        dve.wait_ge(f1_ready, it * 4 + (2 * pb + s + 1))
                        a = f1[:, pb, s].rearrange("p (q g n) -> p q g n", g=4, n=8)
                        b2 = ps[:, 2 * pb + s, 256:512].rearrange("p (q g n) -> p q g n", g=4, n=8)
                        V.tensor_tensor(a[:, :, :, 0:7], a[:, :, :, 0:7], b2[:, :, :, 1:8], ALU.add)
                        V.tensor_tensor(a[:, 0:7, :, 7], a[:, 0:7, :, 7], b2[:, 1:8, :, 0],
                                        ALU.add).then_inc(h1_done, 1)
            dve.wait_ge(row_copied, 5)
            dve.wait_ge(kc_copied, 2 + NB)
            V.tensor_tensor(gm[0:NTS], vrow[0:NTS, QT, 512:VR].unsqueeze(1).to_broadcast([NTS, NB, 48]),
                            const("own_b", NTS).unsqueeze(2).to_broadcast([NTS, NB, 48]), ALU.mult).then_inc(gm_ready, 1)
            dve.wait_ge(cs_ps, 1)
            s0 = ps[:, 0, 0:NB * NCS].rearrange("p (a b) -> p a b", b=NCS)
            link(V.tensor_reduce(m8, s0, AX.X, ALU.max))
            V.tensor_tensor(sc, s0, m8.unsqueeze(2).to_broadcast([P, NB, NCS]), ALU.subtract).then_inc(cs_shift, 1)
            dve.wait_ge(cs_exp, 1)
            link(V.tensor_reduce(s8, sc, AX.X, ALU.add))
            link(V.reciprocal(s8, s8))
            V.tensor_tensor(sc, sc, s8.unsqueeze(2).to_broadcast([P, NB, NCS]), ALU.mult).then_inc(cs_prob, 1)
            dve.wait_ge(gsel_ps, 1)
            hof = const("head_of").unsqueeze(1).to_broadcast([P, 24, HEADS])
            link(V.tensor_tensor(gtmp, ps[:, 6, 0:NB * 48].rearrange("p (a b) -> p a b", b=HEADS), hof, ALU.mult))
            link(V.tensor_reduce(gs.rearrange("p a b -> p (a b)"), gtmp, AX.X, ALU.add))
            dve.wait_ge(imp_ps, 1)
            V.tensor_copy(imp1.rearrange("p a b -> p (a b)"), ps[:, 3, 0:NB * NSEL]).then_inc(imp_copied, 1)
            dve.wait_ge(imp_ps, 2)
            link(V.tensor_tensor(ocs, ps[:, 4, :].rearrange("p (a b) -> p a b", b=HD),
                                 gs[:, :, 0:1].to_broadcast([P, NB, HD]), ALU.mult))
            dve.wait_ge(grp_ps, 1)
            im = ps[:, 5, 0:NB * NSEL].rearrange("p (a b) -> p a b", b=NSEL)[:, :, 1:15]
            no = const("block_no")[:, 1:15].unsqueeze(1).to_broadcast([P, NB, 14])
            link(V.tensor_reduce(m8, im, AX.X, ALU.min))
            link(V.tensor_tensor(eqj, im, m8.unsqueeze(2).to_broadcast([P, NB, 14]), ALU.is_equal))
            link(V.tensor_tensor(eqj, eqj, no, ALU.mult))
            link(V.tensor_reduce(di8, eqj, AX.X, ALU.max))
            link(V.tensor_tensor(eqj, di8.unsqueeze(2).to_broadcast([P, NB, 14]), no, ALU.is_equal))
            V.tensor_scalar(negm, eqj, NEG, None, ALU.mult).then_inc(sel_done, 1)

            def mask_max(i):
                br, g, qt = UNITS[i]
                dve.wait_ge(sc_ps, i + 1)
                nk = NCP if br == 0 else (qt + 1) * P
                if br == 0:
                    blk = ps[:, 0:4, 0:NCP]
                    msk = const("cmp_neg")[:, qt * NCP:qt * NCP + NCP].unsqueeze(1).to_broadcast([P, 4, NCP])
                else:
                    blk = ps[:, 0:4, qt * P:qt * P + P]
                    msk = const("causal").unsqueeze(1).to_broadcast([P, 4, P])
                link(V.tensor_tensor(blk, blk, msk, ALU.add))
                link(V.tensor_reduce(mx4, ps[:, 0:4, 0:nk], AX.X, ALU.max))
                V.tensor_scalar(mx4, mx4, -SCALE, None, ALU.mult).then_inc(sc_max, 1)

            mask_max(0)
            for i, (br, g, qt) in enumerate(UNITS):
                dve.wait_ge(sc_exp, i + 1)
                if br == 0:
                    pv = prob[:, :, 0:NCP]
                    vd = const("cmp_valid")[:, qt * NCP:qt * NCP + NCP].unsqueeze(1).to_broadcast([P, 4, NCP])
                    V.tensor_tensor(pv, pv, vd, ALU.mult).then_inc(sc_masked, 1)
                if i + 1 < len(UNITS):
                    mask_max(i + 1)
                link(V.reciprocal(cf4, den4))
                link(V.tensor_tensor(cf4, cf4, vrow[:, qt, 512 + br * HEADS + g * REP:512 + br * HEADS + g * REP + REP],
                                     ALU.mult))
                dve.wait_ge(o_ps, i + 1)
                o = ps[:, 6 + i % 2, 0:256].rearrange("p (r d) -> p r d", d=HD)
                cb = cf4.unsqueeze(2).to_broadcast([P, REP, HD])
                acc = oacc[:, qt, g * 256:g * 256 + 256].rearrange("p (r d) -> p r d", d=HD)
                if br == 0:
                    V.tensor_tensor(acc, o, cb, ALU.mult).then_inc(o_used, 1)
                else:
                    tv = tmp256[:, :].rearrange("p (r d) -> p r d", d=HD)
                    link(V.tensor_tensor(tv, o, cb, ALU.mult))
                    V.tensor_tensor(acc, acc, tv, ALU.add).then_inc(o_used, 1)
                dve.wait_ge(o_used, i + 1)

            dve.wait_ge(vtail_in, 16 * NB)
            with dve.Fori(0, NB) as b:
                link.enter(b, 9)
                V.tensor_copy(qcur, qkeep[:, b])
                V.tensor_copy(kcur, qk[:, 12:16, bass.ds(b * DS + SEQ, DS)])
                V.tensor_copy(vcur[0:DS, :], vtail[0:DS, b, :]).then_inc(d_staged, 1)
                kwin = Chunk(plan["selwin"], 2, b)
                dve.wait_ge(done[kwin.slot], kwin.done_at)
                blk = ps[:, 0:2, :].rearrange("p a b -> p (a b)")[:, 64:960].rearrange("p (a b) -> p a b", b=64)
                V.tensor_tensor(blk, blk, negm[:, b].unsqueeze(2).to_broadcast([P, 14, 64]), ALU.add)
                V.tensor_tensor(ps[:, 2, 0:DS], ps[:, 2, 0:DS], const("win_edge"), ALU.add)
                link(V.tensor_tensor(ps[:, 3, 0:2 * DS], ps[:, 3, 0:2 * DS], const("tails"), ALU.add))
                V.tensor_reduce(m2s[:, 0:1], ps[:, 0:2, :].rearrange("p a b -> p (a b)"), AX.X, ALU.max)
                V.tensor_reduce(m2s[:, 1:2], ps[:, 2, :], AX.X, ALU.max)
                link(V.tensor_reduce(t2s, ps[:, 3, 0:2 * DS].rearrange("p (a b) -> p a b", b=DS), AX.X, ALU.max))
                link(V.tensor_tensor(m2s, m2s, t2s, ALU.max))
                V.tensor_scalar(nm2, m2s, -SCALE, None, ALU.mult).then_inc(d_max, 1)
                dve.wait_ge(d_exp, b + 1)
                link(V.tensor_tensor(d2, d4[:, 0:2], d4[:, 2:4], ALU.add))
                link(V.reciprocal(d2, d2))
                link(V.tensor_tensor(c2, d2, gs[:, b, 1:3], ALU.mult))
                dve.wait_ge(d_ops, b + 1)
                link(V.scalar_tensor_tensor(tmpo, ps[:, 7, 0:HD], c2[:, 0:1], ocs[:, b, :], ALU.mult, ALU.add))
                link(V.scalar_tensor_tensor(osum[:, b, 0, :], ps[:, 7, HD:2 * HD], c2[:, 1:2], tmpo, ALU.mult, ALU.add))
                link(V.tensor_copy(osum[:, b, 1, :], osum[:, b, 0, :]))
            link.leave(NB)
            V.tensor_copy(tmpo[0:1, 0:1], osum[0:1, NB - 1, 1, 0:1]).then_inc(d_osum, 1)
            dve.wait_ge(ot_ps, 1)
            for par in range(2):
                for rh in range(2):
                    for bh in range(2):
                        src = ps[par * HD:par * HD + HD, bh, :].rearrange("p (b g r t) -> p g b r t", b=4, g=4, r=8)
                        dst = u[par * HD:par * HD + HD, rh::2, SEQ + 16 * bh:SEQ + 16 * bh + 16]
                        last = V.tensor_copy(dst.rearrange("p g (b t) -> p g b t", t=DS), src[:, :, :, 2 * rh + par, :])
            last.then_inc(ot_copied, 1)
            for m in range(KT):
                ch = Chunk(plan["aout"], m // 2, 0)
                if m % 2:
                    dve.wait_ge(done[ch.slot], ch.done_at)
                else:
                    dve.wait_ge(aout_even, m // 2 + 1)
                residual(1, m, 2 * (m % 2), tmp_d[:, m % 2], link)
        top[0] = 0
        mrow = carve(T)
        m0r = carve(NB)
        bg = carve(1)
        acol = carve(5, MH)
        wcol = carve(5, MH)
        emcol = carve(MH)
        ncm = carve(MH, T)
        em = carve(MH, T)
        wint = carve(MH, NTS)
        xp = carve(4, XPW)
        acc = carve(4, XPW)
        xc = carve(4, T)
        zs = carve(4, T)
        qT = carve(4, T)
        kT = carve(4, T)
        vr = carve(5, SEQ)
        kw = carve(5, SEQ)
        bd = carve(3, 4, P)
        ex = carve(2, SEQ)
        vb = carve(2, SEQ)
        convw = carve(16, 5)
        skipgn = carve(16, 2)
        nst = carve(16, NB)
        sconv = carve(16, NB * 3)
        nnew = carve(16, C9)
        cvo = carve(16, C9 * 3)
        qw = carve(4, NTS)
        nprod = carve(4, NTS)
        ssp = carve(NTS)[0:NTS]
        den1 = carve(1)[0:NTS]
        rden = carve(SEQ)
        xm_d = carve(4, NTS)
        AT_ACC = 544 + 8 + 1 + 20 + 20 + 4 + 2 * MH * T + MH * NTS + 4 * XPW
        spt = carve(4, SEQ, at=AT_ACC)
        qwm = ex.rearrange("p a b -> p (a b)").rearrange("p (a b c) -> p a b c", a=4, b=NB)
        work = xp[:, :, 0:T]
        ig, lf, cumf, av, cm, wsr = (carve(T, at=AT_ACC + 4 * XPW + i * T) for i in range(6))
        hrow = qkeep[0:NTS].rearrange("p a b c -> p (a b c)")
        KS = MHD ** -0.5
        c_stored = [sem(f"c_stored{i}") for i in range(RING)]

        (ml_in, bd_in, gt_dve, gt_act, col_ps, bc_ps, bc_copied, gates_done) = (sem(n) for n in (
            "ml_in bd_in gt_dve gt_act col_ps bc_ps bc_copied gates_done").split())
        (pr_even, pr_copied, xp_ready, conv_init, conv_done, xc_ready, qk_ps, qk_copied, vk_ps, vk_copied, sm_ps, ex_ready,
         ex_done, sp_ready, h_ps, h_scaled, h_sq, h_ms, h_root, hn_ready, y_even, qw_ready, s_ps, s_pre, s_exp, ssp_ready,
         vb_ready, up_ps, c_new, hd_scaled, hdt_ps, cf_ps, cf_copied, cf_stored, nn_ps, nn_done) = (sem(n) for n in (
             "pr_even pr_copied xp_ready conv_init conv_done xc_ready qk_ps qk_copied vk_ps vk_copied sm_ps ex_ready "
             "ex_done sp_ready h_ps h_scaled h_sq h_ms h_root hn_ready y_even qw_ready s_ps s_pre s_exp ssp_ready "
             "vb_ready up_ps c_new hd_scaled hdt_ps cf_ps cf_copied cf_stored nn_ps nn_done").split())

        def hchunk(h, k):
            pl = plan["mlstm"]
            n0, _, fu, do, full0, done0 = pl
            s = (n0 + k) % RING
            f_head = sum(fu[j % len(fu)] for j in range(16) if (j - k) % RING == 0)
            d_head = sum(do[j % len(do)] for j in range(16) if (j - k) % RING == 0)
            f_before = sum(16 for j in range(k) if (j - k) % RING == 0)
            d_before = sum(do[j] for j in range(k) if (j - k) % RING == 0)
            c = Chunk.__new__(Chunk)
            c.slot, c.k = s, k
            c.full_at = h * f_head + (full0[s] + f_before + 16)
            c.free_at = h * d_head + (done0[s] + d_before)
            c.done_at = h * d_head + (done0[s] + d_before + do[k])
            return c

        def mlstm_sp(sp):
            for ch in (Chunk(plan["mgate"], 0, 0),):
                sp.wait_ge(done[ch.slot], ch.free_at)
                sp.dma_start(ring[:, ch.slot, 0:KT * 36], io["mgate"]).then_inc(full[ch.slot], 16)
            with sp.Fori(0, MH) as h:
                for k in range(16):
                    ch = hchunk(h, k)
                    if 8 <= k:
                        sp.wait_ge(c_stored[ch.slot], h * 32 + (16 if k < 12 else 32))
                    else:
                        sp.wait_ge(done[ch.slot], ch.free_at)
                    if k < 4:
                        src, w = io["ml_in"][h * 4 + k], SLOT
                    elif k < 12:
                        src, w = io["state_c"][h * NB + (k - 4)], SLOT
                    else:
                        src, w = io["ml_out"][h * 4 + (k - 12)], 1024
                    sp.dma_start(ring[:, ch.slot, 0:w], src).then_inc(full[ch.slot], 16)

        def mlstm_pool(gp):
            gp.wait_ge(x_tile, 8 * 5)
            for dst, name in ((convw, "convw"), (skipgn, "skipgn"), (nst, "nst"), (sconv, "sconv")):
                gp.dma_start(dst[:, :, :], io[name]).then_inc(ml_in, 16)
            gp.dma_start(m0r[0:MH, :], io["m0"]).then_inc(ml_in, 16)
            gp.dma_start(bg[0:36, :], io["bg"]).then_inc(ml_in, 16)
            gp.dma_start(bd, io["bd"][0]).then_inc(bd_in, 16)

            def head(h, last):
                gp.wait_ge(vk_ps, h * 10 + 10)
                if not last:
                    gp.dma_start(bd, io["bd"][h + 1]).then_inc(bd_in, 16)
                gp.wait_ge(cf_copied, h + 1)
                gp.dma_start(io["cp_out"][h], spt.rearrange("p a b -> p (a b)")).then_inc(cf_stored, 16)
                for b in range(NB):
                    gp.wait_ge(c_new, h * NB + (b + 1))
                    gp.dma_start(io["c_out"][h * NB + b], ring[:, hchunk(h, 4 + b).slot, :])\
                        .then_inc(c_stored[hchunk(h, 4 + b).slot], 16)

            with gp.Fori(0, MH - 1) as h:
                head(h, False)
            head(MH - 1, True)
            gp.dma_start(io["m_out"], mrow[0:MH, :]).then_inc(stored, 16)
            gp.wait_ge(nn_done, MH)
            gp.dma_start(io["n_out"], nnew[:, :, :]).then_inc(stored, 16)
            gp.dma_start(io["conv_out"], cvo[:, :, :]).then_inc(stored, 16)
            NSTORE[0] += 48
            gp.wait_ge(cf_stored, 16 * MH)
            for s in range(RING):
                gp.wait_ge(c_stored[s], 16 * 2 * MH)

        def mlstm_pe(pe):
            n = 4
            u_ready(pe, n)
            ch = Chunk(plan["mgate"], 0, 0)
            pe.wait_ge(full[ch.slot], ch.full_at)
            w = ring[:, ch.slot, 0:KT * 36].rearrange("p (k c) -> p k c", c=36)
            for kt in range(KT):
                for hf in range(2):
                    last = PE.matmul(ps[0:36, hf, 0:HB], w[:, kt, :], u[:, kt, hf * HB:hf * HB + HB],
                                     start=kt == 0, stop=kt == KT - 1)
            last.then_inc(done[ch.slot], 1)
            pe.wait_ge(gates_done, 1)
            for r, (row, o) in enumerate(((av, 0), (wsr, 20), (em, 40))):
                src = row if r < 2 else em[:, 0]
                for i in range(5):
                    if r == 2 and i < 4:
                        continue
                    rows = P if i < 4 else NTS
                    last = PE.matmul(ps[0:rows, 2, o + MH * i:o + MH * i + MH],
                                     (src[0:MH, i * P:i * P + rows]), const("ident", MH)[:, 0:MH],
                                     start=True, stop=True)
            last.then_inc(col_ps, 1)
            for r, row in enumerate((cm, mrow)):
                for hh in range(MH):
                    j = r * MH + hh
                    if j >= 2:
                        pe.wait_ge(bc_copied, j - 1)
                    for hf in range(2):
                        last = PE.matmul(ps[:, 4 + 2 * (j % 2) + hf, 0:HB], const("head_row", MH)[:, hh * P:hh * P + P],
                                         row[0:MH, hf * HB:hf * HB + HB], start=True, stop=True)
                    last.then_inc(bc_ps, 1)
            for hh in range(MH):
                last = PE.matmul(ps[:, 3, hh * NTS:hh * NTS + NTS], const("head_row", MH)[:, hh * P:hh * P + P],
                                 lf[0:MH, SEQ:T], start=True, stop=True)
            last.then_inc(bc_ps, 1)
            pe.wait_ge(gates_done, 2)

            with pe.Fori(0, MH) as h:
                for k in range(4):
                    c = hchunk(h, k)
                    pe.wait_ge(full[c.slot], c.full_at)
                    w = ring[:, c.slot, :].rearrange("p (k c) -> p k c", c=256)
                    for j in range(2):
                        t = 2 * k + j
                        if t >= 2:
                            pe.wait_ge(pr_copied, h * 8 + (t - 1))
                        for kt in range(KT):
                            for hf in range(2):
                                last = PE.matmul(ps[:, 2 * j + hf, 0:HB], w[:, kt, j * P:j * P + P],
                                                 u[:, kt, hf * HB:hf * HB + HB], start=kt == 0, stop=kt == KT - 1)
                        last.then_inc(done[c.slot] if j else pr_even, 1)
                pe.wait_ge(bd_in, h * 16 + 16)
                pe.wait_ge(xc_ready, h * 4 + 4)
                for t in range(8):
                    b0 = 4 + 2 * (t % 2)
                    if t >= 2:
                        pe.wait_ge(qk_copied, h * 8 + (t - 1))
                    for hf in range(2):
                        last = PE.matmul(ps[:, b0 + hf, 0:HB], bd[:, t // 4, t % 4, :],
                                         xc[:, t % 4, hf * HB:hf * HB + HB], start=True, stop=True)
                    last.then_inc(qk_ps, 1)
                pe.wait_ge(pr_copied, h * 8 + 8)
                pe.wait_ge(bd_in, 16)
                for i in range(5):
                    rows = P if i < 4 else NTS
                    for v in range(2):
                        j = 2 * i + v
                        if j >= 4:
                            pe.wait_ge(vk_copied, h * 10 + (j - 3))
                        for t in range(4):
                            if v == 0:
                                a = xp[:, t, 3 + i * P:3 + i * P + P] if i < 4 else xm_d[:, t, :]
                            else:
                                a = xc[:, t, i * P:i * P + rows]
                            last = PE.matmul(ps[0:rows, j % 4, t * P:t * P + P], a, bd[:, 2 if v == 0 else 1, t, :],
                                             start=True, stop=True)
                        last.then_inc(vk_ps, 1)
                pe.wait_ge(qk_copied, h * 8 + 8)
                for t in range(4):
                    last = PE.matmul(ps[0:NTS, 4, 0:NTS], kT[:, t, SEQ:T], qT[:, t, SEQ:T], start=t == 0, stop=t == 3)
                last.then_inc(s_ps, 1)
                for i in range(4):
                    if i >= 2:
                        pe.wait_ge(sp_ready, h * 4 + (i - 1))
                    for t in range(4):
                        last = PE.matmul(ps[:, 5, 0:SEQ - i * P] if i % 2 == 0 else ps[:, 6, 0:SEQ - i * P],
                                         kT[:, t, i * P:i * P + P], qT[:, t, i * P:SEQ], start=t == 0, stop=t == 3)
                    last.then_inc(sm_ps, 1)
                pe.wait_ge(sp_ready, h * 4 + 4)
                pe.wait_ge(vk_copied, h * 10 + 10)
                for i in range(4):
                    last = PE.matmul(ps[:, 7, i * P:SEQ], const("ones"), spt[:, i, 0:SEQ - i * P],
                                     start=i == 0, stop=i == 3)
                for e in range(4):
                    for i in range(4):
                        last = PE.matmul(ps[:, e, i * P:SEQ], vr[:, i, e * P:e * P + P], spt[:, i, 0:SEQ - i * P],
                                         start=i == 0, stop=i == 3)
                last.then_inc(h_ps, 1)
                pe.wait_ge(qw_ready, h + 1)
                pe.wait_ge(ssp_ready, h + 1)
                for t in range(4):
                    PE.matmul(ps[0:NTS, 6, 0:1], nprod[:, t, :], const("ones")[:, 0:1], start=t == 0, stop=False)
                PE.matmul(ps[0:NTS, 6, 0:1], ssp[:, :], const("ones", NTS)[:, 0:1], start=False, stop=True)
                PE.matmul(ps[0:NTS, 5, :], ssp[:, :], vr[0:NTS, 4, :], start=True, stop=False)
                pe.wait_ge(h_scaled, h + 1)
                for t in range(4):
                    for i in range(4):
                        last = PE.matmul(ps[:, t, :], kw[:, i, t * P:t * P + P], vr[:, i, :], start=i == 0, stop=i == 3)
                last.then_inc(cf_ps, 1)
                for t in range(4):
                    for i in range(4):
                        last = PE.matmul(ps[:, 4, t * C9:t * C9 + 1], kw[:, i, t * P:t * P + P], const("ones")[:, 0:1],
                                         start=i == 0, stop=i == 3)
                    last = PE.matmul(ps[:, 4, t * C9 + 1:t * C9 + C9], kw[0:NTS, 4, t * P:t * P + P],
                                     const("own_b", NTS), start=True, stop=True)
                last.then_inc(nn_ps, 1)
                for b in range(NB):
                    c = hchunk(h, 4 + b)
                    pe.wait_ge(full[c.slot], c.full_at)
                    if b == 0:
                        pe.wait_ge(cf_copied, h + 1)
                    for t in range(4):
                        last = PE.matmul(ps[0:NTS, 5, :], qwm[:, t, b, :], ring[:, c.slot, t * SEQ:t * SEQ + SEQ],
                                         start=False, stop=b == NB - 1 and t == 3)
                    pe.wait_ge(vb_ready, h * NB + (b + 1))
                    if b:
                        pe.wait_ge(c_new, h * NB + b)
                    for t in range(4):
                        last = PE.matmul(ps[:, t, :], kw[0:NTS, 4, t * P:t * P + P], vb[0:NTS, b % 2, :],
                                         start=True, stop=True)
                    last.then_inc(up_ps, 1)
                pe.wait_ge(hd_scaled, h + 1)
                for t in range(4):
                    last = PE.matmul(ps[:, 7, t * NTS:t * NTS + NTS], hrow[:, t * P:t * P + P],
                                     const("ident", NTS)[:, 0:NTS], start=True, stop=True)
                last.then_inc(hdt_ps, 1)
                pe.wait_ge(h_sq, h + 1)
                for t in range(4):
                    for hf in range(2):
                        last = PE.matmul(ps[:, 5 + hf, 0:HB], const("mean_h"), work[:, t, hf * HB:hf * HB + HB],
                                         start=t == 0, stop=t == 3)
                last.then_inc(h_ms, 1)
                pe.wait_ge(hn_ready, h + 1)
                for k in range(4):
                    c = hchunk(h, 12 + k)
                    pe.wait_ge(full[c.slot], c.full_at)
                    w = ring[:, c.slot, 0:1024].rearrange("p (k c) -> p k c", c=256)
                    for j in range(2):
                        m = 2 * k + j
                        pe.wait_ge(x_tile, h * 8 + (8 * (n + 1) + m - 1 if m >= 2 else 8 * (n + 1)))
                        for t in range(4):
                            for hf in range(2):
                                last = PE.matmul(ps[:, 2 * j + hf, 0:HB], w[:, t, j * P:j * P + P],
                                                 zs[:, t, hf * HB:hf * HB + HB], start=t == 0, stop=t == 3)
                        last.then_inc(done[c.slot] if j else y_even, 1)
                pe.wait_ge(x_tile, h * 8 + 8 * (n + 2))
                pe.wait_ge(nn_done, h + 1)

        def mlstm_act(act, link):
            act.wait_ge(ml_in, 16 * 6)
            act.wait_ge(gt_dve, 1)
            S.activation(cumf[0:MH, :], av[0:MH, :], ACT.Exp).then_inc(gt_act, 1)
            act.wait_ge(gt_act, 1)
            S.activation(av[0:MH, :], cumf[0:MH, :], ACT.Ln, bias=1.0).then_inc(gt_act, 1)
            act.wait_ge(gt_dve, 2)
            S.activation(em[0:MH, 0, :], mrow[0:MH, :], ACT.Exp, scale=-1.0)
            S.activation(wsr[0:MH, :], wsr[0:MH, :], ACT.Exp)
            S.activation(lf[0:MH, SEQ:T], lf[0:MH, SEQ:T], ACT.Exp).then_inc(gates_done, 1)
            act.wait_ge(col_ps, 1)
            ac, wc = acol.rearrange("p a b -> p (a b)"), wcol.rearrange("p a b -> p (a b)")
            S.activation(ac[:, 0:16], ps[:, 2, 0:16], ACT.Copy)
            S.activation(ac[0:NTS, 16:20], ps[0:NTS, 2, 16:20], ACT.Copy)
            S.activation(wc[:, 0:16], ps[:, 2, 20:36], ACT.Copy, scale=KS)
            S.activation(wc[0:NTS, 16:20], ps[0:NTS, 2, 36:40], ACT.Copy, scale=KS)
            S.activation(emcol[0:NTS, :], ps[0:NTS, 2, 56:60], ACT.Copy)
            for j in range(8):
                act.wait_ge(bc_ps, j + 1)
                b0 = 4 + 2 * (j % 2)
                src = ps[:, b0:b0 + 2, 0:HB]
                dst = (ncm if j < 4 else em)[:, j % 4].rearrange("p (a b) -> p a b", b=HB)
                S.activation(dst, src, ACT.Copy if j < 4 else ACT.Exp, scale=-1.0).then_inc(bc_copied, 1)
            act.wait_ge(bc_ps, 9)
            S.activation(wint.rearrange("p a b -> p (a b)"), ps[:, 3, 0:MH * NTS], ACT.Copy).then_inc(gates_done, 1)
            act.wait_ge(gates_done, 2)

            with act.Fori(0, MH) as h:
                for t in range(8):
                    c = hchunk(h, t // 2)
                    if t == 0:
                        act.wait_ge(xp_ready, h + 1)
                    if t % 2:
                        act.wait_ge(done[c.slot], c.done_at)
                    else:
                        act.wait_ge(pr_even, h * 4 + (t // 2 + 1))
                    b0 = 2 * (t % 2)
                    if t < 4:
                        S.activation(xp[:, t, 3:3 + HB], ps[:, b0, 0:HB], ACT.Copy)
                        S.activation(xp[:, t, 3 + HB:3 + SEQ], ps[:, b0 + 1, 0:SEQ - HB], ACT.Copy)
                        S.activation(xm_d[:, t, :], ps[:, b0 + 1, SEQ - HB:HB], ACT.Copy)
                        S.activation(xp[:, t, 3 + SEQ:XPW].rearrange("p (b c) -> p b c", c=7)[:, :, 3:7],
                                     ps[:, b0 + 1, SEQ - HB:HB].rearrange("p (b c) -> p b c", c=DS),
                                     ACT.Copy).then_inc(pr_copied, 1)
                    else:
                        if t == 4:
                            act.wait_ge(pr_copied, h * 8 + 4)
                            for z in range(4):
                                S.activation(acc[:, z, 0:XCW], xp[:, z, 0:XCW], ACT.Identity,
                                             scale=convw[:, h * 4 + z, 0:1],
                                             bias=convw[:, h * 4 + z, 4:5]).then_inc(conv_init, 1)
                        S.activation(zs[:, t - 4].rearrange("p (a b) -> p a b", b=HB), ps[:, b0:b0 + 2, 0:HB],
                                     ACT.Sigmoid).then_inc(pr_copied, 1)
                for z in range(4):
                    act.wait_ge(conv_done, h * 4 + (z + 1))
                    S.activation(xc[:, z, 0:SEQ], acc[:, z, 0:SEQ], ACT.Silu)
                    S.activation(xc[:, z, SEQ:T].rearrange("p (b c) -> p b c", c=DS),
                                 acc[:, z, 3 + SEQ:XPW].rearrange("p (b c) -> p b c", c=7)[:, :, 0:DS],
                                 ACT.Silu).then_inc(xc_ready, 1)
                for t in range(8):
                    act.wait_ge(qk_ps, h * 8 + (t + 1))
                    b0 = 4 + 2 * (t % 2)
                    dst = (qT if t < 4 else kT)[:, t % 4]
                    S.activation(dst.rearrange("p (a b) -> p a b", b=HB), ps[:, b0:b0 + 2, 0:HB], ACT.Copy,
                                 scale=1.0 if t < 4 else KS).then_inc(qk_copied, 1)
                for i in range(5):
                    rows = P if i < 4 else NTS
                    act.wait_ge(vk_ps, h * 10 + (2 * i + 1))
                    S.activation(vr[0:rows, i, :], ps[0:rows, (2 * i) % 4, :], ACT.Copy).then_inc(vk_copied, 1)
                    act.wait_ge(vk_ps, h * 10 + (2 * i + 2))
                    S.activation(kw[0:rows, i, :], ps[0:rows, (2 * i + 1) % 4, :], ACT.Copy,
                                 scale=wcol[0:rows, i, bass.ds(h, 1)]).then_inc(vk_copied, 1)
                act.wait_ge(s_pre, h + 1)
                S.activation(ssp[:, :], ssp[:, :], ACT.Exp).then_inc(s_exp, 1)
                for i in range(4):
                    act.wait_ge(ex_ready, h * 4 + (i + 1))
                    last = S.activation(ex[:, i % 2, 0:P], ex[:, i % 2, 0:P], ACT.Exp)
                    if i < 3:
                        last = S.activation(ex[:, i % 2, P:SEQ - i * P], ncm[:, h, (i + 1) * P:SEQ], ACT.Exp,
                                            bias=acol[:, i, bass.ds(h, 1)])
                    last.then_inc(ex_done, 1)
                act.wait_ge(cf_ps, h + 1)
                S.activation(spt, ps[:, 0:4, :], ACT.Copy).then_inc(cf_copied, 1)
                act.wait_ge(vk_copied, h * 10 + 10)
                for b in range(NB):
                    if b >= 2:
                        act.wait_ge(up_ps, h * NB + (b - 1))
                    S.activation(vb[0:NTS, b % 2, :], vr[0:NTS, 4, :], ACT.Copy,
                                 scale=const("own_b", NTS)[:, b:b + 1]).then_inc(vb_ready, 1)
                act.wait_ge(h_ms, h + 1)
                S.activation(rms[:, :, :], ps[:, 5:7, 0:HB], ACT.Sqrt, bias=const("eps")).then_inc(h_root, 1)

        def mlstm_dve(dve, link):
            dve.wait_ge(ml_in, 16 * 6)
            mg = Chunk(plan["mgate"], 0, 0)
            dve.wait_ge(done[mg.slot], mg.done_at)
            H = slice(0, MH)

            def two(v):
                return v.rearrange("p (a b) -> p a b", b=HB)

            def dec(v):
                return v[H, SEQ:T].rearrange("p (b t) -> p b t", t=DS)

            link(V.tensor_scalar(two(ig[H]), ps[0:MH, 0:2, 0:HB], bg[H, 0:1], None, ALU.add))
            link(V.tensor_scalar(two(lf[H]), ps[32:32 + MH, 0:2, 0:HB], bg[32:32 + MH, 0:1], None, ALU.add))
            link(V.tensor_scalar(av[H], lf[H], -1.0, None, ALU.mult))
            V.tensor_tensor(av[H], av[H], lf[H], ALU.min).then_inc(gt_dve, 1)
            dve.wait_ge(gt_act, 2)
            link(V.scalar_tensor_tensor(lf[H], lf[H], 0.0, av[H], ALU.min, ALU.subtract))
            link(V.tensor_tensor_scan(cumf[H], const("restart", MH), lf[H], 0.0, ALU.mult, ALU.add))
            link(V.tensor_tensor(av[H], ig[H], cumf[H], ALU.subtract))
            link(V.tensor_copy(wsr[H], av[H]))
            link(V.tensor_tensor(dec(wsr)[:, :, 0], dec(wsr)[:, :, 0], m0r[H], ALU.max))
            link(V.tensor_tensor_scan(cm[H], const("restart_neg", MH), wsr[H], 0.0, ALU.add, ALU.max))
            link(V.tensor_tensor(mrow[H], cumf[H], cm[H], ALU.add))
            link(V.tensor_scalar(wsr[H, 0:SEQ], av[H, 0:SEQ], cm[H, SEQ - 1:SEQ], None, ALU.subtract))
            link(V.tensor_tensor(dec(wsr), dec(av), dec(cm)[:, :, 3:4].to_broadcast([MH, NB, DS]), ALU.subtract))
            V.tensor_tensor(dec(lf), m0r[H].unsqueeze(2).to_broadcast([MH, NB, DS]), dec(cm),
                            ALU.subtract).then_inc(gt_dve, 1)
            dve.wait_ge(gates_done, 2)
            with dve.Fori(0, MH) as h:
                link.enter(h, 35)
                link(V.memset(xp[:, :, 0:3], 0.0))
                V.tensor_copy(xp[:, :, 3 + SEQ:XPW].rearrange("p a (b c) -> p a b c", c=7)[:, :, :, 0:3],
                              sconv[:, bass.ds(h * 4, 4), :].rearrange("p a (b c) -> p a b c", c=3)).then_inc(xp_ready, 1)
                for z in range(4):
                    dve.wait_ge(conv_init, h * 4 + (z + 1))
                    for w in range(1, 4):
                        ins = V.scalar_tensor_tensor(acc[:, z, 0:XCW], xp[:, z, w:w + XCW], convw[:, h * 4 + z, w:w + 1],
                                                     acc[:, z, 0:XCW], ALU.mult, ALU.add)
                        if w < 3:
                            link(ins)
                        else:
                            ins.then_inc(conv_done, 1)
                V.tensor_copy(cvo[:, bass.ds(h * 4, 4), 0:3], xp[:, :, SEQ:SEQ + 3])
                link(V.tensor_copy(cvo[:, bass.ds(h * 4, 4), 3:27].rearrange("p a (b c) -> p a b c", c=3),
                                   xp[:, :, 3 + SEQ:XPW].rearrange("p a (b c) -> p a b c", c=7)[:, :, :, 4:7]))
                V.scalar_tensor_tensor(ssp[:, :], ncm[0:NTS, h, SEQ:T], acol[0:NTS, 4, bass.ds(h, 1)],
                                       const("causal_b", NTS), ALU.add, ALU.add).then_inc(s_pre, 1)
                dve.wait_ge(qk_copied, h * 8 + 8)
                link(V.tensor_tensor(qw[:, :, :], qT[:, :, SEQ:T], wint[:, h, :].unsqueeze(1).to_broadcast([P, 4, NTS]),
                                     ALU.mult))
                link(V.tensor_tensor(nprod[:, :, :].rearrange("p a (b t) -> p a b t", t=DS),
                                     qw[:, :, :].rearrange("p a (b t) -> p a b t", t=DS),
                                     nst[:, bass.ds(h * 4, 4), :].unsqueeze(3).to_broadcast([P, 4, NB, DS]), ALU.mult))
                for i in range(4):
                    link(V.scalar_tensor_tensor(ex[:, i % 2, 0:P], ncm[:, h, i * P:i * P + P], acol[:, i, bass.ds(h, 1)],
                                                const("causal_t"), ALU.add, ALU.add))
                    V.tensor_copy(den1[0:1, 0:1], acol[0:1, 0, 0:1]).then_inc(ex_ready, 1)
                    if i == 0:
                        dve.wait_ge(s_exp, h + 1)
                        dve.wait_ge(s_ps, h + 1)
                        V.tensor_tensor(ssp[:, :], ssp[:, :], ps[0:NTS, 4, 0:NTS], ALU.mult).then_inc(ssp_ready, 1)
                    dve.wait_ge(ex_done, h * 4 + (i + 1))
                    dve.wait_ge(sm_ps, h * 4 + (i + 1))
                    V.tensor_tensor(spt[:, i, 0:SEQ - i * P], ex[:, i % 2, 0:SEQ - i * P],
                                    ps[:, 5 + i % 2, 0:SEQ - i * P], ALU.mult).then_inc(sp_ready, 1)
                    dve.wait_ge(sp_ready, h * 4 + (i + 1))
                V.tensor_tensor(qwm, qw[:, :, :].unsqueeze(2).to_broadcast([P, 4, NB, NTS]),
                                const("own_cols").rearrange("p (b c) -> p b c", b=NB).unsqueeze(1).to_broadcast([P, 4, NB, NTS]),
                                ALU.mult).then_inc(qw_ready, 1)
                dve.wait_ge(h_ps, h + 1)
                link(V.tensor_tensor(rden[:, :], ps[:, 7, :], em[:, h, 0:SEQ], ALU.max))
                link(V.scalar_tensor_tensor(rden[:, :], ps[:, 7, :], -1.0, rden[:, :], ALU.mult, ALU.max))
                link(V.reciprocal(rden[:, :], rden[:, :]))
                V.tensor_tensor(work[:, :, 0:SEQ], ps[:, 0:4, :], rden[:, :].unsqueeze(1).to_broadcast([P, 4, SEQ]),
                                ALU.mult).then_inc(h_scaled, 1)
                dve.wait_ge(h_scaled, h + 1)
                link(V.tensor_tensor(zs[:, :, 0:SEQ], zs[:, :, 0:SEQ], work[:, :, 0:SEQ], ALU.mult))
                dve.wait_ge(nn_ps, h + 1)
                nn = ps[:, 4, 0:4 * C9].rearrange("p (a b) -> p a b", b=C9)
                V.tensor_copy(nnew[:, bass.ds(h * 4, 4), 0:1], nn[:, :, 0:1])
                wd = wint[:, h, :].rearrange("p (b t) -> p b t", t=DS)[:, :, 3]
                link(V.tensor_tensor(nnew[:, bass.ds(h * 4, 4), 1:C9], nst[:, bass.ds(h * 4, 4), :],
                                     wd.unsqueeze(1).to_broadcast([P, 4, NB]), ALU.mult))
                V.tensor_tensor(nnew[:, bass.ds(h * 4, 4), 1:C9], nnew[:, bass.ds(h * 4, 4), 1:C9], nn[:, :, 1:C9],
                                ALU.add).then_inc(nn_done, 1)
                for b in range(NB):
                    dve.wait_ge(up_ps, h * NB + (b + 1))
                    r = ring[:, hchunk(h, 4 + b).slot, :]
                    V.scalar_tensor_tensor(r, r, wint[:, h, DS * b + 3:DS * b + 4],
                                           ps[:, 0:4, :].rearrange("p a b -> p (a b)"), ALU.mult, ALU.add).then_inc(c_new, 1)
                link(V.tensor_tensor(den1[:, :], ps[0:NTS, 6, 0:1], emcol[0:NTS, bass.ds(h, 1)], ALU.max))
                link(V.scalar_tensor_tensor(den1[:, :], ps[0:NTS, 6, 0:1], -1.0, den1[:, :], ALU.mult, ALU.max))
                link(V.reciprocal(den1[:, :], den1[:, :]))
                V.tensor_scalar(hrow, ps[0:NTS, 5, :], den1[:, 0:1], None, ALU.mult).then_inc(hd_scaled, 1)
                dve.wait_ge(hdt_ps, h + 1)
                link(V.tensor_tensor(zs[:, :, SEQ:T], zs[:, :, SEQ:T],
                                     ps[:, 7, 0:4 * NTS].rearrange("p (a b) -> p a b", b=NTS), ALU.mult))
                V.tensor_tensor(work, zs, zs, ALU.mult).then_inc(h_sq, 1)
                dve.wait_ge(h_root, h + 1)
                link(V.reciprocal(rms[:, :, :], rms[:, :, :]))
                rt = rms[:, :, :].rearrange("p a b -> p (a b)")
                for e in range(4):
                    last = V.scalar_tensor_tensor(zs[:, e], zs[:, e], skipgn[:, h * 4 + e, 1:2], rt, ALU.mult, ALU.mult)
                link(last)
                for e in range(4):
                    last = V.scalar_tensor_tensor(zs[:, e], xc[:, e], skipgn[:, h * 4 + e, 0:1], zs[:, e], ALU.mult, ALU.add)
                last.then_inc(hn_ready, 1)
                dve.wait_ge(cf_stored, h * 16 + 16)
                for m in range(KT):
                    c = hchunk(h, 12 + m // 2)
                    if m % 2:
                        dve.wait_ge(done[c.slot], c.done_at)
                    else:
                        dve.wait_ge(y_even, h * 4 + (m // 2 + 1))
                    residual(4, m, 2 * (m % 2), tmp_d[:, m % 2], link)
            link.leave(MH)
        def load_chunks(sp, name, src, w, first=False):
            for ch in chunks(sp, plan[name], first):
                if not (first and isinstance(ch.free_at, int)):
                    sp.wait_ge(done[ch.slot], ch.free_at)
                sp.dma_start(ring[:, ch.slot, 0:w], src(ch.index)).then_inc(full[ch.slot], 16)

        block = ctx.enter_context(nc.Block())

        @block.sync
        def _(sp):
            sp.dma_start(cT[:, :, :], io["cT"]).then_inc(consts_in, 16)
            sp.dma_start(cst[:, :], io["const"]).then_inc(consts_in, 16)
            sp.dma_start(adab[:, :], io["adab"]).then_inc(consts_in, 16)
            sp.dma_start(norm_g[:, :, :], io["norm_g"]).then_inc(consts_in, 16)
            sp.dma_start(pages[:, :], io["pages"]).then_inc(consts_in, 16)
            load_chunks(sp, "ada", lambda i: io["ada"][i], SLOT, first=True)
            for f in range(4):
                load_chunks(sp, f"in{f}", lambda i, f=f: io["ffn_in"][i + f * FT], SLOT)
                load_chunks(sp, f"out{f}", lambda i, f=f: io["ffn_out"][i + f * 2 * KT], FT // 2 * P)
                if f == 0:
                    nsa_sp(sp)
                if f == 2:
                    mlstm_sp(sp)

        @block.gpsimd
        def _(gp):
            gp.dma_start(x[:, :, :], io["x"]).then_inc(x_in, 16)
            nsa_pool(gp)
            mlstm_pool(gp)
            ARENA_STORED[0] = NSTORE[0]
            gp.wait_ge(u_decode, 2 + KT)
            gp.dma_start(io["y"], u[:, :, :]).then_inc(stored, 16)
            NSTORE[0] += 16
            gp.wait_ge(stored, NSTORE[0])

        @block.scalar
        def _(act):
            link = Chain(act, chain_s)
            act.wait_ge(consts_in, 16 * 5)
            norm_act(act, 0)
            ada_act(act)
            modulate_act(act, 0, 0)
            ffn_act(act, 0, 0)
            norm_act(act, 1)
            modulate_act(act, 1)
            nsa_act(act, link)
            norm_act(act, 2)
            modulate_act(act, 2, 1)
            ffn_act(act, 1, 2)
            norm_act(act, 3)
            modulate_act(act, 3, 2)
            ffn_act(act, 2, 3)
            norm_act(act, 4)
            modulate_act(act, 4)
            mlstm_act(act, link)
            norm_act(act, 5)
            modulate_act(act, 5, 3)
            ffn_act(act, 3, 5)
            norm_act(act, 6)

        @block.vector
        def _(dve):
            link = Chain(dve, chain_v)
            dve.wait_ge(x_in, 16)
            V.memset(tmp_d[0:1, 0, 0:1], 0.0).then_inc(x_tile, 8)
            V.memset(tmp_d[0:1, 1, 0:1], 0.0).then_inc(mods_in, 1)
            V.memset(tmp256[0:1, 0:1], 0.0).then_inc(hidden, 2)
            V.memset(tmp256[0:1, 1:2], 0.0).then_inc(w_used, 2)
            dve.wait_ge(consts_in, 16 * 5)
            ada_dve(dve, link)
            split_norm_dve(dve, 0, 0, link)
            ffn_dve(dve, 0, 0, link)
            norm_dve(dve, 1, link)
            nsa_dve(dve, link)
            split_norm_dve(dve, 2, 1, link)
            ffn_dve(dve, 1, 2, link)
            split_norm_dve(dve, 3, 2, link)
            ffn_dve(dve, 2, 3, link)
            norm_dve(dve, 4, link)
            mlstm_dve(dve, link)
            dve.wait_ge(stored, ARENA_STORED[0])
            split_norm_dve(dve, 5, 3, link)
            ffn_dve(dve, 3, 5, link)
            norm_dve(dve, 6, link)

        @block.tensor
        def _(pe):
            norm_pe(pe, 0)
            ada_pe(pe)
            ffn_pe(pe, 0, 0)
            norm_pe(pe, 1)
            nsa_pe(pe)
            norm_pe(pe, 2)
            ffn_pe(pe, 1, 2)
            norm_pe(pe, 3)
            ffn_pe(pe, 2, 3)
            norm_pe(pe, 4)
            mlstm_pe(pe)
            norm_pe(pe, 5)
            ffn_pe(pe, 3, 5)
            norm_pe(pe, 6)


def q_order():
    heads = [((2 * gp + par) * REP + r) for gp in range(2) for r in range(REP) for par in range(2)]
    return np.concatenate([np.arange(h * HD, h * HD + HD) for h in heads])


def layout(inputs):
    f = {k: np.asarray(v) for k, v in inputs.items()}
    a = {"const": CONST}
    c = np.concatenate([f["c_prompt"], f["c_sample"]], 0)
    a["cT"] = c.T.reshape(KT, P, C9).transpose(1, 0, 2)
    xx = np.concatenate([f["x_prompt"].reshape(SEQ, D), f["x_sample"].reshape(NTS, D)], 0)
    a["x"] = xx.T.reshape(KT, P, T).transpose(1, 0, 2)
    a["adab"] = f["ada_b"].reshape(144, P).T
    a["norm_g"] = np.concatenate([f["norm_g"].reshape(6, D), f["final_norm_g"][None]], 0).reshape(7, KT, P).transpose(2, 0, 1)
    a["pages"] = f["page_table"].reshape(1, NB * NPAGE)
    a["ada"] = f["ada_w"].reshape(2, 4, 2, P, 9, D).transpose(0, 4, 1, 3, 2, 5).reshape(72, P, SLOT)
    a["ffn_in"] = f["ffn_w_in"].reshape(4, KT, P, 2, FT, P).transpose(0, 4, 2, 1, 3, 5).reshape(4 * FT, P, SLOT)
    a["ffn_out"] = f["ffn_w_out"].reshape(4, 2, FT // 2, P, KT, P)[:, ::-1].transpose(0, 4, 1, 3, 2, 5).reshape(4 * 2 * KT, P, FT // 2 * P)
    w = f["attn_w_in"][0]
    kv = w[:, 1024:1024 + 1536].reshape(D, 3, 2, 256)
    cols = [w[:, :1024][:, q_order()], kv[:, 0, 0], kv[:, 0, 1], kv[:, 1, 0], kv[:, 2, 0]]
    a["qkv"] = np.concatenate(cols, 1).reshape(KT, P, 8, 256).transpose(2, 1, 0, 3).reshape(8, P, SLOT)
    rows = np.concatenate([kv[:, 1, 1], kv[:, 2, 1], w[:, 2560:2608]], 1)
    a["row"] = rows.reshape(4, 2, P, VR).transpose(0, 2, 1, 3).reshape(4, P, 2 * VR)
    a["attn_out"] = f["attn_w_out"][0].reshape(KT, P, 4, 256).transpose(2, 1, 0, 3).reshape(4, P, SLOT)
    a["w1"] = f["cmp_w1"][0].reshape(2, 16, 2, HD, P).transpose(2, 3, 0, 1, 4).reshape(P, 2, 16, P)
    a["w2k"] = np.concatenate([f["cmp_w2"][0, 0]] * 2, 1)
    a["w2v"] = f["cmp_w2"][0, 1]
    a["cpos"] = f["cmp_pos"][0].reshape(16, 2, 2, HD).transpose(1, 3, 2, 0).reshape(P, 2, 16)
    a["rope"] = rope_tables()
    pg = f["cache_cmp"][0].reshape(NPOOL, 8, 8, 2, 2, KVH, HD)
    a["cmp_pages"] = pg.transpose(0, 3, 6, 4, 2, 5, 1).reshape(NPOOL, P, 512)
    pg = f["cache_sel"][0]
    k = pg[:, :, 0].reshape(NPOOL, P, 2, 2, HD).transpose(0, 3, 4, 2, 1).reshape(NPOOL, P, 256)
    a["sel_pages"] = np.concatenate([k, pg[:, :, 1].reshape(NPOOL, P, 256)], 2)
    wn = f["cache_win"][0]
    k = wn[:, :, 0].reshape(NB, SEQ, 2, 2, HD).transpose(0, 3, 4, 2, 1).reshape(NB, P, 1024)
    v = wn[:, :, 1].reshape(NB, 4, P, 256).transpose(0, 2, 1, 3).reshape(NB, P, 1024)
    a["win"] = np.stack([k, v])
    a["win_v"] = wn[:, :, 1].reshape(NB, SEQ, 256)

    w = f["ml_w_in"][0]
    g = np.zeros((D, 36), np.float32)
    g[:, 0:MH], g[:, 32:36] = w[:, 2 * MI:2 * MI + MH], w[:, 2 * MI + MH:]
    a["mgate"] = g.reshape(KT, P, 36).transpose(1, 0, 2).reshape(P, KT * 36)
    a["ml_in"] = w[:, :2 * MI].reshape(KT, P, 2, MH, 2, 256).transpose(3, 2, 4, 1, 0, 5).reshape(16, P, SLOT)
    a["ml_out"] = f["ml_w_out"][0].reshape(MH, 4, P, 4, 256).transpose(0, 3, 2, 1, 4).reshape(16, P, 1024)
    a["state_c"] = f["state_C"][0].reshape(NB, MH, 4, P, MHD).transpose(1, 0, 3, 2, 4).reshape(MH * NB, P, SLOT)
    a["nst"] = f["state_n"][0].reshape(NB, 16, P).transpose(2, 1, 0)
    a["sconv"] = f["state_conv"][0].reshape(NB, 3, 16, P).transpose(3, 2, 0, 1).reshape(P, 16, NB * 3)
    a["convw"] = np.concatenate([f["ml_conv_w"][0], f["ml_conv_b"]], 0).reshape(5, 16, P).transpose(2, 1, 0)
    a["skipgn"] = np.concatenate([f["ml_skip"], f["ml_gn_g"]], 0).reshape(2, 16, P).transpose(2, 1, 0)
    a["m0"] = f["state_m"][0].T
    b = np.zeros((36, 1), np.float32)
    b[0:MH, 0], b[32:36, 0] = f["ml_b_gate"][0, 0], f["ml_b_gate"][0, 1]
    a["bg"] = b
    bd = np.zeros((3, 16, 32, 4, 32, 4), np.float32)
    for j, name in enumerate(("ml_wq", "ml_wk", "ml_wv")):
        for k in range(32):
            bd[j, :, k, :, k, :] = f[name][0].reshape(16, 32, 4, 4)[:, k]
    a["bd"] = bd.reshape(3, MH, 4, P, P).transpose(1, 3, 0, 2, 4)
    return {k: np.ascontiguousarray(v) for k, v in a.items()}


OUTS = dict(y=(P, KT, T), kv_t=(P, 8, T), v_rows=(P, QT, 512), v_rows_d=(NTS, 512), win_k_out=(NB, P, 2, SEQ - DS),
            win_v_out=(NB, SEQ - DS, 256), c_out=(MH * NB, P, SLOT), cp_out=(MH, P, SLOT), n_out=(P, 16, C9),
            conv_out=(P, 16, C9 * 3), m_out=(MH, T))


def kernel(**inputs):
    import concourse.bacc as _bacc
    from concourse.bass_utils import run_bass_kernel_spmd as _run
    nc = _bacc.Bacc("TRN2", target_bir_lowering=False, num_devices=1)
    arrays = layout(inputs)
    io = {}
    for k, v in arrays.items():
        io[k] = nc.dram_tensor(f"in_{k}_dram", v.shape, mybir.dt.from_np(v.dtype), kind="ExternalInput").ap()
    for k, shape in OUTS.items():
        io[k] = nc.dram_tensor(f"out_{k}_dram", shape, F32, kind="ExternalOutput").ap()
    program(nc, io)
    r = _run(nc, [{f"in_{k}_dram": v for k, v in arrays.items()}], core_ids=[0])
    o = {k: r.results[0][f"out_{k}_dram"] for k in OUTS}
    y = o["y"].transpose(2, 1, 0).reshape(T, D)
    kt = o["kv_t"].reshape(2, HD, 4, 2, T)
    kt = kt.transpose(2, 4, 3, 0, 1).reshape(4, T, KVH, HD)
    v = np.concatenate([o["v_rows"].transpose(1, 0, 2).reshape(SEQ, 512), o["v_rows_d"]], 0).reshape(T, 2, KVH, HD)
    cmp_kv = np.stack([kt[0], kt[1]], 1)
    sel_kv = np.stack([kt[2], v[:, 0]], 1)
    win_kv = np.stack([kt[3], v[:, 1]], 1)

    def prompt(a):
        return a[:SEQ].reshape(1, 1, SEQ, 2, KVH, HD)

    def decode(a):
        return a[SEQ:].reshape(1, NB, DS, 2, KVH, HD)

    kold = o["win_k_out"].reshape(NB, 2, HD, 2, SEQ - DS).transpose(0, 4, 3, 1, 2).reshape(NB, SEQ - DS, KVH, HD)
    vold = o["win_v_out"].reshape(NB, SEQ - DS, KVH, HD)
    win_s = np.concatenate([np.stack([kold, vold], 2), decode(win_kv)[0]], 1)[None]
    c_p = o["cp_out"].reshape(MH, P, 4, MHD).transpose(0, 2, 1, 3).reshape(1, 1, MH, MHD, MHD)
    c_s = o["c_out"].reshape(MH, NB, P, 4, MHD).transpose(1, 0, 3, 2, 4).reshape(1, NB, MH, MHD, MHD)
    n = o["n_out"].transpose(2, 1, 0).reshape(C9, MH, MHD)
    cv = o["conv_out"].reshape(P, 16, C9, 3).transpose(2, 3, 1, 0).reshape(C9, 3, MI)
    m = o["m_out"]
    return (y[:SEQ].reshape(1, SEQ, D), y[SEQ:].reshape(NB, DS, D),
            prompt(cmp_kv), prompt(sel_kv), prompt(win_kv),
            c_p, n[0].reshape(1, 1, MH, MHD), m[:, SEQ - 1].reshape(1, 1, MH), cv[0].reshape(1, 1, 3, MI),
            decode(cmp_kv), decode(sel_kv), win_s,
            c_s, n[1:].reshape(1, NB, MH, MHD), m[:, SEQ + DS - 1::DS].T.reshape(1, NB, MH), cv[1:].reshape(1, NB, 3, MI))
```

```python
import concourse.bass as bass
from concourse import mybir
from concourse.alu_op_type import AluOpType as ALU
from contextlib import ExitStack
import numpy as np

F32 = mybir.dt.float32
F32R = mybir.dt.float32r
I32 = mybir.dt.int32
ACT = mybir.ActivationFunctionType
AX = mybir.AxisListType

P = 128
D = 1024
KT = D // P
SEQ = 512
QT = SEQ // P
NB = 8
DS = 4
NTS = NB * DS
T = SEQ + NTS
HB = T // 2
FF = 2816
FT = FF // P
EPS = 1e-6
NEG = -1e30
C9 = 1 + NB
RING = 4
SLOT = 2048
HEADS = 16
KVH = 4
REP = HEADS // KVH
HD = 64
SCALE = HD ** -0.5
NPAGE = 8
NPOOL = 80
NCP = SEQ // 16 - 1
NCS = NPAGE * 8 - 1
NSEL = 17
VR = 560
MH = 4
MI = 2048
MHD = MI // MH
ET = MHD // P
XPW = 3 + SEQ + NB * 7
XCW = XPW - 3


class Stream:

    def __init__(self):
        self.n = 0
        self.full = [0] * RING
        self.done = [0] * RING
        self.plan = {}

    def add(self, name, count, full=(16,), done=(1,)):
        self.plan[name] = (self.n, count, full, done, list(self.full), list(self.done))
        for i in range(count):
            self.full[(self.n + i) % RING] += full[i % len(full)]
            self.done[(self.n + i) % RING] += done[i % len(done)]
        self.n += count


class Chunk:

    def __init__(self, plan, k, it):
        n0, _, full, done, full0, done0 = plan
        s = (n0 + k) % RING
        f, d = full[k % len(full)], done[k % len(done)]
        self.slot = s
        self.k = k
        self.index = it * RING + k
        self.full_at = it * f + (full0[s] + f)
        self.free_at = it * d + done0[s]
        self.done_at = it * d + (done0[s] + d)


def chunks(eng, plan, first=False):
    rounds = plan[1] // RING
    start = 1 if first else 0
    if first:
        for k in range(RING):
            yield Chunk(plan, k, 0)
    with eng.Fori(start, rounds) as it:
        for k in range(RING):
            yield Chunk(plan, k, it)
    for k in range(plan[1] % RING):
        yield Chunk(plan, k, rounds)


class Chain:

    def __init__(self, eng, sem):
        self.eng, self.sem, self.base, self.k = eng, sem, 0, 0

    def __call__(self, ins):
        self.k += 1
        ins.then_inc(self.sem, 1)
        self.eng.wait_ge(self.sem, self.base + self.k)

    def enter(self, it, per):
        self.start, self.per = self.base + self.k, per
        self.base, self.k = it * per + self.start, 0

    def leave(self, rounds):
        assert self.k == self.per, (self.k, self.per)
        self.base, self.k = self.start + rounds * self.per, 0


def constants():
    cols, at = [], {}

    def put(name, a):
        a = np.asarray(a, np.float32)
        full = np.zeros((P, a.shape[1]), np.float32)
        full[:a.shape[0]] = a
        at[name] = (sum(c.shape[1] for c in cols), a.shape[1])
        cols.append(full)

    i = np.arange(P)
    put("ident", np.eye(P))
    put("ones", np.ones((P, P)))
    put("fold", np.tile(np.eye(NTS), (P // NTS, 1)))
    put("mean_d", np.full((P, P), 1.0 / D))
    put("mean_h", np.full((P, P), 1.0 / MHD))
    rot = np.zeros((P, P))
    for h in (0, HD):
        for j in range(8):
            rot[h + 8 + j, h + j] = -1.0
            rot[h + j, h + 8 + j] = 1.0
    put("rot", rot)
    put("causal", np.where(i[None, :] <= i[:, None], 0.0, NEG))
    put("causal_t", np.where(i[:, None] <= i[None, :], 0.0, NEG))
    g, r, t = i // 32, (i % 32) // DS, i % DS
    put("same_gt", (g[:, None] == g[None, :]) & (t[:, None] == t[None, :]) & (r[:, None] < REP))
    c, j = np.arange(NCS)[:, None], np.arange(NSEL)[None, :]
    put("overlap", np.maximum(np.minimum(c * 16 + 32, (j + 1) * 64) - np.maximum(c * 16, j * 64), 0) / 16)
    put("block_no", np.tile(np.arange(NSEL), (P, 1)))
    tail = np.where(np.arange(DS)[None, :] <= t[:, None], 0.0, NEG)
    put("tails", np.concatenate([tail, tail], 1))
    put("win_edge", np.where(np.arange(DS)[None, :] <= t[:, None], NEG, 0.0))
    q, kk = np.arange(SEQ).reshape(QT, P).T[:, :, None], np.arange(NCP)[None, None, :]
    put("cmp_valid", (kk * 16 + 31 <= q).reshape(P, QT * NCP))
    put("cmp_neg", np.where(kk * 16 + 31 <= q, 0.0, NEG).reshape(P, QT * NCP))
    bt = np.arange(NTS)
    put("pick_t", bt[:, None] % DS == np.where(r < REP, t, -1)[None, :])
    put("own_b", bt[:, None] // DS == np.arange(NB)[None, :])
    put("head_of", np.arange(HEADS)[None, :] == (g * REP + r)[:, None])
    put("own_cols", np.tile((np.arange(NB)[:, None] == bt[None, :] // DS).reshape(1, -1), (P, 1)))
    put("causal_b", np.where((bt[:, None] // DS == bt[None, :] // DS) & (bt[:, None] <= bt[None, :]), 0.0, NEG))
    put("head_row", np.repeat(np.eye(MH), P, 1))
    keep = np.ones(T)
    keep[0] = 0
    keep[SEQ::DS] = 0
    pen = np.zeros(T)
    pen[SEQ::DS] = NEG
    put("restart", np.tile(keep, (MH, 1)))
    put("restart_neg", np.tile(pen, (MH, 1)))
    put("eps", np.full((P, 1), EPS))
    return np.concatenate(cols, 1), at


CONST, CONST_AT = constants()


def rope_tables():
    pos = np.concatenate([np.arange(SEQ), np.tile(1024 + np.arange(DS), NB)]).astype(np.float32)
    inv = np.float32(500000.0) ** (-np.arange(0, 16, 2, dtype=np.float32) / np.float32(16))
    ang = pos[None, :] * inv.astype(np.float32)[:, None]
    cos, sin = np.ones((HD, T), np.float32), np.zeros((HD, T), np.float32)
    cos[:8], cos[8:16], sin[:8], sin[8:16] = np.cos(ang), np.cos(ang), np.sin(ang), np.sin(ang)
    return np.stack([np.tile(cos, (2, 1)), np.tile(sin, (2, 1))], 1)


def program(nc, io):
    V, S, G, PE = nc.vector, nc.scalar, nc.gpsimd, nc.tensor
    stream = Stream()
    stream.add("ada", 2 * 36)
    for f in range(2):
        stream.add(f"in{f}", FT)
        stream.add(f"out{f}", 2 * KT)
        if f == 0:
            stream.add("qkv", 8)
            stream.add("row", 4)
            stream.add("cmp", NB, full=(64,))
            stream.add("selwin", 4 * -(-NB // 3), full=(64, 64, 16, 16))
            stream.add("aout", 4)
    for f in range(2, 4):
        stream.add(f"in{f}", FT)
        stream.add(f"out{f}", 2 * KT)
        if f == 2:
            stream.add("mgate", 1)
            stream.add("mlstm", 16 * MH, done=(1,) * 4 + (0,) * 8 + (1,) * 4)
    plan = stream.plan
    cs = {k: v for k, v in CONST_AT.items()}

    ctx = ExitStack()
    with ctx:
        def sb(name, shape, dt=F32):
            return ctx.enter_context(nc.sbuf_tensor(name, shape, dt))

        def sem(name):
            return ctx.enter_context(nc.semaphore(name))

        ring = sb("ring", [P, RING, SLOT])
        x = sb("x", [P, KT, T])
        u = sb("u", [P, KT, T])
        mods = sb("mods", [P, 144, C9])
        adab = sb("adab", [P, 144])
        norm_g = sb("norm_g", [P, 7, KT])
        cT = sb("cT", [P, KT, C9])
        cst = sb("cst", [P, CONST.shape[1]])
        rms = sb("rms", [P, 2, HB])
        pages = sb("pages", [1, NB * NPAGE], I32)
        tmp_d = sb("tmp_d", [P, 2, NTS])
        tmp256 = sb("tmp256", [P, 256])
        ARENA = 29660
        with (nc.sbuf_tensor("w_parts", [P, 2, 2, 1024], F32R) as w_parts,
              nc.sbuf_tensor("h_hi", [P, FT, T], F32R) as h_hi,
              nc.sbuf_tensor("h_lo", [P, FT, T], F32R) as h_lo,
              nc.sbuf_tensor("sg", [P, 2, 2, HB], F32) as sg,
              nc.sbuf_tensor("modrow", [P, 256], F32) as modrow):
            pass
        arena = sb("arena", [P, ARENA])
        ps = ctx.enter_context(nc.psum_tensor("ps", [P, 8, 512], F32))

        def const(name, rows=P):
            a, w = cs[name]
            return cst[0:rows, a:a + w]

        top = [0]

        def carve(*dims, at=None):
            n = int(np.prod(dims))
            a = top[0] if at is None else at
            if at is None:
                top[0] = a + n
            assert a + n <= ARENA, (a + n, dims)
            v = arena[:, a:a + n]
            names = "abcd"[:len(dims)]
            if len(dims) > 1:
                v = v.rearrange(f"p ({' '.join(names)}) -> p {' '.join(names)}", **dict(zip(names, dims)))
            return v

        u_hi, u_lo = h_hi[:, 0:KT], h_lo[:, 0:KT]
        full = [sem(f"slot_full{i}") for i in range(RING)]
        done = [sem(f"slot_done{i}") for i in range(RING)]
        consts_in = sem("consts_in")
        x_in = sem("x_in")
        pages_in = sem("pages_in")
        stored = sem("stored")
        c_silu = sem("c_silu")
        ada_rows = sem("ada_rows")
        ada_copied = sem("ada_copied")
        ada_cols = sem("ada_cols")
        mods_in = sem("mods_in")
        mods_done = sem("mods_done")
        x_tile = sem("x_tile")
        squares = sem("squares")
        rms_root = sem("rms_root")
        mean_sq = sem("mean_sq")
        scaled = sem("scaled")
        u_prompt = sem("u_prompt")
        u_decode = sem("u_decode")
        gate_up = sem("gate_up")
        silus = sem("silus")
        hidden = sem("hidden")
        w_rounded = sem("w_rounded")
        w_lo = sem("w_lo")
        w_used = sem("w_used")
        u_dec = sem("u_dec")
        u_rounded = sem("u_rounded")
        u_split = sem("u_split")
        h_rounded = sem("h_rounded")
        h_split = sem("h_split")
        chain_v = sem("chain_v")
        chain_s = sem("chain_s")
        NSTORE = [0]
        ARENA_STORED = [0]

        def ada_pe(pe):
            pe.wait_ge(c_silu, 1)
            pe.wait_ge(scaled, 1)
            with pe.Fori(0, 18) as it:
                for k in range(4):
                    ch = Chunk(plan["ada"], k, it)
                    pe.wait_ge(full[ch.slot], ch.full_at)
                    w = ring[:, ch.slot, :].rearrange("p (k c) -> p k c", c=D)
                    for j in range(2):
                        kt = 2 * k + j
                        for q in range(4):
                            last = PE.matmul(ps[32 * q:32 * q + C9, 0, 0:256], cT[:, kt, :],
                                             w[:, j, 256 * q:256 * q + 256], start=kt == 0, stop=kt == KT - 1,
                                             skip_group_check=True)
                    last.then_inc(done[ch.slot], 1)
                pe.wait_ge(ada_copied, it + 1)
                pe.wait_ge(mods_in, it + 1)
                for t in range(KT):
                    q = 32 * (t // 2)
                    last = PE.matmul(ps[:, 4 + t // 2, C9 * (t % 2):C9 * (t % 2) + C9], modrow[q:q + C9, P * (t % 2):P * (t % 2) + P],
                                     const("ident")[q:q + C9, q:q + C9], start=True, stop=True)
                last.then_inc(ada_cols, 1)

        def ada_act(act):
            S.activation(cT[:, :, :], cT[:, :, :], ACT.Silu).then_inc(c_silu, 1)
            with act.Fori(0, 18) as it:
                ch = Chunk(plan["ada"], 3, it)
                act.wait_ge(done[ch.slot], ch.done_at)
                for q in range(4):
                    last = S.activation(modrow[32 * q:32 * q + C9, :], ps[32 * q:32 * q + C9, 0, 0:256], ACT.Copy)
                last.then_inc(ada_copied, 1)

        def ada_dve(dve, link):
            with dve.Fori(0, 18) as it:
                dve.wait_ge(ada_cols, it + 1)
                V.tensor_tensor(mods[:, bass.ds(it * KT, KT), :].rearrange("p (q a) b -> p q a b", q=4),
                                ps[:, 4:8, 0:2 * C9].rearrange("p q (a b) -> p q a b", b=C9),
                                adab[:, bass.ds(it * KT, KT)].rearrange("p (q a) -> p q a", q=4).unsqueeze(3)
                                .to_broadcast([P, 4, 2, C9]), ALU.add).then_inc(mods_in, 1)
            dve.wait_ge(mods_in, 19)
            for ls in range(6):
                scale = mods[:, ls * 24 + 8:ls * 24 + 16, :]
                gate = mods[:, ls * 24 + 16:ls * 24 + 24, :]
                link(V.tensor_scalar(scale, scale, 1.0, None, ALU.add))
                V.tensor_tensor(scale, scale, norm_g[:, ls, :].unsqueeze(2).to_broadcast([P, KT, C9]),
                                ALU.mult).then_inc(mods_done, 1)
                half = 1.0 if ls % 3 == 1 else 0.5
                V.tensor_scalar(gate, gate, 1.0, half, ALU.add, ALU.mult).then_inc(mods_done, 1)
            dve.wait_ge(mods_done, 12)

        def x_base(n):
            return 8 * (n if n < 5 else n - 1 + MH)

        def norm_act(act, n, f=None):
            for j in range(KT):
                act.wait_ge(x_tile, x_base(n) + (8 if n == 2 else j + 1))
                S.activation(u[:, j, :], x[:, j, :], ACT.Square).then_inc(squares, 1)
            if f == 3:
                act.wait_ge(stored, ARENA_STORED[0])
            if f:
                for _ in round_weights(act, plan[f"in{f}"], 0, 0, CHUNKS * f, IN_ROWS):
                    pass
            act.wait_ge(mean_sq, n + 1)
            S.activation(rms[:, :, :], ps[:, 4:6, 0:HB], ACT.Sqrt, bias=const("eps")).then_inc(rms_root, 1)

        def modulate_act(act, n, f=None):
            act.wait_ge(mods_done, 12)
            for kt in range(KT + 1):
                if kt < KT:
                    act.wait_ge(scaled, (KT + 1) * n + kt + 2)
                    S.activation(u[:, kt, 0:SEQ], u[:, kt, 0:SEQ], ACT.Identity,
                                 bias=mods[:, n * 24 + kt, 0:1],
                                 scale=mods[:, n * 24 + 8 + kt, 0:1]).then_inc(u_prompt, 1)
                if kt >= 1 and f is not None:
                    act.wait_ge(u_prompt, KT * n + kt)
                    act.wait_ge(u_dec, KT * f + kt)
                    S.activation(u_hi[:, kt - 1, :], u[:, kt - 1, :], ACT.Copy).then_inc(u_rounded, 1)

        def norm_pe(pe, n):
            if n == 0:
                pe.wait_ge(consts_in, 16 * 5)
            for kt in range(KT):
                pe.wait_ge(squares, KT * n + kt + 1)
                for hf in range(2):
                    last = PE.matmul(ps[:, 4 + hf, 0:HB], const("mean_d"), u[:, kt, hf * HB:hf * HB + HB],
                                     start=kt == 0, stop=kt == KT - 1, skip_group_check=True)
            last.then_inc(mean_sq, 1)

        def inverse_rms(dve, n):
            dve.wait_ge(rms_root, n + 1)
            V.reciprocal(rms[:, :, :], rms[:, :, :]).then_inc(scaled, 1)
            dve.wait_ge(scaled, (KT + 1) * n + 1)

        def norm_dve(dve, n, link):
            inverse_rms(dve, n)
            r = rms[:, :, :].rearrange("p a b -> p (a b)")
            for kt in range(KT):
                if n == 6:
                    V.scalar_tensor_tensor(u[:, kt, :], x[:, kt, :], norm_g[:, 6, kt:kt + 1], r, ALU.mult,
                                           ALU.mult).then_inc(u_decode, 1)
                else:
                    V.tensor_tensor(u[:, kt, :], x[:, kt, :], r, ALU.mult).then_inc(scaled, 1)
            if n == 6:
                return
            dve.wait_ge(scaled, (KT + 1) * (n + 1))
            ud = u[:, :, SEQ:T].rearrange("p k (b t) -> p k b t", t=DS)
            for kt in range(KT):
                sc = mods[:, n * 24 + 8 + kt, 1:C9].unsqueeze(2).to_broadcast([P, NB, DS])
                last = V.tensor_tensor(ud[:, kt], ud[:, kt], sc, ALU.mult)
            link(last)
            for kt in range(KT):
                sh = mods[:, n * 24 + kt, 1:C9].unsqueeze(2).to_broadcast([P, NB, DS])
                last = V.tensor_tensor(ud[:, kt], ud[:, kt], sh, ALU.add)
            last.then_inc(u_decode, 1)

        def split_norm_dve(dve, n, f, link):
            if f:
                rest_of_weights(dve, plan[f"in{f}"], 0, 0, CHUNKS * f, IN_ROWS)
            if n:
                inverse_rms(dve, n)
            r = rms[:, :, :].rearrange("p a b -> p (a b)")
            for kt in range(KT + 2):
                if f == 0 and kt == KT:
                    rest_of_weights(dve, plan["in0"], 0, 0, 0, IN_ROWS)
                if kt < KT:
                    V.tensor_tensor(u[:, kt, :], x[:, kt, :], r, ALU.mult).then_inc(scaled, 1)
                    dve.wait_ge(scaled, (KT + 1) * n + kt + 2)
                    ud = u[:, kt, SEQ:T].rearrange("p (b t) -> p b t", t=DS)
                    sc = mods[:, n * 24 + 8 + kt, 1:C9].unsqueeze(2).to_broadcast([P, NB, DS])
                    sh = mods[:, n * 24 + kt, 1:C9].unsqueeze(2).to_broadcast([P, NB, DS])
                    link(V.tensor_tensor(ud, ud, sc, ALU.mult))
                    V.tensor_tensor(ud, ud, sh, ALU.add).then_inc(u_dec, 1)
                if kt >= 2:
                    dve.wait_ge(u_rounded, KT * f + kt - 1)
                    V.tensor_tensor(u_lo[:, kt - 2, :], u[:, kt - 2, :], u_hi[:, kt - 2, :].bitcast(F32),
                                    ALU.subtract).then_inc(u_split, 1)

        def u_ready(pe, n):
            pe.wait_ge(u_prompt, KT * (n + 1))
            pe.wait_ge(u_decode, 1 if n == 1 else 2)

        def residual(n, m, pair, tmp, link):
            g = mods[:, n * 24 + 16 + m, :]
            rest = SEQ - HB
            V.scalar_tensor_tensor(x[:, m, 0:HB], ps[:, pair, 0:HB], g[:, 0:1], x[:, m, 0:HB], ALU.mult, ALU.add)
            V.scalar_tensor_tensor(x[:, m, HB:SEQ], ps[:, pair + 1, 0:rest], g[:, 0:1], x[:, m, HB:SEQ],
                                   ALU.mult, ALU.add)
            y = ps[:, pair + 1, rest:HB].rearrange("p (b t) -> p b t", t=DS)
            link(V.tensor_tensor(tmp.rearrange("p (b t) -> p b t", t=DS), y,
                                 g[:, 1:C9].unsqueeze(2).to_broadcast([P, NB, DS]), ALU.mult))
            V.tensor_tensor(x[:, m, SEQ:T], x[:, m, SEQ:T], tmp, ALU.add).then_inc(x_tile, 1)

        top[0] = 0
        K2 = FT // 2
        CHUNKS = FT + 2 * KT

        def half_in(g):
            return lambda v: v.rearrange("p (k c) -> p k c", c=256)[:, :, g * P:g * P + P]

        def half_out(g):
            return lambda v: v[:, 0:K2 * P].rearrange("p (k c) -> p k c", c=P)[:, 6 * g:6 + 5 * g]

        def parts(g, n):
            return [w_parts[:, g, part, 0:n * P].rearrange("p (k c) -> p k c", c=P) for part in range(2)]

        def split_products(dst, w, x_hi, x_lo, first, last):
            for a, xs, at in ((w[0], x_hi, 0), (w[0], x_lo, 1), (w[1], x_hi, 2)):
                for hf in range(2):
                    ins = PE.matmul(dst[hf], a, xs[:, hf * HB:hf * HB + HB], start=first and at == 0,
                                    stop=last and at == 2)
            return ins

        def round_weights(act, pl, k, it, base, rows):
            ch = Chunk(pl, k, it)
            act.wait_ge(full[ch.slot], ch.full_at)
            for g in range(2):
                act.wait_ge(w_used, ch.index * 2 + (2 * base + g + 1))
                S.activation(parts(g, rows[g])[0], (half_in if rows[0] == KT else half_out)(g)(ring[:, ch.slot, :]),
                             ACT.Copy).then_inc(w_rounded, 1)
                yield

        def rest_of_weights(dve, pl, k, it, base, rows):
            ch = Chunk(pl, k, it)
            for g in range(2):
                dve.wait_ge(w_rounded, ch.index * 2 + (2 * base + g + 1))
                hi, lo = parts(g, rows[g])
                src = (half_in if rows[0] == KT else half_out)(g)(ring[:, ch.slot, :])
                V.tensor_tensor(lo, src, hi.bitcast(F32), ALU.subtract).then_inc(done[ch.slot] if g else w_lo, 1)

        IN_ROWS, OUT_ROWS = (KT, KT), (6, 5)

        def ffn_pe(pe, f, n):
            c0 = CHUNKS * f

            def weights(ch, base, g):
                if g == 0:
                    pe.wait_ge(w_lo, ch.index + (base + 1))
                else:
                    pe.wait_ge(done[ch.slot], ch.done_at)

            for ch in chunks(pe, plan[f"in{f}"]):
                for g in range(2):
                    weights(ch, c0, g)
                    if g == 0:
                        pe.wait_ge(hidden, ch.index + (FT * f + 1))
                    w = parts(g, KT)
                    b = 4 * (ch.k % 2) + 2 * g
                    dst = [ps[:, b + hf, 0:HB] for hf in range(2)]
                    for kt in range(KT):
                        if g == 0:
                            pe.wait_ge(u_split, KT * f + kt + 1)
                        last = split_products(dst, (w[0][:, kt], w[1][:, kt]), u_hi[:, kt], u_lo[:, kt],
                                              kt == 0, kt == KT - 1)
                    last.then_inc(w_used, 1)
            pe.wait_ge(hidden, FT * (f + 1) + 2)
            for ch in chunks(pe, plan[f"out{f}"]):
                m2, half = ch.k // 2, ch.k % 2
                if half == 0:
                    pe.wait_ge(x_tile, (ch.index - ch.k) // 2 + (x_base(n) + 7 + m2))
                dst = [ps[:, 2 * m2 + hf, 0:HB] for hf in range(2)]
                for g in range(2):
                    weights(ch, c0 + FT, g)
                    if half == 0:
                        pe.wait_ge(h_split, FT * f + (FT - KT if g else K2 + 6 - KT))
                    elif g == 0:
                        pe.wait_ge(h_split, FT * f + FT)
                    w = parts(g, OUT_ROWS[g])
                    for k in range(OUT_ROWS[g]):
                        t = (0 if half else K2) + 6 * g + k
                        last = split_products(dst, (w[0][:, k], w[1][:, k]), h_hi[:, t], h_lo[:, t],
                                              half == 0 and g == 0 and k == 0,
                                              half == 1 and g == 1 and k == OUT_ROWS[1] - 1)
                    last.then_inc(w_used, 1)

        def ffn_act(act, f, n):
            p_in, p_out, c0 = plan[f"in{f}"], plan[f"out{f}"], CHUNKS * f
            rounds_in, rounds_out = FT // RING, 2 * KT // RING

            def all_of(steps):
                for _ in steps:
                    pass

            def silu(k, it):
                act.wait_ge(w_used, (it * RING + k) * 2 + (2 * c0 + 4))
                b = 4 * (k % 2)
                S.activation(sg[:, k % 2], ps[:, b:b + 2, 0:HB], ACT.Silu).then_inc(silus, 1)

            if f == 0:
                all_of(round_weights(act, p_in, 0, 0, c0, IN_ROWS))
            with act.Fori(0, rounds_in) as it:
                for k in range(RING):
                    nk, ni = (k + 1, it) if k + 1 < RING else (0, it + 1)
                    all_of(round_weights(act, p_in, nk, ni, c0, IN_ROWS))
                    silu(k, it)
            all_of(round_weights(act, p_in, 1, rounds_in, c0, IN_ROWS))
            silu(0, rounds_in)
            steps = round_weights(act, p_out, 0, 0, c0 + FT, OUT_ROWS)
            next(steps)
            silu(1, rounds_in)
            all_of(steps)
            for j in range(0, KT, 4):
                S.activation(h_hi[:, j:j + 4, :], u[:, j:j + 4, :], ACT.Copy).then_inc(h_rounded, 1)

            def out_round(it, last):
                for k in range(1, RING if last else RING + 1):
                    all_of(round_weights(act, p_out, k % RING, it + 1 if k == RING else it, c0 + FT, OUT_ROWS))

            with act.Fori(0, rounds_out - 1) as it:
                out_round(it, False)
            out_round(rounds_out - 1, True)

        def ffn_dve(dve, f, n, link):
            p_in, p_out, c0 = plan[f"in{f}"], plan[f"out{f}"], CHUNKS * f
            rounds_in, rounds_out = FT // RING, 2 * KT // RING

            def hide(k, it, defer):
                t = it * RING + k
                dve.wait_ge(silus, t + (FT * f + 1))
                b = 4 * (k % 2)
                if defer:
                    V.tensor_tensor(u[:, t, :].rearrange("p (a b) -> p a b", b=HB), sg[:, k % 2], ps[:, b + 2:b + 4, 0:HB],
                                    ALU.mult).then_inc(hidden, 1)
                    return
                V.tensor_tensor(sg[:, k % 2], sg[:, k % 2], ps[:, b + 2:b + 4, 0:HB], ALU.mult).then_inc(hidden, 1)
                dve.wait_ge(hidden, t + (FT * f + 3))
                whole = sg[:, k % 2].rearrange("p a b -> p (a b)")
                link(V.tensor_copy(h_hi[:, t, :], whole))
                V.tensor_tensor(h_lo[:, t, :], whole, h_hi[:, t, :].bitcast(F32), ALU.subtract).then_inc(h_split, 1)

            def in_rounds(a, b, defer):
                with dve.Fori(a, b) as it:
                    if not defer:
                        link.enter(it - a, RING)
                    for k in range(RING):
                        nk, ni = (k + 1, it) if k + 1 < RING else (0, it + 1)
                        rest_of_weights(dve, p_in, nk, ni, c0, IN_ROWS)
                        hide(k, it, defer)
                if not defer:
                    link.leave(b - a)

            in_rounds(0, KT // RING, True)
            in_rounds(KT // RING, rounds_in, False)
            rest_of_weights(dve, p_in, 1, rounds_in, c0, IN_ROWS)
            hide(0, rounds_in, False)
            rest_of_weights(dve, p_out, 0, 0, c0 + FT, OUT_ROWS)
            hide(1, rounds_in, False)
            for j in range(0, KT, 4):
                dve.wait_ge(h_rounded, 2 * f + j // 4 + 1)
                V.tensor_tensor(h_lo[:, j:j + 4, :], u[:, j:j + 4, :], h_hi[:, j:j + 4, :].bitcast(F32),
                                ALU.subtract).then_inc(h_split, 4)

            def out_round(it, last):
                for m2 in range(2):
                    k = 2 * m2 + 1
                    rest_of_weights(dve, p_out, k, it, c0 + FT, OUT_ROWS)
                    if m2 == 0:
                        rest_of_weights(dve, p_out, 2, it, c0 + FT, OUT_ROWS)
                    elif not last:
                        rest_of_weights(dve, p_out, 0, it + 1, c0 + FT, OUT_ROWS)
                    dve.wait_ge(w_used, it * 2 * RING + (2 * (c0 + FT + k) + 4))
                    residual(n, it * 2 + m2, 2 * m2, tmp_d[:, m2], link)

            with dve.Fori(0, rounds_out - 1) as it:
                link.enter(it, 2)
                out_round(it, False)
            link.leave(rounds_out - 1)
            out_round(rounds_out - 1, True)

        top[0] = 0
        qk = carve(16, T)
        vrow = carve(5, VR)
        sel_b = carve(2, SLOT)
        kc_d = carve(NB, 256)
        vc_d = carve(NB, 256)
        w1 = carve(2, 16, P)
        w2k = carve(P)
        w2v = carve(HD)
        cpos = carve(2, 16)
        rope_cs = carve(2, T)
        kc_p = carve(4 * NCP)
        vc_p = carve(256)
        cc = carve(2)
        mx = carve(2, 2)
        den = carve(2, 2)
        cf = carve(2, 2)
        YB = top[0]
        pairs = carve(2, 4, SEQ)
        raw = carve(2, T, at=YB)
        t1 = carve(T, at=YB + 2 * T)
        t2 = carve(T, at=YB + 3 * T)
        hid_p = carve(2, 4, NCP, at=8704 + 5 * VR + 4096 + 4096 + 4096 + P + HD + 32)
        f1 = carve(2, 2, 256, at=YB)
        hid = carve(2, 2, 256, at=YB + 1024)
        W1A = 8704 + 5 * VR + 4096 + 4096
        vtail = carve(NB, 512, at=W1A)
        qs = carve(NB, 2, 32, at=YB + 2048)
        sc = carve(NB, NCS, at=YB)
        pt_c = carve(NB, P, at=YB + 512)
        gm = carve(NB, 48, at=YB + 1536)
        prob = carve(2, 2, SEQ, at=YB)
        pt = carve(2, 2, 512, at=YB + 2048)
        RC = W1A + 4096 + P + HD + 32
        ocs = carve(NB, HD, at=RC)
        gs = carve(NB, 3, at=RC + 512)
        negm = carve(NB, 14, at=RC + 536)
        m8 = carve(NB, at=RC + 648)
        s8 = carve(NB, at=RC + 656)
        di8 = carve(NB, at=RC + 664)
        imp1 = carve(NB, NSEL, at=RC + 672)
        eqj = carve(NB, 14, at=RC + 808)
        m2s = carve(2, at=RC + 920)
        t2s = carve(2, at=RC + 922)
        nm2 = carve(2, at=RC + 924)
        d4 = carve(4, at=RC + 926)
        d2 = carve(2, at=RC + 930)
        c2 = carve(2, at=RC + 932)
        tmpo = carve(HD, at=RC + 1016)
        qkeep = sb("qkeep", [P, NB, 2, 32])
        osum = carve(NB, 2, HD, at=8 * T)
        win_b = carve(2, 1024, at=0)
        win_c = carve(2, 1024, at=4 * T)
        sel_c = carve(2, SLOT, at=8704 + 5 * VR + 4096)
        gtmp = carve(24, HEADS, at=8704 + 5 * VR + 4096)
        ps_d = carve(1544, at=YB)
        pts_d = carve(12 * P, at=YB + 1544)
        ptt_d = carve(256, at=YB + 1544 + 1536)

        nsa_in = sem("nsa_in")
        proj_even, raw_copied, rope_ps, roped = sem("proj_even"), sem("raw_copied"), sem("rope_ps"), sem("roped")
        row_ready, row_copied = sem("row_ready"), sem("row_copied")
        pairs_in, vtail_in = sem("pairs_in"), sem("vtail_in")
        cc_ready, cc_copied, conv_p, hid_p_ready, kc_p_ps, kc_p_copied = (sem(n) for n in (
            "cc_ready", "cc_copied", "conv_p", "hid_p_ready", "kc_p_ps", "kc_p_copied"))
        cmp_odd_in, cmp_odd_used = sem("cmp_odd_in"), sem("cmp_odd_used")
        conv_d, f1_ready, h1_done, hid_ready, kc_ps, kc_copied = (sem(n) for n in (
            "conv_d", "f1_ready", "h1_done", "hid_ready", "kc_ps", "kc_copied"))
        q_staged, cs_ps, cs_shift, cs_exp, cs_prob, cs_tr, cs_trc, imp_ps, imp_copied, grp_ps, gm_ready, gsel_ps, sel_done = (
            sem(n) for n in ("q_staged", "cs_ps", "cs_shift", "cs_exp", "cs_prob", "cs_tr", "cs_trc", "imp_ps",
                             "imp_copied", "grp_ps", "gm_ready", "gsel_ps", "sel_done"))
        sc_ps, sc_max, sc_exp, sc_scaled, tr_ps, tr_copied, o_ps, o_used = (sem(n) for n in (
            "sc_ps", "sc_max", "sc_exp", "sc_scaled", "tr_ps", "tr_copied", "o_ps", "o_used"))
        d_scores, d_max, d_exp, d_tr, d_trc, d_ops, d_out, sel_b_in, win_b_in, sel_c_in, win_c_in = (sem(n) for n in (
            "d_scores", "d_max", "d_exp", "d_tr", "d_trc", "d_ops", "d_out", "sel_b_in", "win_b_in", "sel_c_in",
            "win_c_in"))
        ot_ps, ot_copied, aout_even = (sem(n) for n in (
            "ot_ps", "ot_copied", "aout_even"))

        ROPED = [t for t in range(16) if t not in (10, 11)]
        UNITS = [(g, j, qt, br) for g in range(KVH) for j in range(2) for qt in range(QT) for br in (1, 0, 2)]
        NU = len(UNITS)

        def keys(i):
            return NCP if UNITS[i][3] == 0 else (UNITS[i][2] + 1) * P

        def groups(i):
            return (keys(i) + 255) // 256

        GROUPS = [0]
        for i in range(NU):
            GROUPS.append(GROUPS[-1] + groups(i))

        DECODE_PLACES = {1: (sel_b, win_b, sel_b_in, win_b_in), 2: (sel_c, win_c, sel_c_in, win_c_in)}

        def page_loads(sp, dst, sem_, first_page, src):
            for j in range(4):
                page = sp.value_load(pages[0:1, bass.ds(first_page + j, 1)], min_val=0, max_val=NPOOL - 1)
                sp.dma_start(dst[:, j * 512:j * 512 + 512], src[page]).then_inc(sem_, 16)

        def nsa_sp(sp):
            load_chunks(sp, "qkv", lambda i: io["qkv"][i], SLOT)
            load_chunks(sp, "row", lambda i: io["row"][i], 2 * VR)
            for ch in chunks(sp, plan["cmp"]):
                seq = 2 * (ch.k // 2)
                sp.wait_ge(done[ch.slot], ch.free_at)
                page_loads(sp, ring[:, ch.slot, :], full[ch.slot], (ch.index - ch.k) * 8 + (seq * NPAGE + 4 * (ch.k % 2)),
                           io["cmp_pages"])
                if ch.k % 2:
                    sp.wait_ge(cmp_odd_used, (ch.index - ch.k) // 2 + (ch.k // 2 + 1))
                    for k in range(2):
                        page_loads(sp, sel_b[:, k, :], cmp_odd_in,
                                   (ch.index - ch.k) * 8 + ((seq + 1) * NPAGE + 4 * k), io["cmp_pages"])

            for b in range(NB):
                place, turn = b % 3, b // 3
                if place == 0:
                    for k in range(4):
                        ch = Chunk(plan["selwin"], k, turn)
                        sp.wait_ge(done[ch.slot], ch.free_at)
                        if k < 2:
                            page_loads(sp, ring[:, ch.slot, :], full[ch.slot], b * NPAGE + 4 * k, io["sel_pages"])
                        else:
                            sp.dma_start(ring[:, ch.slot, 0:1024], io["win"][k - 2, b]).then_inc(full[ch.slot], 16)
                    continue
                sel, win, sel_in, win_in = DECODE_PLACES[place]
                if turn:
                    sp.wait_ge(d_ops, b - 2)
                elif place == 1:
                    sp.wait_ge(cmp_odd_used, NB // 2 + 1)
                else:
                    sp.wait_ge(sel_done, 1)
                for k in range(2):
                    page_loads(sp, sel[:, k, :], sel_in, b * NPAGE + 4 * k, io["sel_pages"])
                if not turn:
                    sp.wait_ge(o_used, NU // 3)
                for k in range(2):
                    sp.dma_start(win[:, k, :], io["win"][k, b]).then_inc(win_in, 16)
            load_chunks(sp, "aout", lambda i: io["attn_out"][i], SLOT)

        def nsa_pool(gp):
            gp.wait_ge(mods_done, 12)
            for b in range(NB):
                gp.dma_start(io["win_k_out"][b, :, :, 0:SEQ - DS],
                             io["win"][0, b].rearrange("p (g t) -> p g t", g=2)[:, :, DS:SEQ]).then_inc(stored, 16)
                gp.dma_start(io["win_v_out"][b, 0:SEQ - DS, :], io["win_v"][b, DS:SEQ, :]).then_inc(stored, 16)
            NSTORE[0] += 32 * NB
            gp.wait_ge(x_tile, 8 * 2)
            for dst, name in ((rope_cs, "rope"), (w1, "w1"), (w2k, "w2k"), (w2v, "w2v"), (cpos, "cpos")):
                gp.dma_start(dst, io[name]).then_inc(nsa_in, 16)
            gp.wait_ge(roped, 14)
            gp.wait_ge(raw_copied, 16)
            for half in range(2):
                for par in range(2):
                    src = qk[par * HD:par * HD + HD, 8:12, half:SEQ].rearrange("p (s g) t -> p s g t", s=2)
                    dst = pairs[half * HD:half * HD + HD, :, par::2, 0:SEQ - half]
                    for s in range(2):
                        gp.dma_start(dst[:, s], src[:, s]).then_inc(pairs_in, 16)
            gp.dma_start(io["kv_t"], qk[:, 8:16, :]).then_inc(stored, 16)
            gp.wait_ge(row_copied, 5)
            gp.dma_start(io["v_rows"], vrow[:, 0:QT, 0:512]).then_inc(stored, 16)
            gp.dma_start(io["v_rows_d"], vrow[0:NTS, QT, 0:512]).then_inc(stored, 16)
            NSTORE[0] += 48
            gp.wait_ge(kc_copied, 2 + NB)
            for b in range(NB):
                gp.dma_start(vtail[0:DS, b, :], vrow[DS * b:DS * b + DS, QT, 0:512]).then_inc(vtail_in, 16)

        def nsa_pe(pe):
            n = 1
            u_ready(pe, n)
            pe.wait_ge(nsa_in, 80)

            def rope(t):
                i = ROPED.index(t)
                pe.wait_ge(raw_copied, t + 1)
                if i >= 1:
                    pe.wait_ge(roped, i)
                for hf in range(2):
                    last = PE.matmul(ps[:, 4 + hf, 0:HB], const("rot"), raw[:, t % 2, hf * HB:hf * HB + HB],
                                     start=True, stop=True)
                last.then_inc(rope_ps, 1)

            for c in range(8):
                ch = Chunk(plan["qkv"], c % RING, c // RING)
                pe.wait_ge(full[ch.slot], ch.full_at)
                w = ring[:, ch.slot, :].rearrange("p (k c) -> p k c", c=256)
                for j in range(2):
                    t = 2 * c + j
                    if t >= 2:
                        pe.wait_ge(raw_copied, t - 1)
                    for kt in range(KT):
                        for hf in range(2):
                            last = PE.matmul(ps[:, 2 * j + hf, 0:HB], w[:, kt, j * P:j * P + P],
                                             u[:, kt, hf * HB:hf * HB + HB], start=kt == 0, stop=kt == KT - 1)
                    last.then_inc(done[ch.slot] if j else proj_even, 1)
                    if t - 1 in ROPED:
                        rope(t - 1)
            rope(15)
            row = [Chunk(plan["row"], k, 0) for k in range(4)]
            for i in range(5):
                rows = P if i < QT else NTS
                bk = 6 if i % 2 == 0 else 2
                if i == 0:
                    for ch in row:
                        pe.wait_ge(full[ch.slot], ch.full_at)
                if i == 1:
                    pe.wait_ge(raw_copied, 16)
                if i >= 2:
                    pe.wait_ge(row_copied, i - 1)
                for kt in range(KT):
                    w = ring[:, row[kt // 2].slot, (kt % 2) * VR:(kt % 2) * VR + VR]
                    a = u[:, kt, i * P:i * P + rows]
                    PE.matmul(ps[0:rows, bk, :], a, w[:, 0:512], start=kt == 0, stop=kt == KT - 1)
                    last = PE.matmul(ps[0:rows, bk + 1, 0:48], a, w[:, 512:VR], start=kt == 0, stop=kt == KT - 1)
                    if i == QT and kt % 2:
                        last.then_inc(done[row[kt // 2].slot], 1)
                if i < QT:
                    last.then_inc(row_ready, 1)
            pe.wait_ge(pairs_in, 16 * 8)
            for s in range(2):
                for lp in range(16):
                    last = PE.matmul(ps[:, 0, s:s + 1], w1[:, s, lp, :], cpos[:, s, lp:lp + 1],
                                     start=lp == 0, stop=lp == 15)
            last.then_inc(cc_ready, 1)
            for s in range(2):
                for lp in range(16):
                    last = PE.matmul(ps[:, 4 + s, 0:4 * NCP], w1[:, s, lp, :],
                                     pairs[:, s, :, 2 * lp:2 * lp + 16 * (NCP - 1) + 1:16],
                                     start=lp == 0, stop=lp == 15)
                last.then_inc(conv_p, 1)
            pe.wait_ge(hid_p_ready, 2)
            PE.matmul(ps[:, 1, 0:4 * NCP], w2k, hid_p[:, 0].rearrange("p a b -> p (a b)"), start=True, stop=True)
            for g in range(KVH):
                last = PE.matmul(ps[0:NCP, 0, g * HD:g * HD + HD], hid_p[:, 1, g, :], w2v, start=True, stop=True)
            last.then_inc(kc_p_ps, 1)
            pe.wait_ge(kc_p_copied, 1)
            def compress(it, q):
                i2 = it * 2 + q
                chs = [Chunk(plan["cmp"], 2 * q + a, it) for a in range(2)]
                assert chs[1].slot == chs[0].slot + 1
                for pb in range(2):
                    if pb:
                        pe.wait_ge(cmp_odd_in, i2 * 128 + 128)
                    else:
                        for ch in chs:
                            pe.wait_ge(full[ch.slot], ch.full_at)
                    pe.wait_ge(h1_done, i2 * 4 + (2 * pb + 2))
                    pages_ = sel_b if pb else ring[:, chs[0].slot:chs[0].slot + 2, :]
                    X = pages_.rearrange("p a (q b n) -> p a q b n", q=4, n=32)
                    for s in range(2):
                        for part in range(2):
                            for lp in range(8):
                                last = PE.matmul(ps[:, 2 * pb + s, part * 256:part * 256 + 256],
                                                 w1[:, s, 8 * part + lp, :], X[:, :, :, s * 8 + lp, :],
                                                 start=lp == 0, stop=lp == 7)
                        last.then_inc(conv_d, 1)
                for pb in range(2):
                    pe.wait_ge(hid_ready, i2 * 4 + (2 * pb + 2))
                    pe.wait_ge(kc_copied, i2 * 2 + (pb + 1))
                    PE.matmul(ps[:, 4 + pb, 0:256], w2k, hid[:, pb, 0, :], start=True,
                              stop=True).then_inc(cmp_odd_used if pb else done[chs[0].slot], 1)
                    for g in range(KVH):
                        last = PE.matmul(ps[0:HD, 6 + pb, g * HD:g * HD + HD], hid[:, pb, 1, g * HD:g * HD + HD],
                                         w2v, start=True, stop=True)
                        if g == 0 and pb == 0:
                            last.then_inc(done[chs[1].slot], 1)
                    last.then_inc(kc_ps, 1)

            with pe.Fori(0, NB // 4) as it:
                for q in range(2):
                    compress(it, q)
            pe.wait_ge(kc_copied, 2 + NB)
            pe.wait_ge(q_staged, 1)
            for b in range(NB):
                for g in range(KVH):
                    par = (g % 2) * HD
                    last = PE.matmul(ps[32 * g:32 * g + 32, 0, b * NCS:b * NCS + NCS],
                                     qkeep[par:par + HD, b, g // 2, :],
                                     kc_d[par:par + HD, b, g * HD:g * HD + NCS], start=True, stop=True)
            last.then_inc(cs_ps, 1)
            pe.wait_ge(gm_ready, 1)
            PE.matmul(ps[:, 6, 0:NB * 48], const("pick_t", NTS), gm[0:NTS].rearrange("p a b -> p (a b)"),
                      start=True, stop=True).then_inc(gsel_ps, 1)
            pe.wait_ge(cs_prob, 1)
            for b in range(NB):
                last = PE.transpose(ps[0:NCS, 1 + b // 4, (b % 4) * P:(b % 4) * P + P], sc[:, b, :], const("ident"))
            last.then_inc(cs_tr, 1)
            pe.wait_ge(cs_trc, 1)
            for b in range(NB):
                last = PE.matmul(ps[:, 3, b * NSEL:b * NSEL + NSEL], pt_c[0:NCS, b, :], const("overlap", NCS),
                                 start=True, stop=True)
            last.then_inc(imp_ps, 1)
            for b in range(NB):
                for g in range(KVH):
                    last = PE.matmul(ps[32 * g:32 * g + 32, 4, b * HD:b * HD + HD],
                                     pt_c[0:NCS, b, 32 * g:32 * g + 32], vc_d[0:NCS, b, g * HD:g * HD + HD],
                                     start=True, stop=True)
            last.then_inc(imp_ps, 1)
            pe.wait_ge(imp_copied, 1)
            PE.matmul(ps[:, 5, 0:NB * NSEL], const("same_gt"), imp1.rearrange("p a b -> p (a b)"),
                      start=True, stop=True).then_inc(grp_ps, 1)
            pe.wait_ge(sel_done, 1)

            def scores(i):
                g, j, qt, br = UNITS[i]
                par = (g % 2) * HD
                nk = keys(i)
                k = (kc_p[par:par + HD, g * NCP:g * NCP + NCP] if br == 0 else
                     qk[par:par + HD, 10 + 2 * br + g // 2, 0:nk])
                if i >= 2:
                    pe.wait_ge(sc_exp, i - 1)
                for s in range(2):
                    last = PE.matmul(ps[:, 2 * (i % 2) + s, 0:nk],
                                     qk[par:par + HD, (g // 2) * 4 + 2 * j + s, qt * P:qt * P + P], k,
                                     start=True, stop=True)
                last.then_inc(sc_ps, 1)

            def transposes(i):
                nk = keys(i)
                pe.wait_ge(sc_scaled, i + 1)
                for gr in range(groups(i)):
                    at = GROUPS[i] + gr
                    if at >= 2:
                        pe.wait_ge(tr_copied, at - 1)
                    for kt in range(2 * gr, min(2 * gr + 2, -(-nk // P))):
                        w = min(P, nk - kt * P)
                        for s in range(2):
                            c = (kt % 2) * 256 + s * P
                            last = PE.transpose(ps[0:w, 4 + at % 2, c:c + P], prob[:, i % 2, s, kt * P:kt * P + w],
                                                const("ident"))
                    last.then_inc(tr_ps, 1)

            def values(i):
                g, j, qt, br = UNITS[i]
                nk, out = keys(i), i // 3
                pe.wait_ge(tr_copied, GROUPS[i + 1])
                if i % 3 == 0 and out >= 2:
                    pe.wait_ge(o_used, out - 1)
                nt = -(-nk // P)
                for kt in range(nt):
                    w = min(P, nk - kt * P)
                    v = (vc_p[0:NCP, g * HD:g * HD + HD] if br == 0 else
                         vrow[:, kt, (br - 1) * 256 + g * HD:(br - 1) * 256 + g * HD + HD])
                    for s in range(2):
                        c = (kt % 2) * 256 + s * P
                        last = PE.matmul(ps[s * HD:s * HD + HD, 6 + out % 2, 0:P], v, pt[0:w, i % 2, kt // 2, c:c + P],
                                         start=i % 3 == 0 and kt == 0, stop=i % 3 == 2 and kt == nt - 1, skip_group_check=True)
                if i % 3 == 2:
                    last.then_inc(o_ps, 1)

            scores(0)
            scores(1)
            for i in range(NU):
                if i + 2 < NU:
                    scores(i + 2)
                if i >= 1:
                    values(i - 1)
                transposes(i)
            values(NU - 1)

            def tail_values(b, br):
                for g in range(KVH):
                    m = PE.matmul(ps[32 * g:32 * g + 32, 7, br * HD:br * HD + HD],
                                  ptt_d[0:DS, P * br + 32 * g:P * br + 32 * g + 32],
                                  vtail[0:DS, b, 256 * br + g * HD:256 * br + g * HD + HD],
                                  start=False, stop=True, skip_group_check=True)
                return m

            def decode_scores(b):
                ch = [Chunk(plan["selwin"], k, b // 3) for k in range(4)]
                if b % 3:
                    sel, win, sel_in, win_in = DECODE_PLACES[b % 3]
                    pe.wait_ge(sel_in, 128 * (b // 3 + 1))
                    pe.wait_ge(win_in, 32 * (b // 3 + 1))
                else:
                    for c in ch:
                        pe.wait_ge(full[c.slot], c.full_at)
                for j in range(3):
                    for g in range(KVH):
                        par, gp = (g % 2) * HD, g // 2
                        if j < 2:
                            k = (sel[par:par + HD, j, :] if b % 3 else ring[par:par + HD, ch[j].slot, :])                                .rearrange("p (a c) -> p a c", a=4)[:, :, gp * P:gp * P + P]
                        else:
                            k = (win[par:par + HD, 0, :] if b % 3 else
                                 ring[par:par + HD, ch[2].slot, :])[:, gp * SEQ:gp * SEQ + SEQ]
                        m = PE.matmul(ps[32 * g:32 * g + 32, j, :], qkeep[par:par + HD, b, gp, :], k, start=True, stop=True)
                if b % 3 == 0:
                    m.then_inc(done[ch[2].slot], 1)
                for j in range(2):
                    for g in range(KVH):
                        par, gp = (g % 2) * HD, g // 2
                        m = PE.matmul(ps[32 * g:32 * g + 32, 3, DS * j:DS * j + DS], qkeep[par:par + HD, b, gp, :],
                                      qk[par:par + HD, 12 + 2 * j + gp, SEQ + DS * b:SEQ + DS * b + DS],
                                      start=True, stop=True)
                m.then_inc(d_scores, 1)

            pe.wait_ge(o_used, NU // 3)
            pe.wait_ge(vtail_in, 16 * NB)
            decode_scores(0)
            for b in range(NB):
                ch = [Chunk(plan["selwin"], k, b // 3) for k in range(4)]
                sel, win = DECODE_PLACES.get(b % 3, (None,) * 4)[:2]
                pe.wait_ge(d_exp, b + 1)
                if b:
                    pe.wait_ge(d_out, b)
                for j in range(12):
                    PE.transpose(ps[:, 4 + j // 4, (j % 4) * P:(j % 4) * P + P], ps_d[:, j * P:j * P + P],
                                 const("ident"))
                for j in range(2):
                    last = PE.transpose(ps[0:DS, 7, 256 + j * P:256 + j * P + P],
                                        ps_d[:, 1536 + DS * j:1536 + DS * j + DS], const("ident"))
                last.then_inc(d_tr, 1)
                if b + 1 < NB:
                    decode_scores(b + 1)
                pe.wait_ge(d_trc, b + 1)
                for kt in range(8):
                    v = sel[:, kt // 4, :] if b % 3 else ring[:, ch[kt // 4].slot, :]
                    for g in range(KVH):
                        at = (kt % 4) * 512 + 256 + g * HD
                        m = PE.matmul(ps[32 * g:32 * g + 32, 7, 0:HD], pts_d[:, kt * P + 32 * g:kt * P + 32 * g + 32],
                                      v[:, at:at + HD], start=kt == 0, stop=False, skip_group_check=True)
                    if kt % 4 == 3 and b % 3 == 0:
                        m.then_inc(done[ch[kt // 4].slot], 1)
                tail_values(b, 0)
                v = win[:, 1, :] if b % 3 else ring[:, ch[3].slot, :]
                for kt in range(4):
                    for g in range(KVH):
                        at = kt * 256 + g * HD
                        m = PE.matmul(ps[32 * g:32 * g + 32, 7, HD:2 * HD],
                                      pts_d[:, (8 + kt) * P + 32 * g:(8 + kt) * P + 32 * g + 32],
                                      v[:, at:at + HD], start=kt == 0, stop=False, skip_group_check=True)
                if b % 3 == 0:
                    m.then_inc(done[ch[3].slot], 1)
                tail_values(b, 1).then_inc(d_ops, 1)
            pe.wait_ge(d_out, NB)
            for b in range(NB):
                last = PE.transpose(ps[:, b // 4, (b % 4) * P:(b % 4) * P + P],
                                    osum[:, b].rearrange("p a b -> p (a b)"), const("ident"))
            last.then_inc(ot_ps, 1)
            pe.wait_ge(ot_copied, 1)
            for c in range(4):
                ch = Chunk(plan["aout"], c, 0)
                pe.wait_ge(full[ch.slot], ch.full_at)
                w = ring[:, ch.slot, :].rearrange("p (k c) -> p k c", c=256)
                for j in range(2):
                    m = 2 * c + j
                    if m >= 2:
                        pe.wait_ge(x_tile, 8 * (n + 1) + m - 1)
                    for kt in range(KT):
                        for hf in range(2):
                            last = PE.matmul(ps[:, 2 * (m % 2) + hf, 0:HB], w[:, kt, j * P:j * P + P],
                                             u[:, kt, hf * HB:hf * HB + HB], start=kt == 0, stop=kt == KT - 1)
                    last.then_inc(done[ch.slot] if j else aout_even, 1)

        def nsa_act(act, link):
            for t in range(16):
                ch = Chunk(plan["qkv"], (t // 2) % RING, t // 2 // RING)
                if t % 2:
                    act.wait_ge(done[ch.slot], ch.done_at)
                else:
                    act.wait_ge(proj_even, t // 2 + 1)
                dst = qk[:, t] if t not in ROPED else raw[:, t % 2]
                if t in ROPED and t >= 2:
                    act.wait_ge(roped, sum(1 for z in ROPED if z <= t - 2))
                S.activation(dst.rearrange("p (a b) -> p a b", b=HB), ps[:, 2 * (t % 2):2 * (t % 2) + 2, 0:HB],
                             ACT.Copy).then_inc(raw_copied, 1)
            row3 = Chunk(plan["row"], 3, 0)
            for i in range(5):
                rows = P if i < QT else NTS
                bk = 6 if i % 2 == 0 else 2
                if i < QT:
                    act.wait_ge(row_ready, i + 1)
                else:
                    act.wait_ge(done[row3.slot], row3.done_at)
                S.activation(vrow[0:rows, i, 0:512], ps[0:rows, bk, :], ACT.Copy)
                S.activation(vrow[0:rows, i, 512:VR], ps[0:rows, bk + 1, 0:48], ACT.Sigmoid).then_inc(row_copied, 1)
            act.wait_ge(cc_ready, 1)
            S.activation(cc, ps[:, 0, 0:2], ACT.Copy).then_inc(cc_copied, 1)
            act.wait_ge(cc_copied, 1)
            for s in range(2):
                act.wait_ge(conv_p, s + 1)
                S.activation(hid_p[:, s].rearrange("p a b -> p (a b)"), ps[:, 4 + s, 0:4 * NCP],
                             ACT.Gelu_apprx_tanh, bias=cc[:, s:s + 1]).then_inc(hid_p_ready, 1)
            act.wait_ge(kc_p_ps, 1)
            S.activation(kc_p, ps[:, 1, 0:4 * NCP], ACT.Copy)
            S.activation(vc_p[0:NCP, :], ps[0:NCP, 0, 0:256], ACT.Copy).then_inc(kc_p_copied, 1)
            with act.Fori(0, NB // 2) as it:
                for pb in range(2):
                    for s in range(2):
                        act.wait_ge(conv_d, it * 4 + (2 * pb + s + 1))
                        S.activation(f1[:, pb, s, :], ps[:, 2 * pb + s, 0:256], ACT.Copy).then_inc(f1_ready, 1)
                    for s in range(2):
                        act.wait_ge(h1_done, it * 4 + (2 * pb + s + 1 + 4))
                        S.activation(hid[:, pb, s].rearrange("p (g q n) -> p q g n", g=4, n=8),
                                     f1[:, pb, s].rearrange("p (q g n) -> p q g n", g=4, n=8),
                                     ACT.Gelu_apprx_tanh, bias=cc[:, s:s + 1]).then_inc(hid_ready, 1)
                for pb in range(2):
                    act.wait_ge(kc_ps, it * 2 + (pb + 1))
                    S.activation(kc_d[:, it * 2 + pb, :], ps[:, 4 + pb, 0:256], ACT.Copy)
                    S.activation(vc_d[0:HD, it * 2 + pb, :], ps[0:HD, 6 + pb, 0:256], ACT.Copy).then_inc(kc_copied, 1)
            act.wait_ge(cs_shift, 1)
            scf = sc.rearrange("p a b -> p (a b)")
            S.activation(scf, scf, ACT.Exp, scale=SCALE).then_inc(cs_exp, 1)
            act.wait_ge(cs_tr, 1)
            S.activation(pt_c[0:NCS].rearrange("p a b -> p (a b)"),
                         ps[0:NCS, 1:3, :].rearrange("p a b -> p (a b)"), ACT.Copy).then_inc(cs_trc, 1)
            act.wait_ge(sel_done, 1)

            def exps(i):
                nk = keys(i)
                act.wait_ge(sc_max, i + 1)
                for s in range(2):
                    last = S.activation(prob[:, i % 2, s, 0:nk], ps[:, 2 * (i % 2) + s, 0:nk], ACT.Exp, scale=SCALE,
                                        bias=mx[:, i % 2, s:s + 1], accum_out=den[:, i % 2, s:s + 1])
                last.then_inc(sc_exp, 1)

            def output(out):
                g, j, qt, _ = UNITS[3 * out]
                act.wait_ge(o_ps, out + 1)
                S.activation(u[:, 2 * g + j, qt * P:qt * P + P], ps[:, 6 + out % 2, 0:P], ACT.Copy).then_inc(o_used, 1)

            exps(0)
            for i in range(NU):
                if i + 1 < NU:
                    exps(i + 1)
                nk = keys(i)
                for gr in range(groups(i)):
                    act.wait_ge(tr_ps, GROUPS[i] + gr + 1)
                    cols = min(512, -(-(nk - gr * 256) // P) * 256)
                    S.activation(pt[0:min(P, nk), i % 2, gr, 0:cols], ps[0:min(P, nk), 4 + (GROUPS[i] + gr) % 2, 0:cols],
                                 ACT.Copy).then_inc(tr_copied, 1)
                if i % 3 == 1 and i > 3:
                    output(i // 3 - 1)
            output(NU // 3 - 1)
            with act.Fori(0, NB) as b:
                act.wait_ge(d_max, b + 1)
                for j, (a0, a1, src) in enumerate(((0, 1024, ps[:, 0:2, :].rearrange("p a b -> p (a b)")),
                                                   (1024, 1536, ps[:, 2, :]),
                                                   (1536, 1540, ps[:, 3, 0:DS]), (1540, 1544, ps[:, 3, DS:2 * DS]))):
                    last = S.activation(ps_d[:, a0:a1], src, ACT.Exp, scale=SCALE, bias=nm2[:, j % 2:j % 2 + 1],
                                        accum_out=d4[:, j:j + 1])
                last.then_inc(d_exp, 1)
                act.wait_ge(d_tr, b + 1)
                S.activation(pts_d, ps[:, 4:7, :].rearrange("p a b -> p (a b)"), ACT.Copy)
                S.activation(ptt_d[0:DS, :], ps[0:DS, 7, 256:512], ACT.Copy).then_inc(d_trc, 1)

        def nsa_dve(dve, link):
            dve.wait_ge(nsa_in, 80)
            for i, t in enumerate(ROPED):
                dve.wait_ge(raw_copied, t + 1)
                link(V.tensor_tensor(t1, raw[:, t % 2], rope_cs[:, 0], ALU.mult))
                dve.wait_ge(rope_ps, i + 1)
                link(V.tensor_tensor(t2.rearrange("p (a b) -> p a b", b=HB), ps[:, 4:6, 0:HB],
                                     rope_cs[:, 1].rearrange("p (a b) -> p a b", b=HB), ALU.mult))
                V.tensor_tensor(qk[:, t], t1, t2, ALU.add).then_inc(roped, 1)
                dve.wait_ge(roped, i + 1)
            link(V.memset(qkeep[:, :, :, :], 0.0))
            V.memset(m8[0:1, 0:1], 0.0).then_inc(h1_done, 4)
            V.memset(s8[0:1, 0:1], 0.0).then_inc(kc_copied, 2)
            V.memset(di8[0:1, 0:1], 0.0).then_inc(cmp_odd_used, 1)
            for gp in range(2):
                last = V.tensor_copy(qkeep[:, :, gp, 0:16].rearrange("p b (r t) -> p b r t", t=DS),
                                     qk[:, 4 * gp:4 * gp + 4, SEQ:T].rearrange("p r (b t) -> p b r t", t=DS))
            last.then_inc(q_staged, 1)
            with dve.Fori(0, NB // 2) as it:
                for pb in range(2):
                    for s in range(2):
                        dve.wait_ge(f1_ready, it * 4 + (2 * pb + s + 1))
                        a = f1[:, pb, s].rearrange("p (q g n) -> p q g n", g=4, n=8)
                        b2 = ps[:, 2 * pb + s, 256:512].rearrange("p (q g n) -> p q g n", g=4, n=8)
                        V.tensor_tensor(a[:, :, :, 0:7], a[:, :, :, 0:7], b2[:, :, :, 1:8], ALU.add)
                        V.tensor_tensor(a[:, 0:7, :, 7], a[:, 0:7, :, 7], b2[:, 1:8, :, 0],
                                        ALU.add).then_inc(h1_done, 1)
            dve.wait_ge(row_copied, 5)
            dve.wait_ge(kc_copied, 2 + NB)
            V.tensor_tensor(gm[0:NTS], vrow[0:NTS, QT, 512:VR].unsqueeze(1).to_broadcast([NTS, NB, 48]),
                            const("own_b", NTS).unsqueeze(2).to_broadcast([NTS, NB, 48]), ALU.mult).then_inc(gm_ready, 1)
            dve.wait_ge(cs_ps, 1)
            s0 = ps[:, 0, 0:NB * NCS].rearrange("p (a b) -> p a b", b=NCS)
            link(V.tensor_reduce(m8, s0, AX.X, ALU.max))
            V.tensor_tensor(sc, s0, m8.unsqueeze(2).to_broadcast([P, NB, NCS]), ALU.subtract).then_inc(cs_shift, 1)
            dve.wait_ge(cs_exp, 1)
            link(V.tensor_reduce(s8, sc, AX.X, ALU.add))
            link(V.reciprocal(s8, s8))
            V.tensor_tensor(sc, sc, s8.unsqueeze(2).to_broadcast([P, NB, NCS]), ALU.mult).then_inc(cs_prob, 1)
            dve.wait_ge(gsel_ps, 1)
            hof = const("head_of").unsqueeze(1).to_broadcast([P, 24, HEADS])
            link(V.tensor_tensor(gtmp, ps[:, 6, 0:NB * 48].rearrange("p (a b) -> p a b", b=HEADS), hof, ALU.mult))
            link(V.tensor_reduce(gs.rearrange("p a b -> p (a b)"), gtmp, AX.X, ALU.add))
            dve.wait_ge(imp_ps, 1)
            V.tensor_copy(imp1.rearrange("p a b -> p (a b)"), ps[:, 3, 0:NB * NSEL]).then_inc(imp_copied, 1)
            dve.wait_ge(imp_ps, 2)
            link(V.tensor_tensor(ocs, ps[:, 4, :].rearrange("p (a b) -> p a b", b=HD),
                                 gs[:, :, 0:1].to_broadcast([P, NB, HD]), ALU.mult))
            dve.wait_ge(grp_ps, 1)
            im = ps[:, 5, 0:NB * NSEL].rearrange("p (a b) -> p a b", b=NSEL)[:, :, 1:15]
            no = const("block_no")[:, 1:15].unsqueeze(1).to_broadcast([P, NB, 14])
            link(V.tensor_reduce(m8, im, AX.X, ALU.min))
            link(V.tensor_tensor(eqj, im, m8.unsqueeze(2).to_broadcast([P, NB, 14]), ALU.is_equal))
            link(V.tensor_tensor(eqj, eqj, no, ALU.mult))
            link(V.tensor_reduce(di8, eqj, AX.X, ALU.max))
            link(V.tensor_tensor(eqj, di8.unsqueeze(2).to_broadcast([P, NB, 14]), no, ALU.is_equal))
            V.tensor_scalar(negm, eqj, NEG, None, ALU.mult).then_inc(sel_done, 1)

            def mask_max(i):
                g, j, qt, br = UNITS[i]
                b0, nk = 2 * (i % 2), keys(i)
                dve.wait_ge(sc_ps, i + 1)
                if br == 0:
                    blk = ps[:, b0:b0 + 2, 0:NCP]
                    msk = const("cmp_neg")[:, qt * NCP:qt * NCP + NCP].unsqueeze(1).to_broadcast([P, 2, NCP])
                else:
                    blk = ps[:, b0:b0 + 2, qt * P:qt * P + P]
                    msk = const("causal").unsqueeze(1).to_broadcast([P, 2, P])
                link(V.tensor_tensor(blk, blk, msk, ALU.add))
                link(V.tensor_reduce(mx[:, i % 2, :], ps[:, b0:b0 + 2, 0:nk], AX.X, ALU.max))
                V.tensor_scalar(mx[:, i % 2, :], mx[:, i % 2, :], -SCALE, None, ALU.mult).then_inc(sc_max, 1)

            mask_max(0)
            for i, (g, j, qt, br) in enumerate(UNITS):
                if i + 1 < NU:
                    mask_max(i + 1)
                nk, c = keys(i), cf[:, i % 2, :]
                dve.wait_ge(sc_exp, i + 1)
                link(V.reciprocal(c, den[:, i % 2, :]))
                gate = 512 + br * HEADS + g * REP + 2 * j
                link(V.tensor_tensor(c, c, vrow[:, qt, gate:gate + 2], ALU.mult))
                for s in range(2):
                    p = prob[:, i % 2, s, 0:nk]
                    if br == 0:
                        last = V.scalar_tensor_tensor(p, p, c[:, s:s + 1], const("cmp_valid")[:, qt * NCP:qt * NCP + NCP],
                                                      ALU.mult, ALU.mult)
                    else:
                        last = V.tensor_scalar(p, p, c[:, s:s + 1], None, ALU.mult)
                last.then_inc(sc_scaled, 1)

            def decode_max(b):
                dve.wait_ge(d_scores, b + 1)
                blk = ps[:, 0:2, :].rearrange("p a b -> p (a b)")[:, 64:960].rearrange("p (a b) -> p a b", b=64)
                V.tensor_tensor(blk, blk, negm[:, b].unsqueeze(2).to_broadcast([P, 14, 64]), ALU.add)
                V.tensor_tensor(ps[:, 2, 0:DS], ps[:, 2, 0:DS], const("win_edge"), ALU.add)
                link(V.tensor_tensor(ps[:, 3, 0:2 * DS], ps[:, 3, 0:2 * DS], const("tails"), ALU.add))
                V.tensor_reduce(m2s[:, 0:1], ps[:, 0:2, :].rearrange("p a b -> p (a b)"), AX.X, ALU.max)
                V.tensor_reduce(m2s[:, 1:2], ps[:, 2, :], AX.X, ALU.max)
                link(V.tensor_reduce(t2s, ps[:, 3, 0:2 * DS].rearrange("p (a b) -> p a b", b=DS), AX.X, ALU.max))
                link(V.tensor_tensor(m2s, m2s, t2s, ALU.max))
                V.tensor_scalar(nm2, m2s, -SCALE, None, ALU.mult).then_inc(d_max, 1)

            def decode_out(b, ahead):
                dve.wait_ge(d_exp, b + 1)
                link(V.tensor_tensor(d2, d4[:, 0:2], d4[:, 2:4], ALU.add))
                link(V.reciprocal(d2, d2))
                link(V.tensor_tensor(c2, d2, gs[:, b, 1:3], ALU.mult))
                if ahead:
                    decode_max(b + 1)
                dve.wait_ge(d_ops, b + 1)
                link(V.scalar_tensor_tensor(tmpo, ps[:, 7, 0:HD], c2[:, 0:1], ocs[:, b, :], ALU.mult, ALU.add))
                link(V.scalar_tensor_tensor(osum[:, b, 0, :], ps[:, 7, HD:2 * HD], c2[:, 1:2], tmpo, ALU.mult, ALU.add))
                V.tensor_copy(osum[:, b, 1, :], osum[:, b, 0, :]).then_inc(d_out, 1)

            dve.wait_ge(stored, 32 * NB + 16)
            decode_max(0)
            with dve.Fori(0, NB - 1) as b:
                link.enter(b, 8)
                decode_out(b, True)
            link.leave(NB - 1)
            decode_out(NB - 1, False)
            dve.wait_ge(ot_ps, 1)
            for par in range(2):
                for rh in range(2):
                    for bh in range(2):
                        src = ps[par * HD:par * HD + HD, bh, :].rearrange("p (b g r t) -> p g b r t", b=4, g=4, r=8)
                        dst = u[par * HD:par * HD + HD, rh::2, SEQ + 16 * bh:SEQ + 16 * bh + 16]
                        last = V.tensor_copy(dst.rearrange("p g (b t) -> p g b t", t=DS), src[:, :, :, 2 * rh + par, :])
            last.then_inc(ot_copied, 1)
            for m in range(KT):
                ch = Chunk(plan["aout"], m // 2, 0)
                if m % 2:
                    dve.wait_ge(done[ch.slot], ch.done_at)
                else:
                    dve.wait_ge(aout_even, m // 2 + 1)
                residual(1, m, 2 * (m % 2), tmp_d[:, m % 2], link)
        top[0] = 0
        mrow = carve(T)
        m0r = carve(NB)
        bg = carve(1)
        acol = carve(5, MH)
        wcol = carve(5, MH)
        emcol = carve(MH)
        ncm = carve(MH, T)
        em = carve(MH, T)
        wint = carve(MH, NTS)
        xp = carve(4, XPW)
        acc = carve(4, XPW)
        xc = carve(4, T)
        zs = carve(4, T)
        qT = carve(4, T)
        kT = carve(4, T)
        vr = carve(5, SEQ)
        kw = carve(5, SEQ)
        bd = carve(3, 4, P)
        ex = carve(2, SEQ)
        vb = carve(2, SEQ)
        convw = carve(16, 5)
        skipgn = carve(16, 2)
        nst = carve(16, NB)
        sconv = carve(16, NB * 3)
        nnew = carve(16, C9)
        cvo = carve(16, C9 * 3)
        qw = carve(4, NTS)
        nprod = carve(4, NTS)
        ssp = carve(NTS)[0:NTS]
        den1 = carve(1)
        rden = carve(SEQ)
        xm_d = carve(4, NTS)
        AT_ACC = 544 + 8 + 1 + 20 + 20 + 4 + 2 * MH * T + MH * NTS + 4 * XPW
        spt = carve(4, SEQ, at=AT_ACC)
        qwm = ex.rearrange("p a b -> p (a b)").rearrange("p (a b c) -> p a b c", a=4, b=NB)
        work = xp[:, :, 0:T]
        ig, lf, cumf, av, cm, wsr = (carve(T, at=AT_ACC + 4 * XPW + i * T) for i in range(6))
        hrow = qkeep[:].rearrange("p a b c -> p (a b c)")
        KS = MHD ** -0.5
        c_stored = [sem(f"c_stored{i}") for i in range(RING)]

        (ml_in, bd_in, gt_dve, gt_act, col_ps, bc_ps, bc_copied, gates_done) = (sem(n) for n in (
            "ml_in bd_in gt_dve gt_act col_ps bc_ps bc_copied gates_done").split())
        (pr_even, pr_copied, xp_ready, conv_init, conv_done, xc_ready, qk_ps, qk_copied, vk_ps, vk_copied, sm_ps, ex_ready,
         ex_done, sp_ready, dn_ps, h_ps, h_scaled, h_sq, h_ms, h_root, hd_sq, hd_ms, hd_root, hn_ready, y_even, qw_ready, s_ps, s_pre, s_exp, ssp_ready,
         vb_ready, up_ps, c_new, hd_scaled, hdt_ps, cf_ps, cf_copied, cf_stored, nn_ps, nn_done) = (sem(n) for n in (
             "pr_even pr_copied xp_ready conv_init conv_done xc_ready qk_ps qk_copied vk_ps vk_copied sm_ps ex_ready "
             "ex_done sp_ready dn_ps h_ps h_scaled h_sq h_ms h_root hd_sq hd_ms hd_root hn_ready y_even qw_ready s_ps s_pre s_exp ssp_ready "
             "vb_ready up_ps c_new hd_scaled hdt_ps cf_ps cf_copied cf_stored nn_ps nn_done").split())

        def hchunk(h, k):
            pl = plan["mlstm"]
            n0, _, fu, do, full0, done0 = pl
            s = (n0 + k) % RING
            f_head = sum(fu[j % len(fu)] for j in range(16) if (j - k) % RING == 0)
            d_head = sum(do[j % len(do)] for j in range(16) if (j - k) % RING == 0)
            f_before = sum(16 for j in range(k) if (j - k) % RING == 0)
            d_before = sum(do[j] for j in range(k) if (j - k) % RING == 0)
            c = Chunk.__new__(Chunk)
            c.slot, c.k = s, k
            c.full_at = h * f_head + (full0[s] + f_before + 16)
            c.free_at = h * d_head + (done0[s] + d_before)
            c.done_at = h * d_head + (done0[s] + d_before + do[k])
            return c

        def mlstm_sp(sp):
            for ch in (Chunk(plan["mgate"], 0, 0),):
                sp.wait_ge(done[ch.slot], ch.free_at)
                sp.dma_start(ring[:, ch.slot, 0:KT * 36], io["mgate"]).then_inc(full[ch.slot], 16)
            with sp.Fori(0, MH) as h:
                for k in range(16):
                    ch = hchunk(h, k)
                    if 8 <= k:
                        sp.wait_ge(c_stored[ch.slot], h * 32 + (16 if k < 12 else 32))
                    else:
                        sp.wait_ge(done[ch.slot], ch.free_at)
                    if k < 4:
                        src, w = io["ml_in"][h * 4 + k], SLOT
                    elif k < 12:
                        src, w = io["state_c"][h * NB + (k - 4)], SLOT
                    else:
                        src, w = io["ml_out"][h * 4 + (k - 12)], 1024
                    sp.dma_start(ring[:, ch.slot, 0:w], src).then_inc(full[ch.slot], 16)

        def mlstm_pool(gp):
            gp.wait_ge(x_tile, 8 * 5)
            for dst, name in ((convw, "convw"), (skipgn, "skipgn"), (nst, "nst"), (sconv, "sconv")):
                gp.dma_start(dst[:, :, :], io[name]).then_inc(ml_in, 16)
            gp.dma_start(m0r[0:MH, :], io["m0"]).then_inc(ml_in, 16)
            gp.dma_start(bg[0:36, :], io["bg"]).then_inc(ml_in, 16)
            gp.dma_start(bd, io["bd"][0]).then_inc(bd_in, 16)

            def head(h, last):
                gp.wait_ge(vk_ps, h * 10 + 10)
                if not last:
                    gp.dma_start(bd, io["bd"][h + 1]).then_inc(bd_in, 16)
                gp.wait_ge(cf_copied, h + 1)
                gp.dma_start(io["cp_out"][h], spt.rearrange("p a b -> p (a b)")).then_inc(cf_stored, 16)
                for b in range(NB):
                    gp.wait_ge(c_new, h * 4 * NB + 4 * (b + 1))
                    gp.dma_start(io["c_out"][h * NB + b], ring[:, hchunk(h, 4 + b).slot, :])\
                        .then_inc(c_stored[hchunk(h, 4 + b).slot], 16)

            with gp.Fori(0, MH - 1) as h:
                head(h, False)
            head(MH - 1, True)
            gp.dma_start(io["m_out"], mrow[0:MH, :]).then_inc(stored, 16)
            gp.wait_ge(nn_done, MH)
            gp.dma_start(io["n_out"], nnew[:, :, :]).then_inc(stored, 16)
            gp.dma_start(io["conv_out"], cvo[:, :, :]).then_inc(stored, 16)
            NSTORE[0] += 48
            gp.wait_ge(cf_stored, 16 * MH)
            for s in range(RING):
                gp.wait_ge(c_stored[s], 16 * 2 * MH)

        def mlstm_pe(pe):
            n = 4
            u_ready(pe, n)
            ch = Chunk(plan["mgate"], 0, 0)
            pe.wait_ge(full[ch.slot], ch.full_at)
            w = ring[:, ch.slot, 0:KT * 36].rearrange("p (k c) -> p k c", c=36)
            for kt in range(KT):
                for hf in range(2):
                    last = PE.matmul(ps[0:36, hf, 0:HB], w[:, kt, :], u[:, kt, hf * HB:hf * HB + HB],
                                     start=kt == 0, stop=kt == KT - 1)
            last.then_inc(done[ch.slot], 1)
            pe.wait_ge(gates_done, 1)
            for r, (row, o) in enumerate(((av, 0), (wsr, 20), (em, 40))):
                src = row if r < 2 else em[:, 0]
                for i in range(5):
                    if r == 2 and i < 4:
                        continue
                    rows = P if i < 4 else NTS
                    if r == 2:
                        for q in range(4):
                            last = PE.matmul(ps[32 * q:32 * q + NTS, 2, 56:60], src[0:MH, SEQ:T],
                                             const("ident", MH)[:, 0:MH], start=True, stop=True, skip_group_check=True)
                        continue
                    last = PE.matmul(ps[0:rows, 2, o + MH * i:o + MH * i + MH],
                                     (src[0:MH, i * P:i * P + rows]), const("ident", MH)[:, 0:MH],
                                     start=True, stop=True)
            last.then_inc(col_ps, 1)
            for r, row in enumerate((cm, mrow)):
                for hh in range(MH):
                    j = r * MH + hh
                    if j >= 2:
                        pe.wait_ge(bc_copied, j - 1)
                    for hf in range(2):
                        last = PE.matmul(ps[:, 4 + 2 * (j % 2) + hf, 0:HB], const("head_row", MH)[:, hh * P:hh * P + P],
                                         row[0:MH, hf * HB:hf * HB + HB], start=True, stop=True)
                    last.then_inc(bc_ps, 1)
            for hh in range(MH):
                last = PE.matmul(ps[:, 3, hh * NTS:hh * NTS + NTS], const("head_row", MH)[:, hh * P:hh * P + P],
                                 lf[0:MH, SEQ:T], start=True, stop=True)
            last.then_inc(bc_ps, 1)
            pe.wait_ge(gates_done, 2)

            with pe.Fori(0, MH) as h:
                for k in range(4):
                    c = hchunk(h, k)
                    pe.wait_ge(full[c.slot], c.full_at)
                    w = ring[:, c.slot, :].rearrange("p (k c) -> p k c", c=256)
                    for j in range(2):
                        t = 2 * k + j
                        if t >= 2:
                            pe.wait_ge(pr_copied, h * 8 + (t - 1))
                        for kt in range(KT):
                            for hf in range(2):
                                last = PE.matmul(ps[:, 2 * j + hf, 0:HB], w[:, kt, j * P:j * P + P],
                                                 u[:, kt, hf * HB:hf * HB + HB], start=kt == 0, stop=kt == KT - 1)
                        last.then_inc(done[c.slot] if j else pr_even, 1)
                pe.wait_ge(bd_in, h * 16 + 16)
                pe.wait_ge(xc_ready, h * 4 + 4)
                for t in range(8):
                    b0 = 4 + 2 * (t % 2)
                    if t >= 2:
                        pe.wait_ge(qk_copied, h * 8 + (t - 1))
                    for hf in range(2):
                        last = PE.matmul(ps[:, b0 + hf, 0:HB], bd[:, t // 4, t % 4, :],
                                         xc[:, t % 4, hf * HB:hf * HB + HB], start=True, stop=True)
                    last.then_inc(qk_ps, 1)
                pe.wait_ge(pr_copied, h * 8 + 8)
                pe.wait_ge(bd_in, 16)
                for i in range(5):
                    rows = P if i < 4 else NTS
                    for v in range(2):
                        j = 2 * i + v
                        if j >= 4:
                            pe.wait_ge(vk_copied, h * 10 + (j - 3))
                        for t in range(4):
                            if v == 0:
                                a = xp[:, t, 3 + i * P:3 + i * P + P] if i < 4 else xm_d[:, t, :]
                            else:
                                a = xc[:, t, i * P:i * P + rows]
                            last = PE.matmul(ps[0:rows, j % 4, t * P:t * P + P], a, bd[:, 2 if v == 0 else 1, t, :],
                                             start=True, stop=True)
                        last.then_inc(vk_ps, 1)
                pe.wait_ge(qk_copied, h * 8 + 8)
                for t in range(4):
                    last = PE.matmul(ps[0:NTS, 4, 0:NTS], kT[:, t, SEQ:T], qT[:, t, SEQ:T], start=t == 0, stop=t == 3)
                last.then_inc(s_ps, 1)
                for i in range(4):
                    if i >= 2:
                        pe.wait_ge(sp_ready, h * 4 + (i - 1))
                    for t in range(4):
                        last = PE.matmul(ps[:, 5, 0:SEQ - i * P] if i % 2 == 0 else ps[:, 6, 0:SEQ - i * P],
                                         kT[:, t, i * P:i * P + P], qT[:, t, i * P:SEQ], start=t == 0, stop=t == 3)
                    last.then_inc(sm_ps, 1)
                pe.wait_ge(sp_ready, h * 4 + 4)
                pe.wait_ge(vk_copied, h * 10 + 10)
                for i in range(4):
                    last = PE.matmul(ps[:, 7, i * P:SEQ], const("ones"), spt[:, i, 0:SEQ - i * P],
                                     start=i == 0, stop=i == 3)
                last.then_inc(dn_ps, 1)
                for e in range(4):
                    for i in range(4):
                        last = PE.matmul(ps[:, e, i * P:SEQ], vr[:, i, e * P:e * P + P], spt[:, i, 0:SEQ - i * P],
                                         start=i == 0, stop=i == 3)
                last.then_inc(h_ps, 1)
                pe.wait_ge(qw_ready, h + 1)
                pe.wait_ge(ssp_ready, h + 1)
                for t in range(4):
                    for q in range(4):
                        PE.matmul(ps[32 * q:32 * q + NTS, 6, 0:1], nprod[:, t, :], const("ones")[:, 0:1],
                                  start=t == 0, stop=False, skip_group_check=True)
                for q in range(4):
                    PE.matmul(ps[32 * q:32 * q + NTS, 6, 0:1], ssp[:, :], const("ones", NTS)[:, 0:1],
                              start=False, stop=True, skip_group_check=True)
                PE.matmul(ps[0:NTS, 5, :], ssp[:, :], vr[0:NTS, 4, :], start=True, stop=False,
                          skip_group_check=True)
                for t in range(4):
                    pe.wait_ge(h_scaled, h * 4 + (t + 1))
                    for i in range(4):
                        last = PE.matmul(ps[:, t, :], kw[:, i, t * P:t * P + P], vr[:, i, :], start=i == 0, stop=i == 3)
                last.then_inc(cf_ps, 1)
                for t in range(4):
                    for i in range(4):
                        last = PE.matmul(ps[:, 4, t * C9:t * C9 + 1], kw[:, i, t * P:t * P + P], const("ones")[:, 0:1],
                                         start=i == 0, stop=i == 3)
                    last = PE.matmul(ps[:, 4, t * C9 + 1:t * C9 + C9], kw[0:NTS, 4, t * P:t * P + P],
                                     const("own_b", NTS), start=True, stop=True)
                last.then_inc(nn_ps, 1)
                pe.wait_ge(h_sq, h + 1)
                for t in range(4):
                    last = PE.matmul(ps[:, 7, :], const("mean_h"), work[:, t, 0:SEQ], start=t == 0, stop=t == 3)
                last.then_inc(h_ms, 1)
                for b in range(NB):
                    c = hchunk(h, 4 + b)
                    pe.wait_ge(full[c.slot], c.full_at)
                    if b == 0:
                        pe.wait_ge(cf_copied, h + 1)
                    for t in range(4):
                        last = PE.matmul(ps[32 * t:32 * t + NTS, 5, :], qwm[:, t, b, :],
                                         ring[:, c.slot, t * SEQ:t * SEQ + SEQ],
                                         start=b == 0 and t > 0, stop=b == NB - 1, skip_group_check=True)
                    pe.wait_ge(vb_ready, h * NB + (b + 1))
                    for t in range(4):
                        if b:
                            pe.wait_ge(c_new, h * 4 * NB + (4 * b + t - 3))
                        PE.matmul(ps[:, t, :], kw[0:NTS, 4, t * P:t * P + P], vb[0:NTS, b % 2, :],
                                  start=True, stop=True).then_inc(up_ps, 1)
                pe.wait_ge(hd_scaled, h + 1)
                pe.wait_ge(h_root, h + 1)
                for t in range(4):
                    last = PE.matmul(ps[:, 7, t * NTS:t * NTS + NTS], hrow[:, t * P:t * P + P],
                                     const("fold"), start=True, stop=True)
                last.then_inc(hdt_ps, 1)
                pe.wait_ge(hd_sq, h + 1)
                for t in range(4):
                    last = PE.matmul(ps[:, 4, 64:64 + NTS], const("mean_h"), work[:, t, SEQ:T], start=t == 0, stop=t == 3)
                last.then_inc(hd_ms, 1)
                pe.wait_ge(hn_ready, h + 1)
                for k in range(4):
                    c = hchunk(h, 12 + k)
                    pe.wait_ge(full[c.slot], c.full_at)
                    w = ring[:, c.slot, 0:1024].rearrange("p (k c) -> p k c", c=256)
                    for j in range(2):
                        m = 2 * k + j
                        pe.wait_ge(x_tile, h * 8 + (8 * (n + 1) + m - 1 if m >= 2 else 8 * (n + 1)))
                        for t in range(4):
                            for hf in range(2):
                                last = PE.matmul(ps[:, 2 * j + hf, 0:HB], w[:, t, j * P:j * P + P],
                                                 zs[:, t, hf * HB:hf * HB + HB], start=t == 0, stop=t == 3)
                        last.then_inc(done[c.slot] if j else y_even, 1)
                pe.wait_ge(x_tile, h * 8 + 8 * (n + 2))
                pe.wait_ge(nn_done, h + 1)

        def mlstm_act(act, link):
            act.wait_ge(ml_in, 16 * 6)
            act.wait_ge(gt_dve, 1)
            S.activation(cumf[0:MH, :], av[0:MH, :], ACT.Exp).then_inc(gt_act, 1)
            act.wait_ge(gt_act, 1)
            S.activation(av[0:MH, :], cumf[0:MH, :], ACT.Ln, bias=1.0).then_inc(gt_act, 1)
            act.wait_ge(gt_dve, 2)
            S.activation(em[0:MH, 0, :], mrow[0:MH, :], ACT.Exp, scale=-1.0)
            S.activation(wsr[0:MH, :], wsr[0:MH, :], ACT.Exp)
            S.activation(lf[0:MH, SEQ:T], lf[0:MH, SEQ:T], ACT.Exp).then_inc(gates_done, 1)
            act.wait_ge(col_ps, 1)
            ac, wc = acol.rearrange("p a b -> p (a b)"), wcol.rearrange("p a b -> p (a b)")
            S.activation(ac[:, 0:16], ps[:, 2, 0:16], ACT.Copy)
            S.activation(ac[0:NTS, 16:20], ps[0:NTS, 2, 16:20], ACT.Copy)
            S.activation(wc[:, 0:16], ps[:, 2, 20:36], ACT.Copy, scale=KS)
            S.activation(wc[0:NTS, 16:20], ps[0:NTS, 2, 36:40], ACT.Copy, scale=KS)
            S.activation(emcol, ps[:, 2, 56:60], ACT.Copy)
            for j in range(8):
                act.wait_ge(bc_ps, j + 1)
                b0 = 4 + 2 * (j % 2)
                src = ps[:, b0:b0 + 2, 0:HB]
                dst = (ncm if j < 4 else em)[:, j % 4].rearrange("p (a b) -> p a b", b=HB)
                S.activation(dst, src, ACT.Copy if j < 4 else ACT.Exp, scale=-1.0).then_inc(bc_copied, 1)
            act.wait_ge(bc_ps, 9)
            S.activation(wint.rearrange("p a b -> p (a b)"), ps[:, 3, 0:MH * NTS], ACT.Copy).then_inc(gates_done, 1)
            act.wait_ge(gates_done, 2)

            with act.Fori(0, MH) as h:
                for t in range(8):
                    c = hchunk(h, t // 2)
                    if t == 0:
                        act.wait_ge(xp_ready, h + 1)
                    if t % 2:
                        act.wait_ge(done[c.slot], c.done_at)
                    else:
                        act.wait_ge(pr_even, h * 4 + (t // 2 + 1))
                    b0 = 2 * (t % 2)
                    if t < 4:
                        S.activation(xp[:, t, 3:3 + HB], ps[:, b0, 0:HB], ACT.Copy)
                        S.activation(xp[:, t, 3 + HB:3 + SEQ], ps[:, b0 + 1, 0:SEQ - HB], ACT.Copy)
                        S.activation(xm_d[:, t, :], ps[:, b0 + 1, SEQ - HB:HB], ACT.Copy)
                        S.activation(xp[:, t, 3 + SEQ:XPW].rearrange("p (b c) -> p b c", c=7)[:, :, 3:7],
                                     ps[:, b0 + 1, SEQ - HB:HB].rearrange("p (b c) -> p b c", c=DS),
                                     ACT.Copy).then_inc(pr_copied, 1)
                    else:
                        if t == 4:
                            act.wait_ge(pr_copied, h * 8 + 4)
                            for z in range(4):
                                S.activation(acc[:, z, 0:XCW], xp[:, z, 0:XCW], ACT.Identity,
                                             scale=convw[:, h * 4 + z, 0:1],
                                             bias=convw[:, h * 4 + z, 4:5]).then_inc(conv_init, 1)
                        S.activation(zs[:, t - 4].rearrange("p (a b) -> p a b", b=HB), ps[:, b0:b0 + 2, 0:HB],
                                     ACT.Sigmoid).then_inc(pr_copied, 1)
                for z in range(4):
                    act.wait_ge(conv_done, h * 4 + (z + 1))
                    S.activation(xc[:, z, 0:SEQ], acc[:, z, 0:SEQ], ACT.Silu)
                    S.activation(xc[:, z, SEQ:T].rearrange("p (b c) -> p b c", c=DS),
                                 acc[:, z, 3 + SEQ:XPW].rearrange("p (b c) -> p b c", c=7)[:, :, 0:DS],
                                 ACT.Silu).then_inc(xc_ready, 1)
                for t in range(8):
                    act.wait_ge(qk_ps, h * 8 + (t + 1))
                    b0 = 4 + 2 * (t % 2)
                    dst = (qT if t < 4 else kT)[:, t % 4]
                    S.activation(dst.rearrange("p (a b) -> p a b", b=HB), ps[:, b0:b0 + 2, 0:HB], ACT.Copy,
                                 scale=1.0 if t < 4 else KS).then_inc(qk_copied, 1)
                for i in range(5):
                    rows = P if i < 4 else NTS
                    act.wait_ge(vk_ps, h * 10 + (2 * i + 1))
                    S.activation(vr[0:rows, i, :], ps[0:rows, (2 * i) % 4, :], ACT.Copy).then_inc(vk_copied, 1)
                    act.wait_ge(vk_ps, h * 10 + (2 * i + 2))
                    S.activation(kw[0:rows, i, :], ps[0:rows, (2 * i + 1) % 4, :], ACT.Copy,
                                 scale=wcol[0:rows, i, bass.ds(h, 1)]).then_inc(vk_copied, 1)
                act.wait_ge(s_pre, h + 1)
                S.activation(ssp[:, :], ssp[:, :], ACT.Exp).then_inc(s_exp, 1)
                for i in range(4):
                    act.wait_ge(ex_ready, h * 4 + (i + 1))
                    last = S.activation(ex[:, i % 2, 0:P], ex[:, i % 2, 0:P], ACT.Exp)
                    if i < 3:
                        last = S.activation(ex[:, i % 2, P:SEQ - i * P], ncm[:, h, (i + 1) * P:SEQ], ACT.Exp,
                                            bias=acol[:, i, bass.ds(h, 1)])
                    last.then_inc(ex_done, 1)
                act.wait_ge(cf_ps, h + 1)
                S.activation(spt, ps[:, 0:4, :], ACT.Copy).then_inc(cf_copied, 1)
                act.wait_ge(vk_copied, h * 10 + 10)
                for b in range(NB):
                    if b == 2:
                        act.wait_ge(h_ms, h + 1)
                        S.activation(rden[:, :], ps[:, 7, :], ACT.Sqrt, bias=const("eps")).then_inc(h_root, 1)
                    if b >= 2:
                        act.wait_ge(up_ps, h * 4 * NB + 4 * (b - 1))
                    S.activation(vb[0:NTS, b % 2, :], vr[0:NTS, 4, :], ACT.Copy,
                                 scale=const("own_b", NTS)[:, b:b + 1]).then_inc(vb_ready, 1)
                act.wait_ge(hd_ms, h + 1)
                S.activation(rms[:, 0, 0:NTS], ps[:, 4, 64:64 + NTS], ACT.Sqrt, bias=const("eps")).then_inc(hd_root, 1)

        def mlstm_dve(dve, link):
            dve.wait_ge(ml_in, 16 * 6)
            mg = Chunk(plan["mgate"], 0, 0)
            dve.wait_ge(done[mg.slot], mg.done_at)
            H = slice(0, MH)

            def two(v):
                return v.rearrange("p (a b) -> p a b", b=HB)

            def dec(v):
                return v[H, SEQ:T].rearrange("p (b t) -> p b t", t=DS)

            link(V.tensor_scalar(two(ig[H]), ps[0:MH, 0:2, 0:HB], bg[H, 0:1], None, ALU.add))
            link(V.tensor_scalar(two(lf[H]), ps[32:32 + MH, 0:2, 0:HB], bg[32:32 + MH, 0:1], None, ALU.add))
            link(V.tensor_scalar(av[H], lf[H], -1.0, None, ALU.mult))
            V.tensor_tensor(av[H], av[H], lf[H], ALU.min).then_inc(gt_dve, 1)
            dve.wait_ge(gt_act, 2)
            link(V.scalar_tensor_tensor(lf[H], lf[H], 0.0, av[H], ALU.min, ALU.subtract))
            link(V.tensor_tensor_scan(cumf[H], const("restart", MH), lf[H], 0.0, ALU.mult, ALU.add))
            link(V.tensor_tensor(av[H], ig[H], cumf[H], ALU.subtract))
            link(V.tensor_copy(wsr[H], av[H]))
            link(V.tensor_tensor(dec(wsr)[:, :, 0], dec(wsr)[:, :, 0], m0r[H], ALU.max))
            link(V.tensor_tensor_scan(cm[H], const("restart_neg", MH), wsr[H], 0.0, ALU.add, ALU.max))
            link(V.tensor_tensor(mrow[H], cumf[H], cm[H], ALU.add))
            link(V.tensor_scalar(wsr[H, 0:SEQ], av[H, 0:SEQ], cm[H, SEQ - 1:SEQ], None, ALU.subtract))
            link(V.tensor_tensor(dec(wsr), dec(av), dec(cm)[:, :, 3:4].to_broadcast([MH, NB, DS]), ALU.subtract))
            V.tensor_tensor(dec(lf), m0r[H].unsqueeze(2).to_broadcast([MH, NB, DS]), dec(cm),
                            ALU.subtract).then_inc(gt_dve, 1)
            dve.wait_ge(gates_done, 2)
            with dve.Fori(0, MH) as h:
                link.enter(h, 38)
                link(V.memset(xp[:, :, 0:3], 0.0))
                V.tensor_copy(xp[:, :, 3 + SEQ:XPW].rearrange("p a (b c) -> p a b c", c=7)[:, :, :, 0:3],
                              sconv[:, bass.ds(h * 4, 4), :].rearrange("p a (b c) -> p a b c", c=3)).then_inc(xp_ready, 1)
                for z in range(4):
                    dve.wait_ge(conv_init, h * 4 + (z + 1))
                    for w in range(1, 4):
                        ins = V.scalar_tensor_tensor(acc[:, z, 0:XCW], xp[:, z, w:w + XCW], convw[:, h * 4 + z, w:w + 1],
                                                     acc[:, z, 0:XCW], ALU.mult, ALU.add)
                        if w < 3:
                            link(ins)
                        else:
                            ins.then_inc(conv_done, 1)
                V.tensor_copy(cvo[:, bass.ds(h * 4, 4), 0:3], xp[:, :, SEQ:SEQ + 3])
                link(V.tensor_copy(cvo[:, bass.ds(h * 4, 4), 3:27].rearrange("p a (b c) -> p a b c", c=3),
                                   xp[:, :, 3 + SEQ:XPW].rearrange("p a (b c) -> p a b c", c=7)[:, :, :, 4:7]))
                V.scalar_tensor_tensor(ssp[:, :], ncm[0:NTS, h, SEQ:T], acol[0:NTS, 4, bass.ds(h, 1)],
                                       const("causal_b", NTS), ALU.add, ALU.add).then_inc(s_pre, 1)
                dve.wait_ge(qk_copied, h * 8 + 8)
                link(V.tensor_tensor(qw[:, :, :], qT[:, :, SEQ:T], wint[:, h, :].unsqueeze(1).to_broadcast([P, 4, NTS]),
                                     ALU.mult))
                link(V.tensor_tensor(nprod[:, :, :].rearrange("p a (b t) -> p a b t", t=DS),
                                     qw[:, :, :].rearrange("p a (b t) -> p a b t", t=DS),
                                     nst[:, bass.ds(h * 4, 4), :].unsqueeze(3).to_broadcast([P, 4, NB, DS]), ALU.mult))
                for i in range(4):
                    link(V.scalar_tensor_tensor(ex[:, i % 2, 0:P], ncm[:, h, i * P:i * P + P], acol[:, i, bass.ds(h, 1)],
                                                const("causal_t"), ALU.add, ALU.add))
                    V.tensor_copy(den1[0:1, 0:1], acol[0:1, 0, 0:1]).then_inc(ex_ready, 1)
                    if i == 0:
                        dve.wait_ge(s_exp, h + 1)
                        dve.wait_ge(s_ps, h + 1)
                        V.tensor_tensor(ssp[:, :], ssp[:, :], ps[0:NTS, 4, 0:NTS], ALU.mult).then_inc(ssp_ready, 1)
                    dve.wait_ge(ex_done, h * 4 + (i + 1))
                    dve.wait_ge(sm_ps, h * 4 + (i + 1))
                    V.tensor_tensor(spt[:, i, 0:SEQ - i * P], ex[:, i % 2, 0:SEQ - i * P],
                                    ps[:, 5 + i % 2, 0:SEQ - i * P], ALU.mult).then_inc(sp_ready, 1)
                    dve.wait_ge(sp_ready, h * 4 + (i + 1))
                V.tensor_tensor(qwm, qw[:, :, :].unsqueeze(2).to_broadcast([P, 4, NB, NTS]),
                                const("own_cols").rearrange("p (b c) -> p b c", b=NB).unsqueeze(1).to_broadcast([P, 4, NB, NTS]),
                                ALU.mult).then_inc(qw_ready, 1)
                dve.wait_ge(dn_ps, h + 1)
                link(V.tensor_tensor(rden[:, :], ps[:, 7, :], em[:, h, 0:SEQ], ALU.max))
                link(V.scalar_tensor_tensor(rden[:, :], ps[:, 7, :], -1.0, rden[:, :], ALU.mult, ALU.max))
                link(V.reciprocal(rden[:, :], rden[:, :]))
                dve.wait_ge(h_ps, h + 1)
                for e in range(4):
                    V.tensor_tensor(work[:, e, 0:SEQ], ps[:, e, :], rden[:, :], ALU.mult).then_inc(h_scaled, 1)
                dve.wait_ge(h_scaled, h * 4 + 4)
                link(V.tensor_tensor(zs[:, :, 0:SEQ], zs[:, :, 0:SEQ], work[:, :, 0:SEQ], ALU.mult))
                V.tensor_tensor(work[:, :, 0:SEQ], zs[:, :, 0:SEQ], zs[:, :, 0:SEQ], ALU.mult).then_inc(h_sq, 1)
                dve.wait_ge(nn_ps, h + 1)
                nn = ps[:, 4, 0:4 * C9].rearrange("p (a b) -> p a b", b=C9)
                V.tensor_copy(nnew[:, bass.ds(h * 4, 4), 0:1], nn[:, :, 0:1])
                wd = wint[:, h, :].rearrange("p (b t) -> p b t", t=DS)[:, :, 3]
                link(V.tensor_tensor(nnew[:, bass.ds(h * 4, 4), 1:C9], nst[:, bass.ds(h * 4, 4), :],
                                     wd.unsqueeze(1).to_broadcast([P, 4, NB]), ALU.mult))
                V.tensor_tensor(nnew[:, bass.ds(h * 4, 4), 1:C9], nnew[:, bass.ds(h * 4, 4), 1:C9], nn[:, :, 1:C9],
                                ALU.add).then_inc(nn_done, 1)
                def normalise(r, a, z):
                    for e in range(4):
                        last = V.scalar_tensor_tensor(zs[:, e, a:z], zs[:, e, a:z], skipgn[:, h * 4 + e, 1:2], r,
                                                      ALU.mult, ALU.mult)
                    link(last)
                    for e in range(4):
                        last = V.scalar_tensor_tensor(zs[:, e, a:z], xc[:, e, a:z], skipgn[:, h * 4 + e, 0:1],
                                                      zs[:, e, a:z], ALU.mult, ALU.add)
                    return last

                for b in range(NB):
                    if b == 3:
                        dve.wait_ge(h_root, h + 1)
                        link(V.reciprocal(rden[:, :], rden[:, :]))
                        link(normalise(rden[:, :], 0, SEQ))
                    r = ring[:, hchunk(h, 4 + b).slot, :].rearrange("p (a b) -> p a b", a=4)
                    for t in range(4):
                        dve.wait_ge(up_ps, h * 4 * NB + (4 * b + t + 1))
                        V.scalar_tensor_tensor(r[:, t], r[:, t], wint[:, h, DS * b + 3:DS * b + 4], ps[:, t, :],
                                               ALU.mult, ALU.add).then_inc(c_new, 1)
                link(V.tensor_tensor(den1[:, :], ps[:, 6, 0:1], emcol[:, bass.ds(h, 1)], ALU.max))
                link(V.scalar_tensor_tensor(den1[:, :], ps[:, 6, 0:1], -1.0, den1[:, :], ALU.mult, ALU.max))
                link(V.reciprocal(den1[:, :], den1[:, :]))
                V.tensor_scalar(hrow, ps[:, 5, :], den1[:, 0:1], None, ALU.mult).then_inc(hd_scaled, 1)
                dve.wait_ge(hdt_ps, h + 1)
                link(V.tensor_tensor(zs[:, :, SEQ:T], zs[:, :, SEQ:T],
                                     ps[:, 7, 0:4 * NTS].rearrange("p (a b) -> p a b", b=NTS), ALU.mult))
                V.tensor_tensor(work[:, :, SEQ:T], zs[:, :, SEQ:T], zs[:, :, SEQ:T], ALU.mult).then_inc(hd_sq, 1)
                dve.wait_ge(hd_root, h + 1)
                link(V.reciprocal(rms[:, 0, 0:NTS], rms[:, 0, 0:NTS]))
                normalise(rms[:, 0, 0:NTS], SEQ, T).then_inc(hn_ready, 1)
                dve.wait_ge(cf_stored, h * 16 + 16)
                for m in range(KT):
                    c = hchunk(h, 12 + m // 2)
                    if m % 2:
                        dve.wait_ge(done[c.slot], c.done_at)
                    else:
                        dve.wait_ge(y_even, h * 4 + (m // 2 + 1))
                    residual(4, m, 2 * (m % 2), tmp_d[:, m % 2], link)
            link.leave(MH)
        def load_chunks(sp, name, src, w, first=False):
            for ch in chunks(sp, plan[name], first):
                if not (first and isinstance(ch.free_at, int)):
                    sp.wait_ge(done[ch.slot], ch.free_at)
                sp.dma_start(ring[:, ch.slot, 0:w], src(ch.index)).then_inc(full[ch.slot], 16)

        block = ctx.enter_context(nc.Block())

        @block.sync
        def _(sp):
            sp.dma_start(cT[:, :, :], io["cT"]).then_inc(consts_in, 16)
            sp.dma_start(cst[:, :], io["const"]).then_inc(consts_in, 16)
            sp.dma_start(adab[:, :], io["adab"]).then_inc(consts_in, 16)
            sp.dma_start(norm_g[:, :, :], io["norm_g"]).then_inc(consts_in, 16)
            sp.dma_start(pages[:, :], io["pages"]).then_inc(consts_in, 16)
            load_chunks(sp, "ada", lambda i: io["ada"][i], SLOT, first=True)
            for f in range(4):
                load_chunks(sp, f"in{f}", lambda i, f=f: io["ffn_in"][i + f * FT], SLOT)
                load_chunks(sp, f"out{f}", lambda i, f=f: io["ffn_out"][i + f * 2 * KT], FT // 2 * P)
                if f == 0:
                    nsa_sp(sp)
                if f == 2:
                    mlstm_sp(sp)

        @block.gpsimd
        def _(gp):
            gp.dma_start(x[:, :, :], io["x"]).then_inc(x_in, 16)
            nsa_pool(gp)
            mlstm_pool(gp)
            ARENA_STORED[0] = NSTORE[0]
            for k in range(0, KT, 4):
                gp.wait_ge(u_decode, 2 + k + 4)
                gp.dma_start(io["y"][:, k:k + 4, :], u[:, k:k + 4, :]).then_inc(stored, 16)
            NSTORE[0] += 32
            gp.wait_ge(stored, NSTORE[0])

        @block.scalar
        def _(act):
            link = Chain(act, chain_s)
            act.wait_ge(consts_in, 16 * 5)
            norm_act(act, 0)
            ada_act(act)
            modulate_act(act, 0, 0)
            ffn_act(act, 0, 0)
            norm_act(act, 1)
            modulate_act(act, 1)
            nsa_act(act, link)
            norm_act(act, 2, 1)
            modulate_act(act, 2, 1)
            ffn_act(act, 1, 2)
            norm_act(act, 3, 2)
            modulate_act(act, 3, 2)
            ffn_act(act, 2, 3)
            norm_act(act, 4)
            modulate_act(act, 4)
            mlstm_act(act, link)
            norm_act(act, 5, 3)
            modulate_act(act, 5, 3)
            ffn_act(act, 3, 5)
            norm_act(act, 6)

        @block.vector
        def _(dve):
            link = Chain(dve, chain_v)
            dve.wait_ge(x_in, 16)
            V.memset(tmp_d[0:1, 0, 0:1], 0.0).then_inc(x_tile, 8)
            V.memset(tmp_d[0:1, 1, 0:1], 0.0).then_inc(mods_in, 1)
            V.memset(tmp256[0:1, 0:1], 0.0).then_inc(hidden, 2)
            V.memset(tmp256[0:1, 1:2], 0.0).then_inc(w_used, 2)
            dve.wait_ge(consts_in, 16 * 5)
            inverse_rms(dve, 0)
            ada_dve(dve, link)
            split_norm_dve(dve, 0, 0, link)
            ffn_dve(dve, 0, 0, link)
            norm_dve(dve, 1, link)
            nsa_dve(dve, link)
            split_norm_dve(dve, 2, 1, link)
            ffn_dve(dve, 1, 2, link)
            split_norm_dve(dve, 3, 2, link)
            ffn_dve(dve, 2, 3, link)
            norm_dve(dve, 4, link)
            mlstm_dve(dve, link)
            dve.wait_ge(stored, ARENA_STORED[0])
            split_norm_dve(dve, 5, 3, link)
            ffn_dve(dve, 3, 5, link)
            norm_dve(dve, 6, link)

        @block.tensor
        def _(pe):
            norm_pe(pe, 0)
            ada_pe(pe)
            ffn_pe(pe, 0, 0)
            norm_pe(pe, 1)
            nsa_pe(pe)
            norm_pe(pe, 2)
            ffn_pe(pe, 1, 2)
            norm_pe(pe, 3)
            ffn_pe(pe, 2, 3)
            norm_pe(pe, 4)
            mlstm_pe(pe)
            norm_pe(pe, 5)
            ffn_pe(pe, 3, 5)
            norm_pe(pe, 6)


def q_order():
    heads = [((2 * gp + par) * REP + r) for gp in range(2) for r in range(REP) for par in range(2)]
    return np.concatenate([np.arange(h * HD, h * HD + HD) for h in heads])


def layout(inputs):
    f = {k: np.asarray(v) for k, v in inputs.items()}
    a = {"const": CONST}
    c = np.concatenate([f["c_prompt"], f["c_sample"]], 0)
    a["cT"] = c.T.reshape(KT, P, C9).transpose(1, 0, 2)
    xx = np.concatenate([f["x_prompt"].reshape(SEQ, D), f["x_sample"].reshape(NTS, D)], 0)
    a["x"] = xx.T.reshape(KT, P, T).transpose(1, 0, 2)
    a["adab"] = f["ada_b"].reshape(144, P).T
    a["norm_g"] = np.concatenate([f["norm_g"].reshape(6, D), f["final_norm_g"][None]], 0).reshape(7, KT, P).transpose(2, 0, 1)
    a["pages"] = f["page_table"].reshape(1, NB * NPAGE)
    a["ada"] = f["ada_w"].reshape(2, 4, 2, P, 9, D).transpose(0, 4, 1, 3, 2, 5).reshape(72, P, SLOT)
    a["ffn_in"] = f["ffn_w_in"].reshape(4, KT, P, 2, FT, P).transpose(0, 4, 2, 1, 3, 5).reshape(4 * FT, P, SLOT)
    a["ffn_out"] = f["ffn_w_out"].reshape(4, 2, FT // 2, P, KT, P)[:, ::-1].transpose(0, 4, 1, 3, 2, 5).reshape(4 * 2 * KT, P, FT // 2 * P)
    w = f["attn_w_in"][0]
    kv = w[:, 1024:1024 + 1536].reshape(D, 3, 2, 256)
    cols = [w[:, :1024][:, q_order()], kv[:, 0, 0], kv[:, 0, 1], kv[:, 1, 0], kv[:, 2, 0]]
    a["qkv"] = np.concatenate(cols, 1).reshape(KT, P, 8, 256).transpose(2, 1, 0, 3).reshape(8, P, SLOT)
    rows = np.concatenate([kv[:, 1, 1], kv[:, 2, 1], w[:, 2560:2608]], 1)
    a["row"] = rows.reshape(4, 2, P, VR).transpose(0, 2, 1, 3).reshape(4, P, 2 * VR)
    a["attn_out"] = f["attn_w_out"][0].reshape(KT, P, 4, 256).transpose(2, 1, 0, 3).reshape(4, P, SLOT)
    a["w1"] = f["cmp_w1"][0].reshape(2, 16, 2, HD, P).transpose(2, 3, 0, 1, 4).reshape(P, 2, 16, P)
    a["w2k"] = np.concatenate([f["cmp_w2"][0, 0]] * 2, 1)
    a["w2v"] = f["cmp_w2"][0, 1]
    a["cpos"] = f["cmp_pos"][0].reshape(16, 2, 2, HD).transpose(1, 3, 2, 0).reshape(P, 2, 16)
    a["rope"] = rope_tables()
    pg = f["cache_cmp"][0].reshape(NPOOL, 8, 8, 2, 2, KVH, HD)
    a["cmp_pages"] = pg.transpose(0, 3, 6, 4, 2, 5, 1).reshape(NPOOL, P, 512)
    pg = f["cache_sel"][0]
    k = pg[:, :, 0].reshape(NPOOL, P, 2, 2, HD).transpose(0, 3, 4, 2, 1).reshape(NPOOL, P, 256)
    a["sel_pages"] = np.concatenate([k, pg[:, :, 1].reshape(NPOOL, P, 256)], 2)
    wn = f["cache_win"][0]
    k = wn[:, :, 0].reshape(NB, SEQ, 2, 2, HD).transpose(0, 3, 4, 2, 1).reshape(NB, P, 1024)
    v = wn[:, :, 1].reshape(NB, 4, P, 256).transpose(0, 2, 1, 3).reshape(NB, P, 1024)
    a["win"] = np.stack([k, v])
    a["win_v"] = wn[:, :, 1].reshape(NB, SEQ, 256)

    w = f["ml_w_in"][0]
    g = np.zeros((D, 36), np.float32)
    g[:, 0:MH], g[:, 32:36] = w[:, 2 * MI:2 * MI + MH], w[:, 2 * MI + MH:]
    a["mgate"] = g.reshape(KT, P, 36).transpose(1, 0, 2).reshape(P, KT * 36)
    a["ml_in"] = w[:, :2 * MI].reshape(KT, P, 2, MH, 2, 256).transpose(3, 2, 4, 1, 0, 5).reshape(16, P, SLOT)
    a["ml_out"] = f["ml_w_out"][0].reshape(MH, 4, P, 4, 256).transpose(0, 3, 2, 1, 4).reshape(16, P, 1024)
    a["state_c"] = f["state_C"][0].reshape(NB, MH, 4, P, MHD).transpose(1, 0, 3, 2, 4).reshape(MH * NB, P, SLOT)
    a["nst"] = f["state_n"][0].reshape(NB, 16, P).transpose(2, 1, 0)
    a["sconv"] = f["state_conv"][0].reshape(NB, 3, 16, P).transpose(3, 2, 0, 1).reshape(P, 16, NB * 3)
    a["convw"] = np.concatenate([f["ml_conv_w"][0], f["ml_conv_b"]], 0).reshape(5, 16, P).transpose(2, 1, 0)
    a["skipgn"] = np.concatenate([f["ml_skip"], f["ml_gn_g"]], 0).reshape(2, 16, P).transpose(2, 1, 0)
    a["m0"] = f["state_m"][0].T
    b = np.zeros((36, 1), np.float32)
    b[0:MH, 0], b[32:36, 0] = f["ml_b_gate"][0, 0], f["ml_b_gate"][0, 1]
    a["bg"] = b
    bd = np.zeros((3, 16, 32, 4, 32, 4), np.float32)
    for j, name in enumerate(("ml_wq", "ml_wk", "ml_wv")):
        for k in range(32):
            bd[j, :, k, :, k, :] = f[name][0].reshape(16, 32, 4, 4)[:, k]
    a["bd"] = bd.reshape(3, MH, 4, P, P).transpose(1, 3, 0, 2, 4)
    return {k: np.ascontiguousarray(v) for k, v in a.items()}


OUTS = dict(y=(P, KT, T), kv_t=(P, 8, T), v_rows=(P, QT, 512), v_rows_d=(NTS, 512), win_k_out=(NB, P, 2, SEQ - DS),
            win_v_out=(NB, SEQ - DS, 256), c_out=(MH * NB, P, SLOT), cp_out=(MH, P, SLOT), n_out=(P, 16, C9),
            conv_out=(P, 16, C9 * 3), m_out=(MH, T))


def kernel(**inputs):
    import concourse.bacc as _bacc
    from concourse.bass_utils import run_bass_kernel_spmd as _run
    nc = _bacc.Bacc("TRN2", target_bir_lowering=False, num_devices=1)
    arrays = layout(inputs)
    io = {}
    for k, v in arrays.items():
        io[k] = nc.dram_tensor(f"in_{k}_dram", v.shape, mybir.dt.from_np(v.dtype), kind="ExternalInput").ap()
    for k, shape in OUTS.items():
        io[k] = nc.dram_tensor(f"out_{k}_dram", shape, F32, kind="ExternalOutput").ap()
    program(nc, io)
    r = _run(nc, [{f"in_{k}_dram": v for k, v in arrays.items()}], core_ids=[0])
    o = {k: r.results[0][f"out_{k}_dram"] for k in OUTS}
    y = o["y"].transpose(2, 1, 0).reshape(T, D)
    kt = o["kv_t"].reshape(2, HD, 4, 2, T)
    kt = kt.transpose(2, 4, 3, 0, 1).reshape(4, T, KVH, HD)
    v = np.concatenate([o["v_rows"].transpose(1, 0, 2).reshape(SEQ, 512), o["v_rows_d"]], 0).reshape(T, 2, KVH, HD)
    cmp_kv = np.stack([kt[0], kt[1]], 1)
    sel_kv = np.stack([kt[2], v[:, 0]], 1)
    win_kv = np.stack([kt[3], v[:, 1]], 1)

    def prompt(a):
        return a[:SEQ].reshape(1, 1, SEQ, 2, KVH, HD)

    def decode(a):
        return a[SEQ:].reshape(1, NB, DS, 2, KVH, HD)

    kold = o["win_k_out"].reshape(NB, 2, HD, 2, SEQ - DS).transpose(0, 4, 3, 1, 2).reshape(NB, SEQ - DS, KVH, HD)
    vold = o["win_v_out"].reshape(NB, SEQ - DS, KVH, HD)
    win_s = np.concatenate([np.stack([kold, vold], 2), decode(win_kv)[0]], 1)[None]
    c_p = o["cp_out"].reshape(MH, P, 4, MHD).transpose(0, 2, 1, 3).reshape(1, 1, MH, MHD, MHD)
    c_s = o["c_out"].reshape(MH, NB, P, 4, MHD).transpose(1, 0, 3, 2, 4).reshape(1, NB, MH, MHD, MHD)
    n = o["n_out"].transpose(2, 1, 0).reshape(C9, MH, MHD)
    cv = o["conv_out"].reshape(P, 16, C9, 3).transpose(2, 3, 1, 0).reshape(C9, 3, MI)
    m = o["m_out"]
    return (y[:SEQ].reshape(1, SEQ, D), y[SEQ:].reshape(NB, DS, D),
            prompt(cmp_kv), prompt(sel_kv), prompt(win_kv),
            c_p, n[0].reshape(1, 1, MH, MHD), m[:, SEQ - 1].reshape(1, 1, MH), cv[0].reshape(1, 1, 3, MI),
            decode(cmp_kv), decode(sel_kv), win_s,
            c_s, n[1:].reshape(1, NB, MH, MHD), m[:, SEQ + DS - 1::DS].T.reshape(1, NB, MH), cv[1:].reshape(1, NB, 3, MI))
```
